# Optimizing a Trainium2 kernel written in Bass

```python
import numpy as np
import jax
import jax.numpy as jnp
from jax import lax

D_MODEL = 1024
BATCH = 1
SEQ = 512
DEPTH = 2

SWA_Q_HEADS = 8
SWA_KV_HEADS = 2
SWA_HEAD_DIM = 64
WINDOW = 128
ROT_DIM = SWA_HEAD_DIM // 4
ROPE_THETA = 500000.0

GDN_HEADS = 4
GDN_HEAD_DIM = 128
CONV_K = 4
GDN_CHUNK = 64

RET_HEADS = 4
RET_QK_DIM = 256
RET_V_DIM = 512
RET_CHUNK = 128
XPOS_THETA = 10000.0

N_GROUPS = 4
EXPERTS_PER_GROUP = 8
N_EXPERTS = N_GROUPS * EXPERTS_PER_GROUP
TOP_K = 2
D_EXPERT = 512
MOE_BLOCK = 128

EPS = 1e-6

SWA_Q_W = SWA_Q_HEADS * SWA_HEAD_DIM
SWA_KV_W = SWA_KV_HEADS * SWA_HEAD_DIM
GDN_W = GDN_HEADS * GDN_HEAD_DIM
EVEN_SPLITS = (SWA_Q_W, SWA_KV_W, SWA_KV_W, 3 * GDN_W, GDN_W, GDN_HEADS, GDN_HEADS)
EVEN_IN = SWA_Q_W + 2 * SWA_KV_W + 4 * GDN_W + 2 * GDN_HEADS
EVEN_MIX = SWA_Q_W + GDN_W
RET_QK_W = RET_HEADS * RET_QK_DIM
RET_V_W = RET_HEADS * RET_V_DIM
ODD_SPLITS = (RET_QK_W, RET_QK_W, RET_V_W, RET_V_W)
ODD_IN = 2 * RET_QK_W + 2 * RET_V_W
ODD_MIX = RET_V_W

kernel_name = 'hybrid_swa_gdn_retention_hmoe'

def _split(t, sizes):
    cuts = np.cumsum(np.asarray(sizes))[:-1].tolist()
    return jnp.split(t, cuts, axis=-1)

def rms_norm(x, gain=None):
    xf = x.astype(jnp.float32)
    y = xf * lax.rsqrt(jnp.mean(jnp.square(xf), axis=-1, keepdims=True) + EPS)
    if gain is not None:
        y = y * gain.astype(jnp.float32)
    return y.astype(x.dtype)

def l2_norm(x):
    xf = x.astype(jnp.float32)
    return xf * lax.rsqrt(jnp.sum(xf * xf, axis=-1, keepdims=True) + EPS)

def partial_rope(x, pos):
    half = ROT_DIM // 2
    inv_freq = 1.0 / (ROPE_THETA ** (jnp.arange(half, dtype=jnp.float32) * 2.0 / ROT_DIM))
    ang = pos[:, None] * inv_freq[None, :]
    cos = jnp.cos(ang)[None, :, None, :].astype(x.dtype)
    sin = jnp.sin(ang)[None, :, None, :].astype(x.dtype)
    x1 = x[..., :half]
    x2 = x[..., half:ROT_DIM]
    return jnp.concatenate([x1 * cos - x2 * sin, x2 * cos + x1 * sin, x[..., ROT_DIM:]], axis=-1)

def xpos_rotate(x, pos):
    half = x.shape[-1] // 2
    freq = 1.0 / (XPOS_THETA ** jnp.linspace(0.0, 1.0, half, dtype=jnp.float32))
    ang = pos[:, None] * freq[None, :]
    cos = jnp.cos(ang)[None, :, None, :].astype(x.dtype)
    sin = jnp.sin(ang)[None, :, None, :].astype(x.dtype)
    x1 = x[..., 0::2]
    x2 = x[..., 1::2]
    return jnp.stack([x1 * cos - x2 * sin, x2 * cos + x1 * sin], axis=-1).reshape(x.shape)

def causal_depthwise_conv(x, w):
    k_len, ch = w.shape
    return lax.conv_general_dilated(x, w[:, None, :], window_strides=(1,), padding=[(k_len - 1, 0)],
                                    dimension_numbers=('NWC', 'WIO', 'NWC'), feature_group_count=ch)

def sliding_window_attention(q, k, v, sinks):
    bsz, s, hq, dh = q.shape
    hkv = k.shape[2]
    grp = hq // hkv
    n = s // WINDOW
    qb = q.reshape(bsz, n, WINDOW, hkv, grp, dh)

    def band(t):
        t = t.reshape(bsz, n, WINDOW, hkv, dh)
        prev = jnp.pad(t, ((0, 0), (1, 0), (0, 0), (0, 0), (0, 0)))[:, :-1]
        return jnp.concatenate([prev, t], axis=2)

    kb, vb = band(k), band(v)
    scores = jnp.einsum('bnqhgd,bnkhd->bhgnqk', qb, kb).astype(jnp.float32) * (dh ** -0.5)
    blk = jnp.arange(n)[:, None] * WINDOW
    qpos = blk + jnp.arange(WINDOW)[None, :]
    kpos = blk - WINDOW + jnp.arange(2 * WINDOW)[None, :]
    rel = qpos[:, :, None] - kpos[:, None, :]
    mask = (rel >= 0) & (rel < WINDOW) & (kpos[:, None, :] >= 0)
    scores = jnp.where(mask, scores, -jnp.inf)
    sink = jnp.broadcast_to(sinks.astype(jnp.float32).reshape(1, hkv, grp, 1, 1, 1), scores.shape[:-1] + (1,))
    probs = jax.nn.softmax(jnp.concatenate([scores, sink], axis=-1), axis=-1)[..., :-1]
    out = jnp.einsum('bhgnqk,bnkhd->bnqhgd', probs.astype(v.dtype), vb)
    return out.reshape(bsz, s, hq * dh)

def gated_delta_rule(q, k, v, beta, g):
    bsz, s, h, dk = q.shape
    dv = v.shape[-1]
    c = GDN_CHUNK
    n = s // c

    def to_chunks(t):
        t = t.reshape((bsz, n, c, h) + t.shape[3:])
        return jnp.moveaxis(t, 3, 1)

    q, k, v, beta, g = map(to_chunks, (q, k, v, beta, g))
    g = jnp.cumsum(g, axis=-1)
    incl = jnp.tril(jnp.ones((c, c), dtype=bool))
    strict = jnp.tril(jnp.ones((c, c), dtype=bool), -1)
    decay = jnp.exp(jnp.where(incl, g[..., :, None] - g[..., None, :], -jnp.inf))
    kb = k * beta[..., None]
    lower = jnp.where(strict, jnp.einsum('bhnid,bhnjd->bhnij', kb, k) * decay, 0.0)
    eye = jnp.eye(c, dtype=jnp.float32)
    t_inv = lax.linalg.triangular_solve(eye + lower, jnp.broadcast_to(eye, lower.shape),
                                        left_side=True, lower=True)
    u = t_inv @ (v * beta[..., None])
    w = t_inv @ (kb * jnp.exp(g)[..., None])
    intra = jnp.einsum('bhnid,bhnjd->bhnij', q, k) * decay
    q_dec = q * jnp.exp(g)[..., None]
    g_last = g[..., -1]
    k_dec = k * jnp.exp(g_last[..., None] - g)[..., None]
    xs = tuple(jnp.moveaxis(t, 2, 0) for t in (u, w, intra, q_dec, k_dec, jnp.exp(g_last)))

    def step(state, inp):
        u_c, w_c, a_c, qd_c, kd_c, gl_c = inp
        v_new = u_c - jnp.einsum('bhck,bhkv->bhcv', w_c, state)
        out = jnp.einsum('bhck,bhkv->bhcv', qd_c, state) + jnp.einsum('bhij,bhjv->bhiv', a_c, v_new)
        state = state * gl_c[..., None, None] + jnp.einsum('bhck,bhcv->bhkv', kd_c, v_new)
        return state, out

    state0 = jnp.zeros((bsz, h, dk, dv), jnp.float32)
    _, out = lax.scan(step, state0, xs)
    return jnp.transpose(out, (1, 0, 3, 2, 4)).reshape(bsz, s, h, dv)

def multiscale_retention(q, k, v):
    bsz, s, h, dk = q.shape
    dv = v.shape[-1]
    c = RET_CHUNK
    n = s // c
    log_gamma = jnp.log(1.0 - 2.0 ** (-5.0 - jnp.arange(h, dtype=jnp.float32)))
    idx = jnp.arange(c, dtype=jnp.float32)
    rel = idx[:, None] - idx[None, :]
    decay = jnp.exp(jnp.where(rel >= 0, rel * log_gamma[:, None, None], -jnp.inf))
    xi = jnp.exp((idx + 1.0) * log_gamma[:, None])[..., None]
    zeta = jnp.exp((c - 1.0 - idx) * log_gamma[:, None])[..., None]
    gamma_c = jnp.exp(c * log_gamma)[:, None, None]

    def to_chunks(t):
        return jnp.transpose(t.reshape(bsz, n, c, h, t.shape[-1]), (1, 0, 3, 2, 4))

    def step(state, inp):
        q_c, k_c, v_c = inp
        inner = jnp.einsum('bhik,bhjk->bhij', q_c, k_c) * decay
        out = jnp.einsum('bhij,bhjv->bhiv', inner, v_c) + jnp.einsum('bhik,bhkv->bhiv', q_c, state) * xi
        state = state * gamma_c + jnp.einsum('bhjk,bhjv->bhkv', k_c * zeta, v_c)
        return state, out

    state0 = jnp.zeros((bsz, h, dk, dv), jnp.float32)
    _, out = lax.scan(step, state0, (to_chunks(q), to_chunks(k), to_chunks(v)))
    return jnp.transpose(out, (1, 0, 3, 2, 4)).reshape(bsz, s, h, dv)

def attn_delta_mixer(h, pos, w_in, conv_w, a_log, dt_bias, q_gain, k_gain, sinks, gdn_gain, w_out):
    bsz, s, _ = h.shape
    aq, ak, av, bqkv, bz, ba, bb = _split(h @ w_in, EVEN_SPLITS)
    q = rms_norm(aq.reshape(bsz, s, SWA_Q_HEADS, SWA_HEAD_DIM), q_gain)
    k = rms_norm(ak.reshape(bsz, s, SWA_KV_HEADS, SWA_HEAD_DIM), k_gain)
    v = av.reshape(bsz, s, SWA_KV_HEADS, SWA_HEAD_DIM)
    y_a = sliding_window_attention(partial_rope(q, pos), partial_rope(k, pos), v, sinks)
    qkv = jax.nn.silu(causal_depthwise_conv(bqkv, conv_w))
    bq, bk, bv = jnp.split(qkv, 3, axis=-1)
    head_shape = (bsz, s, GDN_HEADS, GDN_HEAD_DIM)
    bq = l2_norm(bq.reshape(head_shape)) * (GDN_HEAD_DIM ** -0.5)
    bk = l2_norm(bk.reshape(head_shape))
    bv = bv.reshape(head_shape).astype(jnp.float32)
    beta = jax.nn.sigmoid(bb.astype(jnp.float32))
    g = -jnp.exp(a_log.astype(jnp.float32)) * jax.nn.softplus(ba.astype(jnp.float32) + dt_bias.astype(jnp.float32))
    o = gated_delta_rule(bq, bk, bv, beta, g)
    o = rms_norm(o, gdn_gain).astype(h.dtype) * jax.nn.silu(bz.reshape(head_shape))
    y_b = o.reshape(bsz, s, GDN_W)
    return jnp.concatenate([y_a, y_b], axis=-1) @ w_out

def retention_mixer(h, pos, w_in, w_out):
    bsz, s, _ = h.shape
    q, k, v, z = _split(h @ w_in, ODD_SPLITS)
    qk_shape = (bsz, s, RET_HEADS, RET_QK_DIM)
    q = xpos_rotate(q.reshape(qk_shape), pos).astype(jnp.float32)
    k = xpos_rotate(k.reshape(qk_shape), pos).astype(jnp.float32) * (RET_QK_DIM ** -0.5)
    v = v.reshape(bsz, s, RET_HEADS, RET_V_DIM).astype(jnp.float32)
    o = rms_norm(multiscale_retention(q, k, v)).astype(h.dtype).reshape(bsz, s, ODD_MIX)
    return (jax.nn.silu(z) * o) @ w_out

def hierarchical_moe(x, w_rg, b_rg, w_re, b_re, w_gate, w_up, w_down):
    bsz, s, d = x.shape
    xt = x.reshape(-1, d)
    n_tok = xt.shape[0]
    n_assign = n_tok * TOP_K
    grp_prob = jax.nn.softmax((xt @ w_rg).astype(jnp.float32) + b_rg.astype(jnp.float32), axis=-1)
    grp_p, grp_idx = lax.top_k(grp_prob, 1)
    exp_logits = ((xt @ w_re).astype(jnp.float32) + b_re.astype(jnp.float32)).reshape(n_tok, N_GROUPS, EXPERTS_PER_GROUP)
    exp_logits = exp_logits[jnp.arange(n_tok), grp_idx[:, 0]]
    exp_p, exp_idx = lax.top_k(jax.nn.softmax(exp_logits, axis=-1), TOP_K)
    gates = grp_p * exp_p / jnp.sum(exp_p, axis=-1, keepdims=True)
    expert_id = (grp_idx * EXPERTS_PER_GROUP + exp_idx).reshape(-1)
    token_id = jnp.repeat(jnp.arange(n_tok), TOP_K)
    order = jnp.argsort(expert_id)
    e_sorted = expert_id[order]
    tok_sorted = token_id[order]
    gate_sorted = gates.reshape(-1)[order]
    counts = jnp.bincount(expert_id, length=N_EXPERTS)
    start = jnp.cumsum(counts) - counts
    padded = (counts + MOE_BLOCK - 1) // MOE_BLOCK * MOE_BLOCK
    padded_end = jnp.cumsum(padded)
    dest = padded_end[e_sorted] - padded[e_sorted] + jnp.arange(n_assign) - start[e_sorted]
    n_rows = n_assign + N_EXPERTS * MOE_BLOCK
    n_blocks = n_rows // MOE_BLOCK
    x_rows = jnp.zeros((n_rows, d), x.dtype).at[dest].set(xt[tok_sorted])
    block_expert = jnp.minimum(jnp.searchsorted(padded_end, jnp.arange(n_blocks) * MOE_BLOCK, side='right'), N_EXPERTS - 1)

    def expert_block(args):
        xb, e = args
        hid = jax.nn.silu(xb @ w_gate[e]) * (xb @ w_up[e])
        return hid @ w_down[e]

    y_rows = lax.map(expert_block, (x_rows.reshape(n_blocks, MOE_BLOCK, d), block_expert)).reshape(n_rows, d)
    y = jnp.zeros((n_tok, d), x.dtype).at[tok_sorted].add(y_rows[dest] * gate_sorted[:, None].astype(x.dtype))
    return y.reshape(bsz, s, d)

def setup_inputs(seed: int = 0) -> dict:
    key = jax.random.key(seed)
    ks = jax.random.split(key, 24)
    f32 = jnp.float32
    n_even = (DEPTH + 1) // 2
    n_odd = DEPTH // 2

    def normal(k, shape, scale):
        return jax.random.normal(k, shape, f32) * scale

    def gain(k, shape):
        return 1.0 + 0.02 * jax.random.normal(k, shape, f32)

    dt = jnp.exp(jax.random.uniform(ks[5], (n_even, GDN_HEADS), f32, np.log(1e-3), np.log(1e-1)))
    return {
        'x': normal(ks[0], (BATCH, SEQ, D_MODEL), 1.0),
        'ln_mix_even': gain(ks[1], (n_even, D_MODEL)),
        'w_in_even': normal(ks[2], (n_even, D_MODEL, EVEN_IN), D_MODEL ** -0.5),
        'conv_w_even': normal(ks[3], (n_even, CONV_K, 3 * GDN_W), CONV_K ** -0.5),
        'a_log_even': jnp.log(jax.random.uniform(ks[4], (n_even, GDN_HEADS), f32, 1.0, 16.0)),
        'dt_bias_even': dt + jnp.log(-jnp.expm1(-dt)),
        'q_gain_even': gain(ks[6], (n_even, SWA_HEAD_DIM)),
        'k_gain_even': gain(ks[7], (n_even, SWA_HEAD_DIM)),
        'sinks_even': normal(ks[8], (n_even, SWA_Q_HEADS), 1.0),
        'gdn_gain_even': gain(ks[9], (n_even, GDN_HEAD_DIM)),
        'w_out_even': normal(ks[10], (n_even, EVEN_MIX, D_MODEL), EVEN_MIX ** -0.5),
        'ln_mix_odd': gain(ks[11], (n_odd, D_MODEL)),
        'w_in_odd': normal(ks[12], (n_odd, D_MODEL, ODD_IN), D_MODEL ** -0.5),
        'w_out_odd': normal(ks[13], (n_odd, ODD_MIX, D_MODEL), ODD_MIX ** -0.5),
        'ln_ffn': gain(ks[14], (DEPTH, D_MODEL)),
        'w_router_group': normal(ks[15], (DEPTH, D_MODEL, N_GROUPS), D_MODEL ** -0.5),
        'b_router_group': normal(ks[16], (DEPTH, N_GROUPS), 0.01),
        'w_router_expert': normal(ks[17], (DEPTH, D_MODEL, N_EXPERTS), D_MODEL ** -0.5),
        'b_router_expert': normal(ks[18], (DEPTH, N_EXPERTS), 0.01),
        'w_gate': normal(ks[19], (DEPTH, N_EXPERTS, D_MODEL, D_EXPERT), D_MODEL ** -0.5),
        'w_up': normal(ks[20], (DEPTH, N_EXPERTS, D_MODEL, D_EXPERT), D_MODEL ** -0.5),
        'w_down': normal(ks[21], (DEPTH, N_EXPERTS, D_EXPERT, D_MODEL), D_EXPERT ** -0.5),
    }

def reference(x, ln_mix_even, w_in_even, conv_w_even, a_log_even, dt_bias_even, q_gain_even, k_gain_even,
              sinks_even, gdn_gain_even, w_out_even, ln_mix_odd, w_in_odd, w_out_odd, ln_ffn,
              w_router_group, b_router_group, w_router_expert, b_router_expert, w_gate, w_up, w_down):
    pos = jnp.arange(x.shape[1], dtype=jnp.float32)
    for layer in range(DEPTH):
        i = layer // 2
        if layer % 2 == 0:
            x = x + attn_delta_mixer(rms_norm(x, ln_mix_even[i]), pos, w_in_even[i], conv_w_even[i],
                                     a_log_even[i], dt_bias_even[i], q_gain_even[i], k_gain_even[i],
                                     sinks_even[i], gdn_gain_even[i], w_out_even[i])
        else:
            x = x + retention_mixer(rms_norm(x, ln_mix_odd[i]), pos, w_in_odd[i], w_out_odd[i])
        x = x + hierarchical_moe(rms_norm(x, ln_ffn[layer]), w_router_group[layer], b_router_group[layer],
                                 w_router_expert[layer], b_router_expert[layer], w_gate[layer],
                                 w_up[layer], w_down[layer])
    return x


_drawn_inputs = setup_inputs


def setup_inputs(seed=0):
    import zlib

    import numpy as np

    out = dict(_drawn_inputs(seed))
    spreads = {}
    factors = {'k_gain_even': 2.751}
    for name, (base, spread) in spreads.items():
        noise = np.random.default_rng([zlib.crc32(name.encode()), seed]).standard_normal(out[name].shape)
        drawn = base * np.exp(spread * noise) if base else spread * noise
        out[name] = jnp.asarray(drawn.astype(out[name].dtype))
    for name, factor in factors.items():
        out[name] = (out[name] * factor).astype(out[name].dtype)
    return out
```

```python
from contextlib import ExitStack

import numpy as np
import concourse.bass as bass
from concourse import mybir

F32 = mybir.dt.float32
I32 = mybir.dt.int32
ALU = mybir.AluOpType
ACT = mybir.ActivationFunctionType
AX = mybir.AxisListType.X

P = 128
D = 1024
SEQ = 512
NT = SEQ // P
KT = D // P
EPS = 1e-6
BIG = 1e30
RING = 6
SLOT = 4096
AH, AKV, ADH = 8, 2, 64
AQK = AH + AKV
GH, GD, CONV, CH = 4, 128, 4, 64
LEVELS = 6
RH, RQ, RV = 4, 256, 512
NG, EPG, NE, DE = 4, 8, 32, 512
SLOTS = 64
NR = NG + NE


def constants():
    i = np.arange(P)
    same = (i[:, None] // CH) == (i[None, :] // CH)
    even = {
        "ident": np.eye(P),
        "ones": np.ones((P, P)),
        "before": i[:, None] < i[None, :],
        "cum": same & (i[:, None] <= i[None, :]),
        "chunk": same,
        "strict": same & (i[:, None] > i[None, :]),
        "inclT": same & (i[:, None] <= i[None, :]),
    }
    for lv in range(LEVELS):
        b = 1 << lv
        even[f"level{lv}"] = ((i[:, None] // (2 * b)) == (i[None, :] // (2 * b))) & \
            ((i[:, None] // b) % 2 == 1) & ((i[None, :] // b) % 2 == 0)
    q, k = i[:, None], np.arange(2 * P)[None, :] - P
    even["window"] = np.where((q - k >= 0) & (q - k < P), 0.0, -BIG)
    half = ADH // 8
    inv = (np.float32(1.0) / np.float32(500000.0) ** (np.arange(half, dtype=np.float32) * np.float32(2.0) / np.float32(16))).astype(np.float32)
    ang = (np.arange(SEQ, dtype=np.float32)[:, None] * inv[None, :]).astype(np.float32)
    ang = ang.reshape(NT, P, half).transpose(1, 0, 2).reshape(P, NT * half).astype(np.float64)
    even["rcos"], even["rsin"] = np.cos(ang), np.sin(ang)
    even["slot"] = np.broadcast_to(np.arange(SLOTS), (P, SLOTS))
    even["rowbase"] = np.broadcast_to(np.arange(NE) * SLOTS, (P, NE))
    even["first"] = np.broadcast_to(16 - np.arange(EPG), (P, EPG))
    odd = {}
    freq = (np.float32(1.0) / np.float32(10000.0) ** np.linspace(0.0, 1.0, RQ // 2, dtype=np.float32)).astype(np.float32)
    ang = (np.arange(SEQ, dtype=np.float32)[None, :] * freq[:, None]).astype(np.float32).astype(np.float64)
    odd["xcos"], odd["xsin"] = np.cos(ang), np.sin(ang)
    lg = np.log(1.0 - 2.0 ** (-5.0 - np.arange(RH)))
    kscale = RQ ** -0.5
    for h in range(RH):
        rel = i[None, :] - i[:, None]
        odd[f"decay{h}"] = np.where(rel >= 0, np.exp(np.maximum(rel, 0) * lg[h]), 0.0) * kscale
        odd[f"xi{h}"] = np.broadcast_to(np.exp((i + 1) * lg[h]), (P, P))
    odd["zeta"] = np.exp((P - 1 - i)[:, None] * lg[None, :]) * kscale
    return even, odd, [float(np.exp(P * x)) for x in lg]


def columns(tables):
    at, n = {}, 0
    for name, a in tables.items():
        at[name] = (n, n + a.shape[1])
        n += a.shape[1]
    return at, n


def program(nc, x, ln_mix_even, w_in_even, conv_w_even, a_log_even, dt_bias_even, q_gain_even, k_gain_even,
            sinks_even, gdn_gain_even, w_out_even, ln_mix_odd, w_in_odd, w_out_odd, ln_ffn,
            w_router_group, b_router_group, w_router_expert, b_router_expert, w_gate, w_up, w_down,
            const_even, const_odd, out, upto=4):
    tab_even, tab_odd, gamma = constants()
    ce, n_even = columns(tab_even)
    co, n_odd = columns(tab_odd)
    y_rows = nc.dram_tensor("y_rows", (NE * SLOTS, D), F32, kind="Internal").ap()
    gains = [ln_mix_even[0:1, :], ln_ffn[0:1, :], ln_mix_odd[0:1, :], ln_ffn[1:2, :]]
    ctx = ExitStack()
    with ctx:
        def sb(name, shape, dt=F32):
            return ctx.enter_context(nc.sbuf_tensor(name, shape, dt))

        def sem(name):
            return ctx.enter_context(nc.semaphore(name))

        ring = sb("ring", [P, RING, SLOT])
        X = sb("X", [P, NT, D])
        XN = sb("XN", [P, NT, D])
        HT = sb("HT", [P, KT, SEQ])
        CE = sb("CE", [P, n_even])
        gainB = sb("gainB", [P, D])
        sumsq = sb("sumsq", [P, NT])
        rstd = sb("rstd", [P, NT])
        mhalf = sb("mhalf", [P, 64])
        WR = sb("WR", [P, KT, NR])
        br = sb("br", [P, NR])
        SCR_N = 12600
        CO_AT = SCR_N - n_odd
        SCR = sb("SCR", [P, SCR_N])
        PARAMS = 16 * 7
        PB = [ctx.enter_context(nc.psum_tensor(f"bank{i}", [P, 512], F32)) for i in range(8)]

        def const(name):
            a, b = ce[name]
            return CE[:, a:b]

        ident, ones = const("ident"), const("ones")

        class Carve:
            def __init__(self, tensor, size):
                self.t, self.n, self.size = tensor, 0, size

            def __call__(self, n):
                a = self.n
                self.n += n
                assert self.n <= self.size, (self.n, self.size)
                return self.t[:, a:a + n]

        chunks = []

        def slot_of(c):
            return ring[:, c % RING, :]

        def k_rows(w, a, b):
            return w[:, a:b].rearrange("(p k) n -> p k n", p=P)

        w_e = w_in_even[0]
        c_kv = len(chunks)
        chunks.append([(lambda s: s[:, 0:KT * 264].rearrange("p (k n) -> p k n", k=KT)[:, :, 0:256], k_rows(w_e, 512, 768)),
                       (lambda s: s[:, 0:KT * 264].rearrange("p (k n) -> p k n", k=KT)[:, :, 256:264], k_rows(w_e, 2816, 2824))])
        c_q = len(chunks)
        chunks.append([(lambda s: s.rearrange("p (k n) -> p k n", k=KT), k_rows(w_e, 0, 512))])
        c_gdn = len(chunks)
        for h in range(GH):
            src = w_e[:, 768:2816].rearrange("(p k) (s n) -> p k s n", p=P, s=4)[:, :, :, h * GD:(h + 1) * GD]
            chunks.append([(lambda s, i=i: s.rearrange("p (k s n) -> p k s n", k=KT, s=4)[:, :, i, :], src[:, :, i, :]) for i in range(4)])
        c_oute = len(chunks)
        for g in range(2):
            chunks.append([(lambda s: s.rearrange("p (k n) -> p k n", k=4),
                            w_out_even[0, g * 512:(g + 1) * 512, :].rearrange("(p k) n -> p k n", p=P))])
        c_moe = [len(chunks)]
        for e in range(NE):
            chunks += [[None]] * 3
        c_ret = len(chunks)
        w_o = w_in_odd[0]
        for h in range(RH):
            src = w_o[:, 0:2048].rearrange("(p k) (s n) -> p k s n", p=P, s=2)[:, :, :, h * RQ:(h + 1) * RQ]
            chunks.append([(lambda s, i=i: s.rearrange("p (k s n) -> p k s n", k=KT, s=2)[:, :, i, :], src[:, :, i, :]) for i in range(2)])
            for base in (2048, 4096):
                chunks.append([(lambda s: s.rearrange("p (k n) -> p k n", k=KT), k_rows(w_o, base + h * RV, base + (h + 1) * RV))])
            chunks.append([(lambda s: s.rearrange("p (k n) -> p k n", k=4),
                            w_out_odd[0, h * RV:(h + 1) * RV, :].rearrange("(p k) n -> p k n", p=P))])
        c_moe.append(len(chunks))
        for e in range(NE):
            chunks += [[None]] * 3

        def landed(c):
            return 16 * sum(len(chunks[d]) for d in range(c % RING, c + 1, RING))

        w_landed = [sem(f"w_landed{s}") for s in range(RING)]
        w_used = sem("w_used")

        x_in, consts_in, params_in, odd_in, gain_in, router_in = (sem(s) for s in (
            "x_in", "consts_in", "params_in", "odd_in", "gain_in", "router_in"))
        mhalf_set = sem("mhalf_set")
        turns = sem("turns")
        resid = sem("resid")
        ss_done, rstd_done, xn_done, tr_done, tr_out_a, tr_out_d = (sem(s) for s in (
            "ss_done", "rstd_done", "xn_done", "tr_done", "tr_out_a", "tr_out_d"))
        act_step, dve_step, pool_step = sem("act_step"), sem("dve_step"), sem("pool_step")
        S = {}

        def sg(name):
            if name not in S:
                S[name] = sem(name)
            return S[name]

        class Steps:
            def __init__(self, eng, s):
                self.eng, self.sem, self.n = eng, s, 0

            def __call__(self, ins):
                ins.then_inc(self.sem, 1)
                self.n += 1

            def wait(self):
                self.eng.wait_ge(self.sem, self.n)

            def then(self, ins):
                self(ins)
                self.wait()

        def alone(eng):
            eng.sem_inc(turns, 1)

        R_EVEN, R_MOE0, R_ODD, R_MOE1 = 8, 12, 12 + 32, 12 + 32 + 4

        def x_wait(eng, ph, t):
            if ph == 0:
                eng.wait_ge(x_in, 16)
            else:
                eng.wait_ge(resid, [0, R_EVEN, R_EVEN + t + 1, R_ODD - 8 + 2 * (t + 1)][ph])

        def norm_act(act, ph):
            for t in range(NT):
                x_wait(act, ph, t)
                act.activation(HT[:, 2 * t:2 * t + 2, :], X[:, t, :].rearrange("p (a b) -> p a b", a=2), ACT.Square,
                               accum_out=sumsq[:, t:t + 1]).then_inc(ss_done, 1)

        def norm_act_out(act, ph):
            for n in range(0, 8, 2):
                t, kk = n // 2, n % 2
                act.wait_ge(tr_done, 8 * ph + n + 1)
                act.copy(HT[:, 4 * kk:4 * kk + 4, t * P:(t + 1) * P], PB[n % 4][:, :].rearrange("p (k q) -> p k q", k=4)).then_inc(tr_out_a, 1)

        def norm_pool(pool, ph, step):
            pool.wait_ge(ss_done, NT * (ph + 1))
            if ph:
                pool.wait_ge(xn_done, NT * ph)
            step.then(pool.tensor_scalar(rstd[:, :], sumsq[:, :], 1.0 / D, EPS, ALU.mult, ALU.add))
            pool.tensor_tensor(rstd[:, :], rstd[:, :], mhalf[:, 0:NT], ALU.pow).then_inc(rstd_done, 1)

        def gain_pool(pool, ph):
            if ph:
                pool.wait_ge(xn_done, NT * ph)
            pool.dma_start(gainB[:, :], gains[ph].to_broadcast([P, D])).then_inc(gain_in, 16)

        def norm_dve(dve, ph):
            dve.wait_ge(rstd_done, ph + 1)
            dve.wait_ge(gain_in, 16 * (ph + 1))
            if ph:
                dve.wait_ge(resid, [0, R_EVEN, R_MOE0, R_ODD][ph])
            for t in range(NT):
                dve.scalar_tensor_tensor(XN[:, t, :].rearrange("p (a c) -> p c a", a=2), X[:, t, :].rearrange("p (c a) -> p c a", a=2),
                                         rstd[:, t:t + 1], gainB[:, :].rearrange("p (c a) -> p c a", a=2),
                                         ALU.mult, ALU.mult).then_inc(xn_done, 1)

        def norm_dve_out(dve, ph):
            for n in range(1, 8, 2):
                t, kk = n // 2, n % 2
                dve.wait_ge(tr_done, 8 * ph + n + 1)
                dve.tensor_copy(HT[:, 4 * kk:4 * kk + 4, t * P:(t + 1) * P], PB[n % 4][:, :].rearrange("p (k q) -> p k q", k=4)).then_inc(tr_out_d, 1)

        def norm_pe(pe, ph):
            if ph == 0:
                pe.wait_ge(consts_in, 16)
            for n in range(8):
                t, kk = n // 2, n % 2
                pe.wait_ge(xn_done, NT * ph + t + 1)
                if n >= 4:
                    pe.wait_ge((tr_out_a, tr_out_d)[n % 2], 4 * ph + (n - 4) // 2 + 1)
                for j in range(4):
                    k = 4 * kk + j
                    mm = pe.transpose(PB[n % 4][:, j * P:(j + 1) * P], XN[:, t, (k % 2) * 512 + k // 2:(k % 2 + 1) * 512:4], ident)
                mm.then_inc(tr_done, 1)
            pe.wait_ge(tr_out_a, 4 * (ph + 1))
            pe.wait_ge(tr_out_d, 4 * (ph + 1))

        s_ = Carve(SCR, SCR_N)
        prm = s_(640 + 8 + 4 + 4 + 128)
        cwr, cw = s_(128), s_(48)
        qk_gain, sink_b, alog_b, dtb_b, gdn_gain = prm[:, 0:640], prm[:, 640:648], prm[:, 648:652], prm[:, 652:656], prm[:, 656:784]
        smalls = s_(400)
        sm_n = [0]

        def small(n):
            a = sm_n[0]
            sm_n[0] += n
            assert sm_n[0] <= 400
            return smalls[:, a:a + n]

        g_raw, g_abs, g_e, g_sp, g_val, beta, ea = (small(16) for _ in range(7))
        G_col, GL_col, kb_scale, kd_scale, eG = (small(16) for _ in range(5))
        mixed = s_.n
        A1 = s_(NT * 776).rearrange("p (t n) -> p t n", t=NT)
        qT = s_(4 * SEQ).rearrange("p (j n) -> p j n", j=4)
        kT = s_(SEQ)
        SC = s_(AH * 256).rearrange("p (h n) -> p h n", h=AH)
        PT = s_(AH * 256).rearrange("p (h n) -> p h n", h=AH)
        rt = s_(4 * 320).rearrange("p (a n) -> p a n", a=4)
        a_ss, a_rs = small(40), small(40)
        a_max, a_nmax, a_sum, a_sink, a_rec = (small(8) for _ in range(5))
        QKv = A1[:, :, 0:640]
        sq_tmp = SCR[:, mixed + NT * 776:mixed + NT * 776 + NT * 640].rearrange("p (t n) -> p t n", t=NT)

        def attn_pe(pe):
            for n in range(8):
                c, t = (c_kv, n) if n < 4 else (c_q, n - 4)
                if n % 4 == 0:
                    pe.wait_ge(w_landed[c % RING], landed(c))
                if n >= 4:
                    pe.wait_ge(sg("a_proj_out"), n - 3)
                width = 264 if n < 4 else 512
                w = slot_of(c)[:, 0:KT * width].rearrange("p (k n) -> p k n", k=KT)
                for k in range(KT):
                    mm = pe.matmul(PB[4 + n % 4][:, 0:width], HT[:, k, t * P:(t + 1) * P], w[:, k, :], start=(k == 0), stop=(k == KT - 1))
                mm.then_inc(sg("a_proj"), 1)
            pe.wait_ge(sg("g_gates"), 1)
            pe.matmul(PB[0][:, 0:16], const("cum"), g_val, start=True, stop=True)
            pe.matmul(PB[1][:, 0:16], const("chunk"), g_val, start=True, stop=True).then_inc(sg("g_cum"), 1)
            pe.wait_ge(sg("a_rope"), 1)
            for t in range(NT):
                b = PB[2 + t % 2]
                if t >= 2:
                    pe.wait_ge(sg("a_qt_out"), t - 1)
                for j in range(4):
                    pe.transpose(b[:, j * P:(j + 1) * P], QKv[:, t, j * P:(j + 1) * P], ident)
                pe.transpose(PB[6][:, t * P:(t + 1) * P], QKv[:, t, 512:640], ident).then_inc(sg("a_qt"), 1)
            for t in range(NT):
                if t == 0:
                    pe.wait_ge(sg("a_qt_out"), NT + 1)
                    pe.wait_ge(sg("g_left"), 1)
                lo = max(t - 1, 0) * P
                n = (t + 1) * P - lo
                if t:
                    pe.wait_ge(sg("a_masked"), 4 * t)
                for g in range(2):
                    for j in range(4):
                        h = 4 * g + j
                        mm = pe.matmul(PB[h // 2][:, (h % 2) * 256 + 256 - n:(h % 2) * 256 + 256], qT[64 * g:64 * g + 64, j, t * P:(t + 1) * P],
                                       kT[64 * g:64 * g + 64, lo:lo + n], start=True, stop=True)
                        if h % 2:
                            mm.then_inc(sg("a_scores"), 1)
                pe.wait_ge(sg("a_exp"), AH * (t + 1))
                for hp in range(4):
                    if hp >= 2:
                        pe.wait_ge(sg("a_pt_out"), 4 * t + hp - 1)
                    for h in (2 * hp, 2 * hp + 1):
                        for b in range(0 if t else 1, 2):
                            mm = pe.transpose(PB[4 + hp % 2][:, (h % 2) * 256 + b * P:(h % 2) * 256 + (b + 1) * P], SC[:, h, b * P:(b + 1) * P], ident)
                    mm.then_inc(sg("a_pt"), 1)
                for h in range(AH):
                    pe.wait_ge(sg("a_pt_out"), 4 * t + h // 2 + 1)
                    if t and h == 0:
                        pe.wait_ge(sg("a_y"), t)
                    for b in range(0 if t else 1, 2):
                        mm = pe.matmul(PB[6][:, h * 64:(h + 1) * 64], PT[:, h, b * P:(b + 1) * P],
                                       A1[:, t - 1 + b, 640 + 64 * (h // 4):704 + 64 * (h // 4)], start=(b == (0 if t else 1)), stop=(b == 1))
                mm.then_inc(sg("a_pv"), 1)

        def attn_act(act, step):
            for n in range(8):
                t = n % 4
                act.wait_ge(sg("a_proj"), n + 1)
                if n < 4:
                    act.copy(A1[:, t, 512:776], PB[4 + n % 4][:, 0:264]).then_inc(sg("a_proj_out"), 1)
                else:
                    act.copy(A1[:, t, 0:512].rearrange("p (j g d) -> p g j d", j=4, g=2),
                             PB[4 + n % 4][:, :].rearrange("p (g j d) -> p g j d", g=2, j=4)).then_inc(sg("a_proj_out"), 1)
                if n == 3:
                    act.wait_ge(params_in, PARAMS)
                    act.wait_ge(sg("g_pre"), 1)
                    act.activation(g_e, g_abs, ACT.Exp, scale=-1.0)
                    act.activation(ea[:, 0:4], alog_b, ACT.Exp)
                    act.activation(beta.rearrange("p (t h) -> p t h", t=NT), A1[:, :, 772:776], ACT.Exp, scale=-1.0).then_inc(sg("g_exp"), 1)
                    act.wait_ge(sg("g_one"), 1)
                    act.activation(g_sp, g_e, ACT.Ln).then_inc(sg("g_ln"), 1)
            act.wait_ge(sg("a_proj_out"), 8)
            act.activation(sq_tmp, QKv, ACT.Square).then_inc(sg("a_sq"), 1)
            for t in range(NT):
                act.wait_ge(sg("a_qt"), t + 1)
                act.copy(qT[:, :, t * P:(t + 1) * P], PB[2 + t % 2][:, :].rearrange("p (j q) -> p j q", j=4)).then_inc(sg("a_qt_out"), 1)
            act.copy(kT, PB[6][:, :]).then_inc(sg("a_qt_out"), 1)
            for t in range(NT):
                act.wait_ge(sg("a_max"), t + 1)
                w = slice(0, 256) if t else slice(P, 256)
                for h in range(AH):
                    act.activation(SC[:, h, w], SC[:, h, w], ACT.Exp, bias=a_nmax[:, h:h + 1], accum_out=a_sum[:, h:h + 1]).then_inc(sg("a_exp"), 1)
                act.activation(a_sink, a_sink, ACT.Exp).then_inc(sg("a_sinkexp"), 1)
                for hp in range(4):
                    act.wait_ge(sg("a_pt"), 4 * t + hp + 1)
                    o = PT[:, 2 * hp:2 * hp + 2, w]
                    act.copy(o, PB[4 + hp % 2][:, :].rearrange("p (h n) -> p h n", h=2)[:, :, w]).then_inc(sg("a_pt_out"), 1)

        def attn_pool(pool, step):
            pool.wait_ge(sg("a_sums"), 1)
            step.then(pool.tensor_scalar(a_rs, a_ss, 1.0 / ADH, EPS, ALU.mult, ALU.add))
            pool.tensor_tensor(a_rs, a_rs, mhalf[:, 0:40], ALU.pow).then_inc(sg("a_rstd"), 1)

        def attn_dve(dve, step):
            dve.wait_ge(params_in, PARAMS)
            dve.wait_ge(sg("a_proj_out"), 4)
            gv = lambda a: a.rearrange("p (t h) -> p t h", t=NT)
            bh = lambda a: a[:, None, :].to_broadcast([P, NT, 4])
            step.then(dve.tensor_tensor(gv(g_raw), A1[:, :, 768:772], bh(dtb_b), ALU.add))
            step.then(dve.tensor_scalar(g_val, g_raw, -1.0, None, ALU.mult))
            dve.tensor_tensor(g_abs, g_val, g_raw, ALU.max).then_inc(sg("g_pre"), 1)
            step.then(dve.tensor_scalar(g_raw, g_raw, 0.0, None, ALU.max))
            dve.wait_ge(sg("g_exp"), 1)
            dve.tensor_scalar(g_e, g_e, 1.0, None, ALU.add).then_inc(sg("g_one"), 1)
            step.then(dve.tensor_scalar(beta, beta, 1.0, None, ALU.add))
            step.then(dve.reciprocal(beta, beta))
            dve.wait_ge(sg("g_ln"), 1)
            step.then(dve.tensor_tensor(g_raw, g_raw, g_sp, ALU.add))
            dve.scalar_tensor_tensor(gv(g_val), gv(g_raw), -1.0, bh(ea[:, 0:4]), ALU.mult, ALU.mult).then_inc(sg("g_gates"), 1)
            dve.wait_ge(sg("a_sq"), 1)
            dve.tensor_reduce(a_ss.rearrange("p (t h) -> p t h", t=NT), sq_tmp.rearrange("p t (h d) -> p t h d", d=ADH), AX, ALU.add).then_inc(sg("a_sums"), 1)
            dve.wait_ge(sg("a_rstd"), 1)
            dve.wait_ge(sg("a_proj_out"), 8)
            for t in range(NT):
                v = QKv[:, t, :].rearrange("p (h d) -> p h d", d=ADH)
                step(dve.tensor_tensor(v, v, a_rs[:, t * 10:(t + 1) * 10, None].to_broadcast([P, AQK, ADH]), ALU.mult))
            step.wait()
            step.then(dve.tensor_tensor(QKv, QKv, qk_gain[:, None, :].to_broadcast([P, NT, 640]), ALU.mult))
            x1 = [QKv[:, t, :].rearrange("p (h d) -> p h d", d=ADH)[:, :, 0:8] for t in range(NT)]
            x2 = [QKv[:, t, :].rearrange("p (h d) -> p h d", d=ADH)[:, :, 8:16] for t in range(NT)]
            rot = [[rt[:, a, t * 80:(t + 1) * 80].rearrange("p (h d) -> p h d", d=8) for t in range(NT)] for a in range(4)]
            for t in range(NT):
                cs = const("rcos")[:, None, t * 8:(t + 1) * 8].to_broadcast([P, AQK, 8])
                sn = const("rsin")[:, None, t * 8:(t + 1) * 8].to_broadcast([P, AQK, 8])
                step(dve.tensor_tensor(rot[0][t], x1[t], cs, ALU.mult))
                step(dve.tensor_tensor(rot[1][t], x2[t], sn, ALU.mult))
                step(dve.tensor_tensor(rot[2][t], x2[t], cs, ALU.mult))
                step(dve.tensor_tensor(rot[3][t], x1[t], sn, ALU.mult))
            step.wait()
            for t in range(NT):
                step(dve.tensor_tensor(x1[t], rot[0][t], rot[1][t], ALU.subtract))
                step(dve.tensor_tensor(x2[t], rot[2][t], rot[3][t], ALU.add))
            step.wait()
            dve.tensor_copy(rt[:, 0, 0:1], rt[:, 0, 0:1]).then_inc(sg("a_rope"), 1)
            dve.wait_ge(sg("g_cum"), 1)
            step(dve.tensor_copy(G_col, PB[0][:, 0:16]))
            step(dve.tensor_copy(GL_col, PB[1][:, 0:16]))
            step.wait()
            dve.tensor_tensor(GL_col, GL_col, G_col, ALU.subtract).then_inc(sg("g_left"), 1)
            for t in range(NT):
                w = slice(0, 256) if t else slice(P, 256)
                n = 256 if t else P
                for b in range(4):
                    dve.wait_ge(sg("a_scores"), 4 * t + b + 1)
                    dve.scalar_tensor_tensor(SC[:, 2 * b:2 * b + 2, w], PB[b][:, :].rearrange("p (h n) -> p h n", h=2)[:, :, w], ADH ** -0.5,
                                             const("window")[:, None, w].to_broadcast([P, 2, n]), ALU.mult, ALU.add).then_inc(sg("a_masked"), 1)
                dve.wait_ge(sg("a_masked"), 4 * (t + 1))
                step.then(dve.tensor_reduce(a_max, SC[:, :, w], AX, ALU.max))
                step.then(dve.tensor_tensor(a_max, a_max, sink_b, ALU.max))
                step(dve.tensor_tensor(a_sink, sink_b, a_max, ALU.subtract))
                step.wait()
                dve.tensor_scalar(a_nmax, a_max, -1.0, None, ALU.mult).then_inc(sg("a_max"), 1)
                dve.wait_ge(sg("a_exp"), AH * (t + 1))
                dve.wait_ge(sg("a_sinkexp"), t + 1)
                step.then(dve.tensor_tensor(a_rec, a_sum, a_sink, ALU.add))
                step.then(dve.reciprocal(a_rec, a_rec))
                dve.wait_ge(sg("a_pv"), t + 1)
                dve.tensor_tensor(XN[:, t, 0:512].rearrange("p (h d) -> p h d", h=AH), PB[6][:, :].rearrange("p (h d) -> p h d", h=AH),
                                  a_rec[:, :, None].to_broadcast([P, AH, ADH]), ALU.mult).then_inc(sg("a_y"), 1)

        s_.n = mixed
        b512 = lambda: s_(512)
        t4 = lambda a: a.rearrange("p (t n) -> p t n", t=NT)
        xc = s_(3 * 515 + 3)[:, 0:3 * 515].rearrange("p (s n) -> p s n", s=3)
        cv = s_(3 * 512).rearrange("p (s n) -> p s n", s=3)
        sqk = s_(1024).rearrange("p (s n) -> p s n", s=2)
        N1, nwT = t4(sqk[:, 0, :]), t4(sqk[:, 1, :])
        e_dec, e_decT, eGB, Tm, TTm, Cm = (t4(b512()) for _ in range(6))
        qd, kbg, kd, vb, zs, og = (t4(b512()) for _ in range(6))
        Lm, ATg = e_dec, e_decT
        VN, St = s_(128), s_(128)
        n_ss, n_rs, o_ss, o_rs = small(8), small(8), small(4), small(4)

        def gdn_pe(pe):
            pe.wait_ge(params_in, PARAMS)
            pe.transpose(PB[7][:, 0:48], cwr[0:48, :], ident[0:48, 0:48]).then_inc(sg("d_cw"), 1)
            for h in range(GH):
                c = c_gdn + h
                pe.wait_ge(w_landed[c % RING], landed(c))
                w = slot_of(c).rearrange("p (k s n) -> p k s n", k=KT, s=4)
                if h:
                    pe.wait_ge(sg("d_y"), h)
                for s in range(3):
                    for k in range(KT):
                        mm = pe.matmul(PB[s][:, :], w[:, k, s, :], HT[:, k, :], start=(k == 0), stop=(k == KT - 1))
                    mm.then_inc(sg("d_proj"), 1)
                for t in range(NT):
                    for k in range(KT):
                        mm = pe.matmul(PB[3][:, t * P:(t + 1) * P], HT[:, k, t * P:(t + 1) * P], w[:, k, 3, :], start=(k == 0), stop=(k == KT - 1))
                mm.then_inc(sg("d_z"), 1)
                for t in range(NT):
                    mm = pe.matmul(PB[4][:, t * P:(t + 1) * P], g_val[:, 4 * t + h:4 * t + h + 1].to_broadcast([P, P]), const("cum"), start=True, stop=True)
                mm.then_inc(sg("d_gb"), 1)
                pe.wait_ge(sg("d_sq"), h + 1)
                for s in range(2):
                    for t in range(NT):
                        mm = pe.matmul(PB[5][:, 4 * s + t:4 * s + t + 1], sqk[:, s, t * P:(t + 1) * P], ones[:, 0:1], start=True, stop=True)
                mm.then_inc(sg("d_ss"), 1)
                pe.wait_ge(sg("d_rs"), h + 1)
                for s in range(2):
                    for t in range(NT):
                        mm = pe.matmul(PB[6 + s][:, t * P:(t + 1) * P], n_rs[:, 4 * s + t:4 * s + t + 1].to_broadcast([P, P]), ident, start=True, stop=True)
                mm.then_inc(sg("d_rb"), 1)
                pe.wait_ge(sg("d_qk"), h + 1)
                for t in range(NT):
                    mm = pe.matmul(PB[t // 2][:, (t % 2) * 256:(t % 2) * 256 + 256], cv[:, 1, t * P:(t + 1) * P], cv[:, 0:2, t * P:(t + 1) * P],
                                   start=True, stop=True)
                mm.then_inc(sg("d_kk"), 1)
                for s in range(2):
                    for t in range(NT):
                        mm = pe.transpose(PB[2 + 3 * s][:, t * P:(t + 1) * P], cv[:, 1 + s, t * P:(t + 1) * P], ident)
                mm.then_inc(sg("d_kv"), 1)
                for lv in range(LEVELS):
                    pe.wait_ge(sg("d_T"), LEVELS * h + lv + 1)
                    for t in range(NT):
                        mm = pe.matmul(PB[6][:, t * P:(t + 1) * P], Cm[:, t, :], TTm[:, t, :] if lv else ident, start=True, stop=True)
                    mm.then_inc(sg("d_n1"), 1)
                    if lv == 0:
                        continue
                    pe.wait_ge(sg("d_n1_out"), (LEVELS - 1) * h + lv)
                    for t in range(NT):
                        mm = pe.matmul(PB[7][:, t * P:(t + 1) * P], Tm[:, t, :], N1[:, t, :], start=True, stop=True)
                    mm.then_inc(sg("d_tt"), 1)
                    if lv < LEVELS - 1:
                        for t in range(NT):
                            mm = pe.matmul(PB[4][:, t * P:(t + 1) * P], N1[:, t, :], Tm[:, t, :], start=True, stop=True)
                        mm.then_inc(sg("d_t"), 1)
                pe.wait_ge(sg("d_inv"), h + 1)
                pe.wait_ge(sg("d_scaled"), h + 1)
                for t in range(NT):
                    mm = pe.matmul(PB[6][:, t * P:(t + 1) * P], kbg[:, t, :], TTm[:, t, :], start=True, stop=True)
                mm.then_inc(sg("d_w"), 1)
                pe.wait_ge(sg("d_w_out"), h + 1)
                pe.wait_ge(sg("d_qd"), h + 1)
                for n in range(2 * NT):
                    t, half = n // 2, (n % 2) * CH
                    r, m = slice(half, half + CH), n % 2
                    pe.matmul(PB[m][r, 0:GD], TTm[:, t, r], vb[:, t, :], start=True, stop=False)
                    pe.wait_ge(sg("d_S"), (2 * NT + 1) * h + n + 1)
                    pe.matmul(PB[m][r, 0:GD], nwT[:, t, r], St, start=False, stop=True).then_inc(sg("d_v"), 1)
                    ob = PB[3 + 4 * m]
                    if n >= 2:
                        pe.wait_ge(sg("d_o_out"), (2 * NT) * h + n - 1)
                    pe.matmul(ob[r, 0:GD], qd[:, t, r], St, start=True, stop=False)
                    pe.wait_ge(sg("d_v_out"), (2 * NT) * h + n + 1)
                    pe.matmul(ob[r, 0:GD], ATg[r, t, r], VN[r, :], start=False, stop=True).then_inc(sg("d_o"), 1)
                    pe.matmul(PB[5][:, 0:GD], kd[r, t, :], VN[r, :], start=True, stop=True).then_inc(sg("d_kv_new"), 1)

        def gdn_act(act, step):
            for h in range(GH):
                for s in range(3):
                    act.wait_ge(sg("d_proj"), 3 * h + s + 1)
                    if h == 0 and s == 0:
                        act.wait_ge(sg("d_pad"), 1)
                    act.copy(xc[:, s, 3:515], PB[s][:, :]).then_inc(sg("d_x"), 1)
                for s in range(3):
                    act.wait_ge(sg("d_conv"), 3 * h + s + 1)
                    act.activation(cv[:, s, :], cv[:, s, :], ACT.Silu).then_inc(sg("d_silu"), 1)
                act.wait_ge(sg("d_z"), h + 1)
                act.activation(zs, t4(PB[3][:, :]), ACT.Silu).then_inc(sg("d_zs"), 1)
                act.wait_ge(sg("d_silu"), 3 * h + 3)
                act.activation(sqk, cv[:, 0:2, :], ACT.Square).then_inc(sg("d_sq"), 1)
                if h == 0:
                    act.wait_ge(sg("g_left"), 1)
                    act.activation(kd_scale, GL_col, ACT.Exp).then_inc(sg("d_eg"), 1)
                    act.activation(eG, G_col, ACT.Exp).then_inc(sg("d_eg"), 1)
                    act.wait_ge(sg("d_eg"), 2)
                act.wait_ge(sg("d_diff"), h + 1)
                act.activation(eGB, t4(PB[4][:, :]), ACT.Exp).then_inc(sg("d_egb"), 1)
                act.activation(e_dec, e_dec, ACT.Exp).then_inc(sg("d_dec"), 1)
                act.activation(e_decT, e_decT, ACT.Exp, scale=-1.0).then_inc(sg("d_dec"), 1)
                act.wait_ge(sg("d_kv"), h + 1)
                act.wait_ge(sg("d_kbs"), 1)
                for t in range(NT):
                    c = slice(4 * t + h, 4 * t + h + 1)
                    step(act.activation(kbg[:, t, :], PB[2][:, t * P:(t + 1) * P], ACT.Copy, scale=kb_scale[:, c]))
                    step(act.activation(kd[:, t, :], PB[2][:, t * P:(t + 1) * P], ACT.Copy, scale=kd_scale[:, c]))
                    last = act.activation(vb[:, t, :], PB[5][:, t * P:(t + 1) * P], ACT.Copy, scale=beta[:, c])
                    if t < NT - 1:
                        step(last)
                step.wait()
                last.then_inc(sg("d_scaled"), 1)
                for lv in range(1, LEVELS):
                    act.wait_ge(sg("d_n1"), LEVELS * h + lv + 1)
                    act.copy(N1, t4(PB[6][:, :])).then_inc(sg("d_n1_out"), 1)
                act.wait_ge(sg("d_w"), h + 1)
                act.activation(nwT, t4(PB[6][:, :]), ACT.Copy, scale=-1.0).then_inc(sg("d_w_out"), 1)
                for n in range(2 * NT):
                    t, half = n // 2, (n % 2) * CH
                    r, m = slice(half, half + CH), n % 2
                    act.wait_ge(sg("d_v"), (2 * NT) * h + n + 1)
                    act.copy(VN[r, :], PB[m][r, 0:GD]).then_inc(sg("d_v_out"), 1)
                    act.wait_ge(sg("d_o"), (2 * NT) * h + n + 1)
                    act.copy(og[r, t, :], PB[3 + 4 * m][r, 0:GD]).then_inc(sg("d_o_out"), 1)
                act.wait_ge(sg("d_o_out"), (2 * NT) * (h + 1))
                for t in range(NT):
                    ins = act.activation(N1[:, t, :], og[:, t, :], ACT.Square, accum_out=o_ss[:, t:t + 1])
                    ins.then_inc(sg("d_oss"), 1)

        def gdn_pool(pool, step):
            for h in range(GH):
                pool.wait_ge(sg("d_ss_out"), h + 1)
                step.then(pool.tensor_scalar(n_rs, n_ss, 1.0, EPS, ALU.mult, ALU.add))
                step.then(pool.tensor_tensor(n_rs, n_rs, mhalf[:, 0:8], ALU.pow))
                pool.tensor_scalar(n_rs[:, 0:4], n_rs[:, 0:4], GD ** -0.5, None, ALU.mult).then_inc(sg("d_rs"), 1)
                pool.wait_ge(sg("d_oss"), NT * (h + 1))
                step.then(pool.tensor_scalar(o_rs, o_ss, 1.0 / GD, EPS, ALU.mult, ALU.add))
                pool.tensor_tensor(o_rs, o_rs, mhalf[:, 0:4], ALU.pow).then_inc(sg("d_ors"), 1)

        def gdn_dve(dve, step):
            dve.wait_ge(sg("a_pv"), NT)
            step(dve.memset(xc[:, :, 0:3], 0.0))
            step.wait()
            dve.memset(VN, 0.0).then_inc(sg("d_pad"), 1)
            dve.wait_ge(sg("d_cw"), 1)
            step(dve.tensor_copy(cw, PB[7][:, 0:48]))
            step.wait()
            for h in range(GH):
                for s in range(3):
                    dve.wait_ge(sg("d_x"), 3 * h + s + 1)
                    tap = lambda i: cw[:, i * 12 + 4 * s + h:i * 12 + 4 * s + h + 1]
                    step.then(dve.tensor_scalar(cv[:, s, :], xc[:, s, 0:512], tap(0), None, ALU.mult))
                    for i in (1, 2):
                        step.then(dve.scalar_tensor_tensor(cv[:, s, :], xc[:, s, i:i + 512], tap(i), cv[:, s, :], ALU.mult, ALU.add))
                    dve.scalar_tensor_tensor(cv[:, s, :], xc[:, s, 3:515], tap(3), cv[:, s, :], ALU.mult, ALU.add).then_inc(sg("d_conv"), 1)
                dve.wait_ge(sg("d_gb"), h + 1)
                Gi = G_col.rearrange("p (t h) -> p t h", h=4)[:, :, h:h + 1].to_broadcast([P, NT, P])
                step.then(dve.tensor_tensor(e_dec, Gi, t4(PB[4][:, :]), ALU.subtract))
                step.then(dve.tensor_scalar(e_decT, e_dec, 0.0, None, ALU.max))
                dve.tensor_scalar(e_dec, e_dec, 0.0, None, ALU.min).then_inc(sg("d_diff"), 1)
                dve.wait_ge(sg("d_ss"), h + 1)
                dve.tensor_copy(n_ss, PB[5][:, 0:8]).then_inc(sg("d_ss_out"), 1)
                if h == 0:
                    dve.wait_ge(sg("d_eg"), 2)
                    dve.tensor_tensor(kb_scale, beta, eG, ALU.mult).then_inc(sg("d_kbs"), 1)
                dve.wait_ge(sg("d_rb"), h + 1)
                dve.wait_ge(sg("d_silu"), 3 * h + 3)
                dve.wait_ge(sg("d_sq"), h + 1)
                step(dve.tensor_tensor(cv[:, 0, :], cv[:, 0, :], PB[6][:, :], ALU.mult))
                step.wait()
                dve.tensor_tensor(cv[:, 1, :], cv[:, 1, :], PB[7][:, :], ALU.mult).then_inc(sg("d_qk"), 1)
                dve.wait_ge(sg("d_egb"), h + 1)
                dve.tensor_tensor(qd, t4(cv[:, 0, :]), eGB, ALU.mult).then_inc(sg("d_qd"), 1)
                dve.wait_ge(sg("d_dec"), 2 * h + 2)
                for t in range(NT):
                    step(dve.scalar_tensor_tensor(e_dec[:, t, :], e_dec[:, t, :], beta[:, 4 * t + h:4 * t + h + 1], const("strict"), ALU.mult, ALU.mult))
                step(dve.tensor_tensor(e_decT, e_decT, const("inclT")[:, None, :].to_broadcast([P, NT, P]), ALU.mult))
                step.wait()
                dve.wait_ge(sg("d_kk"), h + 1)
                for b in range(2):
                    kk = PB[b][:, :].rearrange("p (t s n) -> p t s n", t=2, s=2)
                    step(dve.tensor_tensor(Lm[:, 2 * b:2 * b + 2, :], kk[:, :, 1, :], e_dec[:, 2 * b:2 * b + 2, :], ALU.mult))
                    step(dve.tensor_tensor(ATg[:, 2 * b:2 * b + 2, :], kk[:, :, 0, :], e_decT[:, 2 * b:2 * b + 2, :], ALU.mult))
                step.wait()
                bc = lambda name: const(name)[:, None, :].to_broadcast([P, NT, P])
                for lv in range(LEVELS):
                    dve.tensor_tensor(Cm, Lm, bc(f"level{lv}"), ALU.mult).then_inc(sg("d_T"), 1)
                    if lv == 0:
                        dve.wait_ge(sg("d_T"), LEVELS * h + 1)
                        step(dve.tensor_tensor(Tm, bc("ident"), Cm, ALU.subtract))
                        dve.wait_ge(sg("d_n1"), LEVELS * h + 1)
                        step.then(dve.tensor_tensor(TTm, bc("ident"), t4(PB[6][:, :]), ALU.subtract))
                        continue
                    dve.wait_ge(sg("d_tt"), (LEVELS - 1) * h + lv)
                    last = dve.tensor_tensor(TTm, TTm, t4(PB[7][:, :]), ALU.subtract)
                    if lv == LEVELS - 1:
                        last.then_inc(sg("d_inv"), 1)
                    else:
                        step(last)
                        dve.wait_ge(sg("d_t"), (LEVELS - 2) * h + lv)
                        step(dve.tensor_tensor(Tm, Tm, t4(PB[4][:, :]), ALU.subtract))
                        step.wait()
                dve.memset(St, 0.0).then_inc(sg("d_S"), 1)
                for n in range(2 * NT):
                    t, half = n // 2, (n % 2) * CH
                    dve.wait_ge(sg("d_S"), (2 * NT + 1) * h + n + 1)
                    dve.wait_ge(sg("d_kv_new"), (2 * NT) * h + n + 1)
                    dve.scalar_tensor_tensor(St, St, eGB[:, t, half + CH - 1:half + CH], PB[5][:, 0:GD], ALU.mult, ALU.add).then_inc(sg("d_S"), 1)
                dve.wait_ge(sg("d_ors"), h + 1)
                dve.wait_ge(sg("d_zs"), h + 1)
                for t in range(NT):
                    step(dve.scalar_tensor_tensor(og[:, t, :], og[:, t, :], o_rs[:, t:t + 1], gdn_gain, ALU.mult, ALU.mult))
                step.wait()
                dve.tensor_tensor(XN[:, :, 512 + h * GD:512 + (h + 1) * GD], og, zs, ALU.mult).then_inc(sg("d_y"), 1)


        def oute_pe(pe):
            pe.wait_ge(sg("d_y"), GH)
            for n in range(8):
                t, g = n // 2, n % 2
                if n >= 4:
                    pe.wait_ge(sg(("m_tr_a", "m_tr_d")[g]), (n - 4) // 2 + 1)
                for j in range(4):
                    mm = pe.transpose(PB[n % 4][:, j * P:(j + 1) * P], XN[:, t, g * 512 + j:(g + 1) * 512:4], ident)
                mm.then_inc(sg("m_tr"), 1)
            for g in range(2):
                pe.wait_ge(w_landed[(c_oute + g) % RING], landed(c_oute + g))
            for n in range(8):
                t, half = n // 2, n % 2
                pe.wait_ge(sg("m_tr_a"), t + 1)
                pe.wait_ge(sg("m_tr_d"), t + 1)
                if n >= 4:
                    pe.wait_ge(resid, n - 3)
                for g in range(2):
                    w = slot_of(c_oute + g).rearrange("p (k n) -> p k n", k=4)
                    for j in range(4):
                        mm = pe.matmul(PB[4 + n % 4][:, :], HT[:, 4 * g + j, t * P:(t + 1) * P], w[:, j, half * 512:(half + 1) * 512],
                                       start=(g + j == 0), stop=(g == 1 and j == 3))
                mm.then_inc(sg("m_out"), 1)

        def oute_act(act):
            for t in range(NT):
                act.wait_ge(sg("m_tr"), 2 * t + 1)
                act.copy(HT[:, 0:4, t * P:(t + 1) * P], PB[(2 * t) % 4][:, :].rearrange("p (k q) -> p k q", k=4)).then_inc(sg("m_tr_a"), 1)

        def oute_dve(dve):
            for t in range(NT):
                dve.wait_ge(sg("m_tr"), 2 * t + 2)
                dve.tensor_copy(HT[:, 4:8, t * P:(t + 1) * P], PB[(2 * t + 1) % 4][:, :].rearrange("p (k q) -> p k q", k=4)).then_inc(sg("m_tr_d"), 1)
            for n in range(8):
                t, half = n // 2, n % 2
                dve.wait_ge(sg("m_out"), n + 1)
                xs = X[:, t, half * 512:(half + 1) * 512]
                dve.tensor_tensor(xs, xs, PB[4 + n % 4][:, :], ALU.add).then_inc(resid, 1)

        s_.n, s_.size = 0, CO_AT
        OH = [s_(NT * SLOTS).rearrange("p (t s) -> p t s", t=NT) for _ in range(2)]
        XG, XTt, SIL, HH = s_(512), s_(512), s_(512), s_(512)
        HHT = s_(4 * SLOTS)
        YS = [s_(512) for _ in range(2)]
        WOV = s_(SLOT)
        OHG, OT = s_(512), s_(512)
        tg = lambda a: a.rearrange("p (t n) -> p t n", t=NT)
        LG = tg(s_(NT * NR))
        dg, eg, selg, ohg = (tg(s_(16)) for _ in range(4))
        EL4 = s_(NT * 32).rearrange("p (t e g) -> p t e g", t=NT, g=NG)
        EL, EL2, dd, sel, oh1, oh2 = (tg(s_(NT * EPG)) for _ in range(6))
        gmax, vmax, m1, m2, e2, gate1, gate2, rsg, used1, used2 = (s_(NT) for _ in range(10))
        M1, M2, MM, POS, POSM, T1, INR = (tg(s_(NT * NE)) for _ in range(7))
        dest_f = s_(2 * NT)
        cnt_f = s_(1)
        dest = sb("dest", [P, 2 * NT], I32)
        cnt = sb("cnt", [P, 1], I32)
        y_view = y_rows.rearrange("(e r) (h n) -> e r h n", e=NE, h=2)

        PER_LAYER = dict(logits=1, masks=1, counts=1, gdiff=1, ediff=1, rexp=2, routed=1, rows_stored=1, first_added=NT,
                         stored0=16 * NE, stored1=16 * NE,
                         **dict.fromkeys(("oh", "gat", "xg", "xt", "xt_out", "gu", "sil", "hh", "ht", "ht_out", "y", "y_out"), NE))

        def moe_sem(l, name):
            return sg(f"m_{name}" if name in PER_LAYER else f"m{l}_{name}")

        OVER = dict(pe=("v_gat", "v_xt", "v_g", "v_u", "v_ht", "v_y", "v_ot", "v_comb"), act=("v_xg", "v_sil", "v_ht_out"),
                    dve=("v_oh", "v_ohg", "v_xt_out", "v_hh", "v_y_out", "v_added"))

        def over_done(l, name):
            return next(sg(f"m{l}_over_{eng}") for eng, stages in OVER.items() if name in stages)

        def over_wait(l, name, n):
            stages = next(x for x in OVER.values() if name in x)
            return over_done(l, name), n * len(stages) + stages.index(name) + 1

        def moe_wait(l, name, value):
            return moe_sem(l, name), value + l * PER_LAYER.get(name, 0)

        def one_hot(dve, step, out_oh, diff):
            n = out_oh.shape[2]
            step.then(dve.tensor_scalar(out_oh, diff, 0.0, None, ALU.is_equal))
            step.then(dve.tensor_tensor(out_oh, out_oh, const("first")[:, None, 0:n].to_broadcast([P, NT, n]), ALU.mult))
            step.then(dve.tensor_reduce(vmax, out_oh, AX, ALU.max))
            step.then(dve.tensor_tensor(out_oh, out_oh, vmax[:, :, None].to_broadcast([P, NT, n]), ALU.is_equal))

        def route_pool(pool, l):
            if l:
                pool.wait_ge(*moe_wait(0, "logits", 1))
                pool.wait_ge(*moe_wait(0, "routed", 1))
            pool.dma_start(WR[:, :, 0:NG], k_rows(w_router_group[l], 0, NG)).then_inc(router_in, 16)
            pool.dma_start(WR[:, :, NG:NR], k_rows(w_router_expert[l], 0, NE)).then_inc(router_in, 16)
            pool.dma_start(br[:, 0:NG], b_router_group[l:l + 1, :].to_broadcast([P, NG])).then_inc(router_in, 16)
            pool.dma_start(br[:, NG:NR], b_router_expert[l:l + 1, :].to_broadcast([P, NE])).then_inc(router_in, 16)

        def route_pe(pe, l):
            ms = lambda n: moe_sem(l, n)
            mw = lambda n, v: moe_wait(l, n, v)
            pe.wait_ge(router_in, 64 * (l + 1))
            for t in range(NT):
                for k in range(KT):
                    mm = pe.matmul(PB[4][:, t * NR:(t + 1) * NR], HT[:, k, t * P:(t + 1) * P], WR[:, k, :], start=(k == 0), stop=(k == KT - 1))
            mm.then_inc(ms("logits"), 1)
            pe.wait_ge(*mw("masks", 1))
            for t in range(NT):
                pe.matmul(PB[5][:, t * NE:(t + 1) * NE], const("before"), MM[:, t, :], start=True, stop=(t == 0))
                for u in range(t):
                    pe.matmul(PB[5][:, t * NE:(t + 1) * NE], ones, MM[:, u, :], start=False, stop=(u == t - 1))
            for u in range(NT):
                mm = pe.matmul(PB[5][:, NT * NE:(NT + 1) * NE], ones, MM[:, u, :], start=(u == 0), stop=(u == NT - 1))
            mm.then_inc(ms("counts"), 1)

        def route_act(act, l):
            ms = lambda n: moe_sem(l, n)
            mw = lambda n, v: moe_wait(l, n, v)
            act.wait_ge(*mw("gdiff", 1))
            act.activation(eg, dg, ACT.Exp).then_inc(ms("rexp"), 1)
            act.wait_ge(*mw("ediff", 1))
            act.activation(e2, m2, ACT.Exp).then_inc(ms("rexp"), 1)

        def route_dve(dve, l, step):
            ms = lambda n: moe_sem(l, n)
            mw = lambda n, v: moe_wait(l, n, v)
            bt = lambda a, n: a[:, :, None].to_broadcast([P, NT, n])
            dve.wait_ge(*mw("logits", 1))
            dve.wait_ge(router_in, 64 * (l + 1))
            step.then(dve.tensor_tensor(LG, tg(PB[4][:, 0:NT * NR]), br[:, None, :].to_broadcast([P, NT, NR]), ALU.add))
            step.then(dve.tensor_reduce(gmax, LG[:, :, 0:NG], AX, ALU.max))
            dve.tensor_tensor(dg, LG[:, :, 0:NG], bt(gmax, NG), ALU.subtract).then_inc(ms("gdiff"), 1)
            dve.wait_ge(*mw("gdiff", 1))
            one_hot(dve, step, ohg, dg)
            step.then(dve.tensor_tensor(EL4, LG[:, :, NG:NR].rearrange("p t (g e) -> p t e g", g=NG),
                                        ohg[:, :, None, :].to_broadcast([P, NT, EPG, NG]), ALU.mult))
            step.then(dve.tensor_reduce(EL, EL4, AX, ALU.add))
            step.then(dve.tensor_reduce(m1, EL, AX, ALU.max))
            step.then(dve.tensor_tensor(dd, EL, bt(m1, EPG), ALU.subtract))
            one_hot(dve, step, oh1, dd)
            step.then(dve.scalar_tensor_tensor(EL2, oh1, -BIG, EL, ALU.mult, ALU.add))
            step.then(dve.tensor_reduce(m2, EL2, AX, ALU.max))
            step.then(dve.tensor_tensor(dd, EL2, bt(m2, EPG), ALU.subtract))
            one_hot(dve, step, oh2, dd)
            dve.tensor_tensor(m2, m2, m1, ALU.subtract).then_inc(ms("ediff"), 1)
            for M, oh in ((M1, oh1), (M2, oh2)):
                step(dve.tensor_tensor(M.rearrange("p t (g e) -> p t g e", g=NG), ohg[:, :, :, None].to_broadcast([P, NT, NG, EPG]),
                                       oh[:, :, None, :].to_broadcast([P, NT, NG, EPG]), ALU.mult))
            step.wait()
            dve.tensor_tensor(MM, M1, M2, ALU.add).then_inc(ms("masks"), 1)
            dve.wait_ge(*mw("rexp", 2))
            step.then(dve.tensor_reduce(rsg, eg, AX, ALU.add))
            step.then(dve.scalar_tensor_tensor(gate1, e2, 1.0, rsg, ALU.add, ALU.mult))
            step.then(dve.reciprocal(gate1, gate1))
            step.then(dve.tensor_tensor(gate2, gate1, e2, ALU.mult))
            dve.wait_ge(*mw("counts", 1))
            dve.wait_ge(*mw("masks", 1))
            step(dve.tensor_copy(POS, tg(PB[5][:, 0:NT * NE])))
            step.then(dve.tensor_reduce(cnt_f, PB[5][:, NT * NE:(NT + 1) * NE], AX, ALU.max))
            step(dve.tensor_copy(cnt[:, :], cnt_f))
            step.then(dve.scalar_tensor_tensor(POSM, POS, 1.0, MM, ALU.add, ALU.mult))
            step(dve.tensor_scalar(POSM, POSM, -1.0, None, ALU.add))
            step.then(dve.tensor_scalar(INR, POS, float(SLOTS), None, ALU.is_lt))
            step.then(dve.tensor_tensor(POS, POS, const("rowbase")[:, None, :].to_broadcast([P, NT, NE]), ALU.add))
            for k, (M, gate, used) in enumerate(((M1, gate1, used1), (M2, gate2, used2))):
                step.then(dve.tensor_tensor(T1, INR, M, ALU.mult))
                step.then(dve.tensor_reduce(used, T1, AX, ALU.add))
                step.then(dve.tensor_tensor(used, used, gate, ALU.mult))
                step.then(dve.tensor_tensor(T1, POS, T1, ALU.mult))
                step.then(dve.tensor_reduce(dest_f[:, k * NT:(k + 1) * NT], T1, AX, ALU.add))
            dve.tensor_copy(dest[:, :], dest_f).then_inc(ms("routed"), 1)
            dve.wait_ge(*mw("routed", 1))

        BX, BXT, BGU, BH, BY = PB[0], PB[1], PB[2], PB[3], PB[6]

        def gather_mm(pe, oh):
            for t in range(NT):
                for half in range(2):
                    mm = pe.matmul(BX[64 * half:64 * half + 64, :], oh[:, t, :], XN[:, t, half * 512:(half + 1) * 512], start=(t == 0), stop=(t == NT - 1))
            return mm

        def xt_mm(pe):
            for j in range(4):
                mm = pe.transpose(BXT[:, j * P:(j + 1) * P], XG[:, j:512:4], ident)
            return mm

        def x_tile(k):
            a = (k // 2) * P + (k % 2) * SLOTS
            return XTt[:, a:a + SLOTS]

        def ht_mm(pe):
            for j in range(4):
                mm = pe.transpose(BH[:, j * SLOTS:(j + 1) * SLOTS], HH[0:SLOTS, j:512:4], ident[0:SLOTS, 0:SLOTS])
            return mm

        def down_mm(pe, w):
            for j in range(4):
                for half in range(2):
                    mm = pe.matmul(BY[64 * half:64 * half + 64, :], HHT[:, j * SLOTS:(j + 1) * SLOTS], w[:, j, half * 512:(half + 1) * 512],
                                   start=(j == 0), stop=(j == 3))
            return mm

        def w_need(l, u, j, i):
            c = c_moe[l] + 3 * u + j
            return w_landed[c % RING], landed(c) + 16 * i

        def experts_pe(pe, l):
            ms = lambda n: moe_sem(l, n)
            mw = lambda n, v: moe_wait(l, n, v)

            def expert(i, u, last=False):
                e = 2 * i + u
                for j in range(2):
                    pe.wait_ge(*w_need(l, u, j, i))
                pe.wait_ge(*mw("xt_out", e + 1))
                wg, wu, wd = (slot_of(c_moe[l] + 3 * u + j).rearrange("p (k n) -> p k n", k=k) for j, k in ((0, KT), (1, KT), (2, 4)))
                for k in range(KT):
                    pe.matmul(BGU[0:SLOTS, :], x_tile(k), wg[:, k, :], start=(k == 0), stop=(k == KT - 1))
                    mm = pe.matmul(BGU[SLOTS:2 * SLOTS, :], x_tile(k), wu[:, k, :], start=(k == 0), stop=(k == KT - 1))
                mm.then_inc(ms("gu"), 1)
                if not last:
                    pe.wait_ge(*mw("oh", e + 2))
                    gather_mm(pe, OH[(u + 1) % 2]).then_inc(ms("gat"), 1)
                pe.wait_ge(*mw("hh", e + 1))
                if not last:
                    pe.wait_ge(*mw("xg", e + 2))
                    xt_mm(pe).then_inc(ms("xt"), 1)
                ht_mm(pe).then_inc(ms("ht"), 1)
                pe.wait_ge(*mw("ht_out", e + 1))
                pe.wait_ge(*w_need(l, u, 2, i))
                if not (isinstance(i, int) and i == 0 and u == 0):
                    pe.wait_ge(*mw("y_out", e))
                down_mm(pe, wd).then_inc(ms("y"), 1)

            pe.wait_ge(*mw("oh", 1))
            gather_mm(pe, OH[0]).then_inc(ms("gat"), 1)
            pe.wait_ge(*mw("xg", 1))
            xt_mm(pe).then_inc(ms("xt"), 1)
            expert(0, 0)
            expert(0, 1)
            with pe.Fori(1, NE // 2 - 1) as i:
                expert(i, 0)
                expert(i, 1)
            expert(NE // 2 - 1, 0)
            expert(NE // 2 - 1, 1, last=True)
            n_most = pe.value_load(cnt[0:1, 0:1], min_val=0, max_val=SEQ)
            with pe.If(n_most > SLOTS):
                with pe.Fori(1, SEQ // SLOTS) as b:
                    with pe.Fori(0, NE) as e:
                        n = (b - 1) * NE + e
                        pe.wait_ge(*over_wait(l, "v_oh", n))
                        gather_mm(pe, OH[0]).then_inc(over_done(l, "v_gat"), 1)
                        pe.wait_ge(*over_wait(l, "v_xg", n))
                        xt_mm(pe).then_inc(over_done(l, "v_xt"), 1)
                        pe.wait_ge(*over_wait(l, "v_xt_out", n))
                        for half, name in enumerate(("v_g", "v_u")):
                            pe.wait_ge(ms("v_w"), 16 * (3 * n + half + 1))
                            w = WOV.rearrange("p (k n) -> p k n", k=KT)
                            for k in range(KT):
                                mm = pe.matmul(BGU[SLOTS * half:SLOTS * half + SLOTS, :], x_tile(k), w[:, k, :], start=(k == 0), stop=(k == KT - 1))
                            mm.then_inc(over_done(l, name), 1)
                        pe.wait_ge(*over_wait(l, "v_hh", n))
                        alone(pe)
                        ht_mm(pe).then_inc(over_done(l, "v_ht"), 1)
                        pe.wait_ge(*over_wait(l, "v_ht_out", n))
                        pe.wait_ge(ms("v_w"), 16 * (3 * n + 3))
                        down_mm(pe, WOV.rearrange("p (k n) -> p k n", k=4)).then_inc(over_done(l, "v_y"), 1)
                        pe.wait_ge(*over_wait(l, "v_ohg", n))
                        alone(pe)
                        for t in range(NT):
                            mm = pe.transpose(PB[4][:, t * P:(t + 1) * P], OHG[:, t * P:(t + 1) * P], ident)
                        mm.then_inc(over_done(l, "v_ot"), 1)
                        pe.wait_ge(*over_wait(l, "v_y_out", n))
                        alone(pe)
                        for m in range(2 * NT):
                            t, r = m // 2, slice(64 * (m % 2), 64 * (m % 2) + 64)
                            mm = pe.matmul(PB[m][:, :], OT[r, t * P:(t + 1) * P], YS[0][r, :], start=True, stop=True)
                        mm.then_inc(over_done(l, "v_comb"), 1)
                        pe.wait_ge(*over_wait(l, "v_added", n))
                        alone(pe)

        def experts_act(act, l, step):
            ms = lambda n: moe_sem(l, n)
            mw = lambda n, v: moe_wait(l, n, v)

            def store(e, u, b, s):
                for half in range(2):
                    act.dma_start(y_view[bass.ds(e, 1) if not isinstance(e, int) else slice(e, e + 1), b:b + SLOTS, half, :],
                                  YS[u][64 * half:64 * half + 64, :]).then_inc(s, 16)

            def expert(i, u, last=False):
                e = 2 * i + u
                act.wait_ge(*mw("gu", e + 1))
                act.activation(SIL[0:SLOTS, :], BGU[0:SLOTS, :], ACT.Silu).then_inc(ms("sil"), 1)
                if not last:
                    act.wait_ge(*mw("gat", e + 2))
                    act.copy(XG, BX[:, :]).then_inc(ms("xg"), 1)
                act.wait_ge(*mw("ht", e + 1))
                act.copy(HHT, BH[:, 0:4 * SLOTS]).then_inc(ms("ht_out"), 1)
                act.wait_ge(*mw("y_out", e + 1))
                store(e, u, 0, ms(f"stored{u}"))

            act.wait_ge(*mw("gat", 1))
            act.copy(XG, BX[:, :]).then_inc(ms("xg"), 1)
            expert(0, 0)
            expert(0, 1)
            with act.Fori(1, NE // 2 - 1) as i:
                expert(i, 0)
                expert(i, 1)
            expert(NE // 2 - 1, 0)
            expert(NE // 2 - 1, 1, last=True)
            for u in range(2):
                act.wait_ge(*mw(f"stored{u}", 32 * (NE // 2)))
            n_most = act.value_load(cnt[0:1, 0:1], min_val=0, max_val=SEQ)
            with act.If(n_most > SLOTS):
                with act.Fori(1, SEQ // SLOTS) as b:
                    with act.Fori(0, NE) as e:
                        n = (b - 1) * NE + e
                        act.wait_ge(*over_wait(l, "v_gat", n))
                        act.copy(XG, BX[:, :]).then_inc(over_done(l, "v_xg"), 1)
                        act.wait_ge(*over_wait(l, "v_g", n))
                        act.wait_ge(*over_wait(l, "v_u", n))
                        act.activation(SIL[0:SLOTS, :], BGU[0:SLOTS, :], ACT.Silu).then_inc(over_done(l, "v_sil"), 1)
                        act.wait_ge(*over_wait(l, "v_ht", n))
                        act.copy(HHT, BH[:, 0:4 * SLOTS]).then_inc(over_done(l, "v_ht_out"), 1)
            act.copy(SIL[0:1, 0:1], SIL[0:1, 0:1]).then_inc(ms("rows_stored"), 1)

        def experts_dve(dve, l, step):
            ms = lambda n: moe_sem(l, n)
            mw = lambda n, v: moe_wait(l, n, v)

            def one_hots(e, buf):
                col = POSM[:, :, bass.ds(e, 1) if not isinstance(e, int) else slice(e, e + 1)]
                dve.tensor_tensor(OH[buf], const("slot")[:, None, :].to_broadcast([P, NT, SLOTS]), col.to_broadcast([P, NT, SLOTS]),
                                  ALU.is_equal).then_inc(ms("oh"), 1)

            def x_out(e):
                dve.wait_ge(*mw("xt", e + 1))
                dve.tensor_copy(XTt, BXT[:, :]).then_inc(ms("xt_out"), 1)

            def expert(i, u, last=False):
                e = 2 * i + u
                dve.wait_ge(*mw("sil", e + 1))
                dve.tensor_tensor(HH[0:SLOTS, :], SIL[0:SLOTS, :], BGU[SLOTS:2 * SLOTS, :], ALU.mult).then_inc(ms("hh"), 1)
                if not last:
                    x_out(e + 1)
                dve.wait_ge(*mw("y", e + 1))
                if not (isinstance(i, int) and i == 0):
                    dve.wait_ge(*mw(f"stored{u}", 32 * i))
                dve.tensor_copy(YS[u], BY[:, :]).then_inc(ms("y_out"), 1)

            def ahead(e, u):
                dve.wait_ge(*mw("gat", e + 1))
                one_hots(e + 2, u)

            one_hots(0, 0)
            one_hots(1, 1)
            x_out(0)
            ahead(0, 0)
            expert(0, 0)
            ahead(1, 1)
            expert(0, 1)
            with dve.Fori(1, NE // 2 - 1) as i:
                for u in range(2):
                    ahead(2 * i + u, u)
                    expert(i, u)
            expert(NE // 2 - 1, 0)
            expert(NE // 2 - 1, 1, last=True)
            n_most = dve.value_load(cnt[0:1, 0:1], min_val=0, max_val=SEQ)
            with dve.If(n_most > SLOTS):
                for u in range(2):
                    dve.wait_ge(*mw(f"stored{u}", 32 * (NE // 2)))
                for M, gate in ((M1, gate1), (M2, gate2)):
                    dve.tensor_tensor(M, M, gate[:, :, None].to_broadcast([P, NT, NE]), ALU.mult).then_inc(ms("v_gates"), 1)
                dve.wait_ge(ms("v_gates"), 2)
                dve.tensor_tensor(M1, M1, M2, ALU.add).then_inc(ms("v_gates"), 1)
                dve.wait_ge(ms("v_gates"), 3)
                with dve.Fori(1, SEQ // SLOTS) as b:
                    dve.tensor_scalar(POSM, POSM, -float(SLOTS), None, ALU.add).then_inc(ms("v_pos"), 1)
                    dve.wait_ge(ms("v_pos"), b)
                    alone(dve)
                    with dve.Fori(0, NE) as e:
                        n = (b - 1) * NE + e
                        dve.tensor_tensor(OH[0], const("slot")[:, None, :].to_broadcast([P, NT, SLOTS]),
                                          POSM[:, :, bass.ds(e, 1)].to_broadcast([P, NT, SLOTS]), ALU.is_equal).then_inc(over_done(l, "v_oh"), 1)
                        dve.wait_ge(*over_wait(l, "v_oh", n))
                        dve.tensor_tensor(OHG.rearrange("p (t a s) -> p t a s", t=NT, a=2), OH[0][:, :, None, :].to_broadcast([P, NT, 2, SLOTS]),
                                          M1[:, :, bass.ds(e, 1), None].to_broadcast([P, NT, 2, SLOTS]), ALU.mult).then_inc(over_done(l, "v_ohg"), 1)
                        dve.wait_ge(*over_wait(l, "v_xt", n))
                        dve.tensor_copy(XTt, BXT[:, :]).then_inc(over_done(l, "v_xt_out"), 1)
                        dve.wait_ge(*over_wait(l, "v_sil", n))
                        dve.tensor_tensor(HH[0:SLOTS, :], SIL[0:SLOTS, :], BGU[SLOTS:2 * SLOTS, :], ALU.mult).then_inc(over_done(l, "v_hh"), 1)
                        dve.wait_ge(*over_wait(l, "v_ot", n))
                        dve.tensor_copy(OT, PB[4][:, :])
                        dve.wait_ge(*over_wait(l, "v_y", n))
                        dve.tensor_copy(YS[0], BY[:, :]).then_inc(over_done(l, "v_y_out"), 1)
                        dve.wait_ge(*over_wait(l, "v_comb", n))
                        for m in range(2 * NT):
                            xs = X[:, m // 2, (m % 2) * 512:(m % 2) * 512 + 512]
                            dve.tensor_tensor(xs, xs, PB[m][:, :], ALU.add).then_inc(ms("v_add") if m < 2 * NT - 1 else over_done(l, "v_added"), 1)
                        dve.wait_ge(*over_wait(l, "v_added", n))
                        alone(dve)
            base = (R_EVEN, R_ODD)[l]
            for n in range(2 * NT):
                t, k = n // 2, n % 2
                dve.wait_ge(sg(f"fetched{n % 4}"), 16 * (2 * l + n // 4 + 1))
                if k:
                    dve.wait_ge(*mw("first_added", t + 1))
                ins = dve.scalar_tensor_tensor(X[:, t, :], XN[:, n % 4, :], (used1, used2)[k][:, t:t + 1], X[:, t, :], ALU.mult, ALU.add)
                ins.then_inc(resid if k else ms("first_added"), 1)

        def experts_sp(sp, l):
            ms = lambda n: moe_sem(l, n)
            mw = lambda n, v: moe_wait(l, n, v)
            mats = (w_gate[l], w_up[l], w_down[l])

            def load(i, u, j):
                e = 2 * i + u
                c = c_moe[l] + 3 * u + j
                if isinstance(i, int) and i == 0:
                    sp.wait_ge(*released[c - RING])
                else:
                    sp.wait_ge(*mw("gu" if j < 2 else "y", e - 1))
                src = mats[j].rearrange("e (p k) n -> p e (k n)", p=P)[:, bass.ds(e, 1) if not isinstance(e, int) else slice(e, e + 1), :]
                sp.dma_start(slot_of(c), src.rearrange("p e n -> p (e n)"), max_dma_last_dim=4096).then_inc(w_landed[c % RING], 16)

            for u in range(2):
                for j in range(3):
                    load(0, u, j)
            with sp.Fori(1, NE // 2) as i:
                for u in range(2):
                    for j in range(3):
                        load(i, u, j)

        def overflow_sp(sp, l):
            ms = lambda n: moe_sem(l, n)
            mw = lambda n, v: moe_wait(l, n, v)
            sp.wait_ge(*mw("routed", 1))
            n_most = sp.value_load(cnt[0:1, 0:1], min_val=0, max_val=SEQ)
            with sp.If(n_most > SLOTS):
                with sp.Fori(1, SEQ // SLOTS) as b:
                    with sp.Fori(0, NE) as e:
                        n = (b - 1) * NE + e
                        for j, name in enumerate(("v_g", "v_u", "v_y")):
                            src = (w_gate[l], w_up[l], w_down[l])[j].rearrange("e (p k) n -> p e (k n)", p=P)[:, bass.ds(e, 1), :]
                            sp.dma_start(WOV, src.rearrange("p e n -> p (e n)"), max_dma_last_dim=4096).then_inc(ms("v_w"), 16)
                            sp.wait_ge(*over_wait(l, name, n))
                        alone(sp)

        def combine_pool(pool, l):
            ms = lambda n: moe_sem(l, n)
            mw = lambda n, v: moe_wait(l, n, v)
            base = (R_EVEN, R_ODD)[l]
            pool.wait_ge(*mw("rows_stored", 1))
            for n in range(2 * NT):
                t, k = n // 2, n % 2
                if n >= 4:
                    pool.wait_ge(*((resid, base + t - 1) if k else mw("first_added", t - 1)))
                pool.indirect_dma_start(XN[:, n % 4, :], None, y_rows, bass.IndirectOffsetOnAxis(ap=dest[:, k * NT + t:k * NT + t + 1], axis=0))\
                    .then_inc(sg(f"fetched{n % 4}"), 16)

        def const_odd_(name):
            a, b = co[name]
            return SCR[:, CO_AT + a:CO_AT + b]

        s_.n = 0
        two = lambda a: a.rearrange("p (m n) -> p m n", m=2)
        QR, KR, QX, Sr = (two(s_(1024)) for _ in range(4))
        ATr = t4(s_(512))
        KZ = s_(3 * 256).rearrange("p (t m n) -> p t m n", t=3, m=2)
        rtmp = [s_(512) for _ in range(4)]
        YTr = s_(2048).rearrange("p (j n) -> p j n", j=4)
        r_ss, r_rs = s_(NT), s_(NT)
        rjunk = s_(512)
        VO = XN[:, 0:2, :].rearrange("p a (b n) -> p (a b) n", b=2)
        ZS = XN[:, 2:4, :].rearrange("p a (b n) -> p (a b) n", b=2)

        def ret_pe(pe):
            for h in range(RH):
                c = c_ret + 4 * h
                pe.wait_ge(w_landed[c % RING], landed(c))
                w = slot_of(c).rearrange("p (k s n) -> p k s n", k=KT, s=2)
                if h:
                    pe.wait_ge(resid, R_MOE0 + 8 * h)
                for s in range(2):
                    for par in range(2):
                        for k in range(KT):
                            mm = pe.matmul(PB[2 * s + par][:, :], w[:, k, s, par:RQ:2], HT[:, k, :], start=(k == 0), stop=(k == KT - 1))
                    mm.then_inc(sg("r_qk"), 1)
                c += 1
                pe.wait_ge(w_landed[c % RING], landed(c))
                w = slot_of(c).rearrange("p (k n) -> p k n", k=KT)
                for t in range(NT):
                    if t >= 2:
                        pe.wait_ge(sg("r_v_out"), NT * h + t - 1)
                    for k in range(KT):
                        mm = pe.matmul(PB[4 + t % 2][:, :], HT[:, k, t * P:(t + 1) * P], w[:, k, :], start=(k == 0), stop=(k == KT - 1))
                    mm.then_inc(sg("r_v"), 1)
                pe.wait_ge(sg("r_rot"), 2 * h + 2)
                for t in range(NT):
                    for m in range(2):
                        mm = pe.matmul(PB[0][:, t * P:(t + 1) * P], KR[:, m, t * P:(t + 1) * P], QR[:, m, t * P:(t + 1) * P], start=(m == 0), stop=(m == 1))
                mm.then_inc(sg("r_in"), 1)
                for t in range(NT - 1):
                    for m in range(2):
                        mm = pe.transpose(PB[6 + t // 2][:, (2 * (t % 2) + m) * P:(2 * (t % 2) + m + 1) * P], KR[:, m, t * P:(t + 1) * P], ident)
                mm.then_inc(sg("r_kt"), 1)
                c += 1
                pe.wait_ge(w_landed[c % RING], landed(c))
                w = slot_of(c).rearrange("p (k n) -> p k n", k=KT)
                for t in range(NT):
                    if t < 2:
                        pe.wait_ge(sg("r_v_out"), NT * h + t + 3)
                    else:
                        pe.wait_ge(sg("r_zs"), NT * h + t - 1)
                    for k in range(KT):
                        mm = pe.matmul(PB[4 + t % 2][:, :], HT[:, k, t * P:(t + 1) * P], w[:, k, :], start=(k == 0), stop=(k == KT - 1))
                    mm.then_inc(sg("r_z"), 1)
                pe.wait_ge(sg("r_at"), h + 1)
                pe.wait_ge(sg("r_kz"), h + 1)
                for t in range(NT):
                    b = PB[1 + t % 2]
                    if t >= 2:
                        pe.wait_ge(sg("r_o_out"), NT * h + t - 1)
                    mm = pe.matmul(b[:, :], ATr[:, t, :], VO[:, t, :], start=True, stop=(t == 0))
                    if t:
                        pe.wait_ge(sg("r_S"), 6 * h + 2 * t)
                        for m in range(2):
                            mm = pe.matmul(b[:, :], QX[:, m, t * P:(t + 1) * P], Sr[:, m, :], start=False, stop=(m == 1))
                    mm.then_inc(sg("r_o"), 1)
                    if t < NT - 1:
                        for m in range(2):
                            pe.matmul(PB[(3, 7)[m]][:, :], KZ[:, t, m, :], VO[:, t, :], start=True, stop=True).then_inc(sg("r_su"), 1)
                pe.wait_ge(sg("r_y"), NT * (h + 1))
                for t in range(NT):
                    if t >= 2:
                        pe.wait_ge(sg("r_yt"), NT * h + t - 1)
                    for j in range(4):
                        mm = pe.transpose(PB[(0, 6)[t % 2]][:, j * P:(j + 1) * P], VO[:, t, j:512:4], ident)
                    mm.then_inc(sg("r_tr"), 1)
                c += 1
                pe.wait_ge(w_landed[c % RING], landed(c))
                w = slot_of(c).rearrange("p (k n) -> p k n", k=4)
                pe.wait_ge(sg("r_zs"), NT * (h + 1))
                for n in range(8):
                    t, half = n // 2, n % 2
                    pe.wait_ge(sg("r_yt"), NT * h + t + 1)
                    if n >= 4:
                        pe.wait_ge(resid, R_MOE0 + 8 * h + n - 3)
                    for j in range(4):
                        mm = pe.matmul(PB[(1, 2, 4, 5)[n % 4]][:, :], YTr[:, j, t * P:(t + 1) * P], w[:, j, half * 512:(half + 1) * 512], start=(j == 0), stop=(j == 3))
                    mm.then_inc(sg("r_out"), 1)

        def ret_act(act, step):
            act.wait_ge(odd_in, 16)
            for h in range(RH):
                for t in range(NT):
                    act.wait_ge(sg("r_v"), NT * h + t + 1)
                    act.copy(VO[:, t, :], PB[4 + t % 2][:, :]).then_inc(sg("r_v_out"), 1)
                act.wait_ge(sg("r_kt"), h + 1)
                for t in range(NT - 1):
                    ins = act.activation(KZ[:, t, :, :], PB[6 + t // 2][:, (t % 2) * 256:(t % 2) * 256 + 256].rearrange("p (m n) -> p m n", m=2), ACT.Copy,
                                         scale=const_odd_("zeta")[:, h:h + 1])
                    if t == NT - 2:
                        ins.then_inc(sg("r_kz"), 1)
                for t in range(NT):
                    act.wait_ge(sg("r_z"), NT * h + t + 1)
                    act.activation(ZS[:, t, :], PB[4 + t % 2][:, :], ACT.Silu).then_inc(sg("r_zs"), 1)
                for t in range(NT):
                    act.wait_ge(sg("r_o"), NT * h + t + 1)
                    step.then(act.activation(rjunk, PB[1 + t % 2][:, :], ACT.Square, accum_out=r_ss[:, t:t + 1]))
                    if t < NT - 1:
                        act.wait_ge(sg("r_su"), 6 * h + 2 * t + 2)
                    act.copy(VO[:, t, :], PB[1 + t % 2][:, :]).then_inc(sg("r_o_out"), 1)
                for t in range(NT):
                    act.wait_ge(sg("r_tr"), NT * h + t + 1)
                    act.copy(YTr[:, :, t * P:(t + 1) * P], PB[(0, 6)[t % 2]][:, :].rearrange("p (j q) -> p j q", j=4)).then_inc(sg("r_yt"), 1)

        def ret_pool(pool, step):
            for h in range(RH):
                pool.wait_ge(sg("r_o_out"), NT * (h + 1))
                step.then(pool.tensor_scalar(r_rs, r_ss, 1.0 / RV, EPS, ALU.mult, ALU.add))
                pool.tensor_tensor(r_rs, r_rs, mhalf[:, 0:NT], ALU.pow).then_inc(sg("r_rstd"), 1)

        def ret_dve(dve, step):
            dve.wait_ge(odd_in, 16)
            cs, sn = const_odd_("xcos"), const_odd_("xsin")
            for h in range(RH):
                for s, R in enumerate((QR, KR)):
                    dve.wait_ge(sg("r_qk"), 2 * h + s + 1)
                    e_, o_ = PB[2 * s][:, :], PB[2 * s + 1][:, :]
                    step(dve.tensor_tensor(rtmp[0], e_, cs, ALU.mult))
                    step(dve.tensor_tensor(rtmp[1], o_, sn, ALU.mult))
                    step(dve.tensor_tensor(rtmp[2], o_, cs, ALU.mult))
                    step(dve.tensor_tensor(rtmp[3], e_, sn, ALU.mult))
                    step.wait()
                    step(dve.tensor_tensor(R[:, 0, :], rtmp[0], rtmp[1], ALU.subtract))
                    dve.tensor_tensor(R[:, 1, :], rtmp[2], rtmp[3], ALU.add).then_inc(sg("r_rot"), 1)
                    step.wait()
                    dve.wait_ge(sg("r_rot"), 2 * h + s + 1)
                for m in range(2):
                    step(dve.tensor_tensor(t4(QX[:, m, :]), t4(QR[:, m, :]), const_odd_(f"xi{h}")[:, None, :].to_broadcast([P, NT, P]), ALU.mult))
                dve.wait_ge(sg("r_in"), h + 1)
                step.wait()
                dve.tensor_tensor(ATr, t4(PB[0][:, :]), const_odd_(f"decay{h}")[:, None, :].to_broadcast([P, NT, P]), ALU.mult).then_inc(sg("r_at"), 1)
                for t in range(NT - 1):
                    for m in range(2):
                        dve.wait_ge(sg("r_su"), 6 * h + 2 * t + m + 1)
                        b = PB[(3, 7)[m]][:, :]
                        if t:
                            dve.wait_ge(sg("r_S"), 6 * h + 2 * (t - 1) + m + 1)
                            dve.wait_ge(sg("r_o"), NT * h + t + 1)
                            ins = dve.scalar_tensor_tensor(Sr[:, m, :], Sr[:, m, :], gamma[h], b, ALU.mult, ALU.add)
                        else:
                            ins = dve.tensor_copy(Sr[:, m, :], b)
                        ins.then_inc(sg("r_S"), 1)
                dve.wait_ge(sg("r_rstd"), h + 1)
                dve.wait_ge(sg("r_zs"), NT * (h + 1))
                for t in range(NT):
                    dve.scalar_tensor_tensor(VO[:, t, :], VO[:, t, :], r_rs[:, t:t + 1], ZS[:, t, :], ALU.mult, ALU.mult).then_inc(sg("r_y"), 1)
                for n in range(8):
                    t, half = n // 2, n % 2
                    dve.wait_ge(sg("r_out"), 8 * h + n + 1)
                    xs = X[:, t, half * 512:(half + 1) * 512]
                    dve.wait_ge(resid, R_MOE0 + 8 * h)
                    dve.tensor_tensor(xs, xs, PB[(1, 2, 4, 5)[n % 4]][:, :], ALU.add).then_inc(resid, 1)

        released = {c_kv: (sg("a_proj"), 4), c_q: (sg("a_proj"), 8)}
        for h in range(GH):
            released[c_gdn + h] = (sg("d_z"), h + 1)
        for g in range(2):
            released[c_oute + g] = (sg("m_out"), 8)
        for l in range(2):
            for e in range(NE):
                released[c_moe[l] + 3 * e] = released[c_moe[l] + 3 * e + 1] = moe_wait(l, "gu", e + 1)
                released[c_moe[l] + 3 * e + 2] = moe_wait(l, "y", e + 1)
        for h in range(RH):
            for j, s in enumerate((("r_qk", 2 * h + 2), ("r_v", NT * (h + 1)), ("r_z", NT * (h + 1)), ("r_out", 8 * (h + 1)))):
                released[c_ret + 4 * h + j] = (sg(s[0]), s[1])

        stored = sem("stored")
        R_END = (0, R_EVEN, R_MOE0, R_ODD, R_MOE1)[upto]
        block = ctx.enter_context(nc.Block())

        @block.sync
        def _(sp):
            sp.dma_start(X[:, :, :], x[0].rearrange("(t p) d -> p t d", p=P)).then_inc(x_in, 16)
            sp.dma_start(CE[:, :], const_even).then_inc(consts_in, 16)

            def load(c):
                if c >= RING:
                    sp.wait_ge(*released[c - RING])
                for dst, src in chunks[c]:
                    sp.dma_start(dst(slot_of(c)), src).then_inc(w_landed[c % RING], 16)

            for c in range(c_moe[0]):
                load(c)
            if upto > 1:
                experts_sp(sp, 0)
                overflow_sp(sp, 0)
            if upto > 2:
                for c in range(c_ret, c_moe[1]):
                    load(c)
            if upto > 3:
                experts_sp(sp, 1)
                overflow_sp(sp, 1)
            for t in range(NT):
                sp.wait_ge(resid, R_END)
                sp.dma_start(out[0].rearrange("(t p) d -> p t d", p=P)[:, t, :], X[:, t, :]).then_inc(stored, 16)
            sp.wait_ge(stored, 16 * NT)

        @block.gpsimd
        def _(pool):
            step = Steps(pool, pool_step)
            pool.memset(mhalf[:, :], -0.5).then_inc(mhalf_set, 1)
            gain_pool(pool, 0)
            for dst, src in ((qk_gain[:, 0:512].rearrange("p (h d) -> p h d", h=AH), q_gain_even[0:1, None, :].to_broadcast([P, AH, ADH])),
                             (qk_gain[:, 512:640].rearrange("p (h d) -> p h d", h=AKV), k_gain_even[0:1, None, :].to_broadcast([P, AKV, ADH])),
                             (sink_b, sinks_even[0:1, :].to_broadcast([P, AH])),
                             (alog_b, a_log_even[0:1, :].to_broadcast([P, GH])),
                             (dtb_b, dt_bias_even[0:1, :].to_broadcast([P, GH])),
                             (gdn_gain, gdn_gain_even[0:1, :].to_broadcast([P, GD]))):
                pool.dma_start(dst, src).then_inc(params_in, 16)
            pool.dma_start(cwr[0:48, :], conv_w_even[0].rearrange("i (c n) -> (i c) n", n=P)).then_inc(params_in, 16)
            pool.wait_ge(mhalf_set, 1)
            if upto > 1:
                route_pool(pool, 0)
            norm_pool(pool, 0, step)
            attn_pool(pool, step)
            gdn_pool(pool, step)
            if upto > 1:
                gain_pool(pool, 1)
                norm_pool(pool, 1, step)
                pool.wait_ge(resid, R_EVEN)
                pool.dma_start(SCR[:, CO_AT:SCR_N], const_odd).then_inc(odd_in, 16)
                combine_pool(pool, 0)
            if upto > 2:
                gain_pool(pool, 2)
                if upto > 3:
                    route_pool(pool, 1)
                norm_pool(pool, 2, step)
                ret_pool(pool, step)
            if upto > 3:
                gain_pool(pool, 3)
                norm_pool(pool, 3, step)
                combine_pool(pool, 1)

        @block.scalar
        def _(act):
            step = Steps(act, act_step)
            norm_act(act, 0)
            norm_act_out(act, 0)
            attn_act(act, step)
            gdn_act(act, step)
            oute_act(act)
            for l in range(2):
                if upto > 2 * l + 1:
                    norm_act(act, 2 * l + 1)
                    norm_act_out(act, 2 * l + 1)
                    route_act(act, l)
                    experts_act(act, l, step)
                if l == 0 and upto > 2:
                    norm_act(act, 2)
                    norm_act_out(act, 2)
                    ret_act(act, step)

        @block.vector
        def _(dve):
            step = Steps(dve, dve_step)
            norm_dve(dve, 0)
            norm_dve_out(dve, 0)
            attn_dve(dve, step)
            gdn_dve(dve, step)
            oute_dve(dve)
            for l in range(2):
                if upto > 2 * l + 1:
                    norm_dve(dve, 2 * l + 1)
                    norm_dve_out(dve, 2 * l + 1)
                    route_dve(dve, l, step)
                    experts_dve(dve, l, step)
                if l == 0 and upto > 2:
                    norm_dve(dve, 2)
                    norm_dve_out(dve, 2)
                    ret_dve(dve, step)

        @block.tensor
        def _(pe):
            norm_pe(pe, 0)
            attn_pe(pe)
            gdn_pe(pe)
            oute_pe(pe)
            for l in range(2):
                if upto > 2 * l + 1:
                    norm_pe(pe, 2 * l + 1)
                    route_pe(pe, l)
                    experts_pe(pe, l)
                if l == 0 and upto > 2:
                    norm_pe(pe, 2)
                    ret_pe(pe)


_INS = ['x', 'ln_mix_even', 'w_in_even', 'conv_w_even', 'a_log_even', 'dt_bias_even', 'q_gain_even', 'k_gain_even',
        'sinks_even', 'gdn_gain_even', 'w_out_even', 'ln_mix_odd', 'w_in_odd', 'w_out_odd', 'ln_ffn',
        'w_router_group', 'b_router_group', 'w_router_expert', 'b_router_expert', 'w_gate', 'w_up', 'w_down']


def packed(tables):
    return np.ascontiguousarray(np.concatenate([np.asarray(a, np.float32) for a in tables.values()], axis=1))


def kernel(**inputs):
    import concourse.bacc as bacc
    from concourse.bass_utils import run_bass_kernel_spmd

    nc = bacc.Bacc("TRN2", target_bir_lowering=False, num_devices=1)
    arrays, args = {}, []
    tab_even, tab_odd, _ = constants()
    for name, a in [(n, inputs[n]) for n in _INS] + [("const_even", packed(tab_even)), ("const_odd", packed(tab_odd))]:
        a = np.ascontiguousarray(a)
        arrays[f"in_{name}_dram"] = a
        args.append(nc.dram_tensor(f"in_{name}_dram", a.shape, mybir.dt.from_np(a.dtype), kind="ExternalInput").ap())
    args.append(nc.dram_tensor("out_0_dram", (1, SEQ, D), F32, kind="ExternalOutput").ap())
    program(nc, *args)
    r = run_bass_kernel_spmd(nc, [arrays], core_ids=[0])
    return r.results[0]["out_0_dram"]
```

```python
from contextlib import ExitStack

import numpy as np
import concourse.bass as bass
from concourse import mybir

F32 = mybir.dt.float32
I32 = mybir.dt.int32
ALU = mybir.AluOpType
ACT = mybir.ActivationFunctionType
AX = mybir.AxisListType.X

P = 128
D = 1024
SEQ = 512
NT = SEQ // P
KT = D // P
EPS = 1e-6
BIG = 1e30
RING = 6
SLOT = 4096
AH, AKV, ADH = 8, 2, 64
AQK = AH + AKV
GH, GD, CONV, CH = 4, 128, 4, 64
LEVELS = 6
RH, RQ, RV = 4, 256, 512
NG, EPG, NE, DE = 4, 8, 32, 512
SLOTS = 64
NR = NG + NE


def constants():
    i = np.arange(P)
    same = (i[:, None] // CH) == (i[None, :] // CH)
    even = {
        "ident": np.eye(P),
        "ones": np.ones((P, P)),
        "before": i[:, None] < i[None, :],
        "cum": same & (i[:, None] <= i[None, :]),
        "chunk": same,
        "strict": same & (i[:, None] > i[None, :]),
        "inclT": same & (i[:, None] <= i[None, :]),
    }
    for lv in range(LEVELS):
        b = 1 << lv
        even[f"level{lv}"] = ((i[:, None] // (2 * b)) == (i[None, :] // (2 * b))) & \
            ((i[:, None] // b) % 2 == 1) & ((i[None, :] // b) % 2 == 0)
    q, k = i[:, None], np.arange(2 * P)[None, :] - P
    even["window"] = np.where((q - k >= 0) & (q - k < P), 0.0, -BIG)
    half = ADH // 8
    inv = (np.float32(1.0) / np.float32(500000.0) ** (np.arange(half, dtype=np.float32) * np.float32(2.0) / np.float32(16))).astype(np.float32)
    ang = (np.arange(SEQ, dtype=np.float32)[:, None] * inv[None, :]).astype(np.float32)
    ang = ang.reshape(NT, P, half).transpose(1, 0, 2).reshape(P, NT * half).astype(np.float64)
    even["rcos"], even["rsin"] = np.cos(ang), np.sin(ang)
    even["slot"] = np.broadcast_to(np.arange(SLOTS), (P, SLOTS))
    even["rowbase"] = np.broadcast_to(np.arange(NE) * SLOTS, (P, NE))
    even["first"] = np.broadcast_to(16 - np.arange(EPG), (P, EPG))
    odd = {}
    freq = (np.float32(1.0) / np.float32(10000.0) ** np.linspace(0.0, 1.0, RQ // 2, dtype=np.float32)).astype(np.float32)
    ang = (np.arange(SEQ, dtype=np.float32)[None, :] * freq[:, None]).astype(np.float32).astype(np.float64)
    odd["xcos"], odd["xsin"] = np.cos(ang), np.sin(ang)
    lg = np.log(1.0 - 2.0 ** (-5.0 - np.arange(RH)))
    kscale = RQ ** -0.5
    for h in range(RH):
        rel = i[None, :] - i[:, None]
        odd[f"decay{h}"] = np.where(rel >= 0, np.exp(np.maximum(rel, 0) * lg[h]), 0.0) * kscale
        odd[f"xi{h}"] = np.broadcast_to(np.exp((i + 1) * lg[h]), (P, P))
    odd["zeta"] = np.exp((P - 1 - i)[:, None] * lg[None, :]) * kscale
    return even, odd, [float(np.exp(P * x)) for x in lg]


def columns(tables):
    at, n = {}, 0
    for name, a in tables.items():
        at[name] = (n, n + a.shape[1])
        n += a.shape[1]
    return at, n


def program(nc, x, ln_mix_even, w_in_even, conv_w_even, a_log_even, dt_bias_even, q_gain_even, k_gain_even,
            sinks_even, gdn_gain_even, w_out_even, ln_mix_odd, w_in_odd, w_out_odd, ln_ffn,
            w_router_group, b_router_group, w_router_expert, b_router_expert, w_gate, w_up, w_down,
            const_even, const_odd, out, upto=4):
    tab_even, tab_odd, gamma = constants()
    ce, n_even = columns(tab_even)
    co, n_odd = columns(tab_odd)
    y_rows = nc.dram_tensor("y_rows", (NE * SLOTS, D), F32, kind="Internal").ap()
    gains = [ln_mix_even[0:1, :], ln_ffn[0:1, :], ln_mix_odd[0:1, :], ln_ffn[1:2, :]]
    ctx = ExitStack()
    with ctx:
        def sb(name, shape, dt=F32):
            return ctx.enter_context(nc.sbuf_tensor(name, shape, dt))

        def sem(name):
            return ctx.enter_context(nc.semaphore(name))

        ring = sb("ring", [P, RING, SLOT])
        X = sb("X", [P, NT, D])
        XN = sb("XN", [P, NT, D])
        HT = sb("HT", [P, KT, SEQ])
        CE = sb("CE", [P, n_even])
        gainB = sb("gainB", [P, D])
        sumsq = sb("sumsq", [P, NT])
        rstd = sb("rstd", [P, NT])
        mhalf = sb("mhalf", [P, 64])
        WR = sb("WR", [P, KT, NR])
        br = sb("br", [P, NR])
        SCR_N = 12600
        CO_AT = SCR_N - n_odd
        SCR = sb("SCR", [P, SCR_N])
        PARAMS = 16 * 7
        PB = [ctx.enter_context(nc.psum_tensor(f"bank{i}", [P, 512], F32)) for i in range(8)]

        def const(name):
            a, b = ce[name]
            return CE[:, a:b]

        ident, ones = const("ident"), const("ones")

        class Carve:
            def __init__(self, tensor, size):
                self.t, self.n, self.size = tensor, 0, size

            def __call__(self, n):
                a = self.n
                self.n += n
                assert self.n <= self.size, (self.n, self.size)
                return self.t[:, a:a + n]

        chunks = []

        def slot_of(c):
            return ring[:, c % RING, :]

        def k_rows(w, a, b):
            return w[:, a:b].rearrange("(p k) n -> p k n", p=P)

        w_e = w_in_even[0]
        c_kv = len(chunks)
        chunks.append([(lambda s: s[:, 0:KT * 264].rearrange("p (k n) -> p k n", k=KT)[:, :, 0:256], k_rows(w_e, 512, 768)),
                       (lambda s: s[:, 0:KT * 264].rearrange("p (k n) -> p k n", k=KT)[:, :, 256:264], k_rows(w_e, 2816, 2824))])
        c_q = len(chunks)
        chunks.append([(lambda s: s.rearrange("p (k n) -> p k n", k=KT), k_rows(w_e, 0, 512))])
        c_gdn = len(chunks)
        for h in range(GH):
            src = w_e[:, 768:2816].rearrange("(p k) (s n) -> p k s n", p=P, s=4)[:, :, :, h * GD:(h + 1) * GD]
            chunks.append([(lambda s, i=i: s.rearrange("p (k s n) -> p k s n", k=KT, s=4)[:, :, i, :], src[:, :, i, :]) for i in range(4)])
        c_oute = len(chunks)
        for g in range(2):
            chunks.append([(lambda s: s.rearrange("p (k n) -> p k n", k=4),
                            w_out_even[0, g * 512:(g + 1) * 512, :].rearrange("(p k) n -> p k n", p=P))])
        c_moe = [len(chunks)]
        for e in range(NE):
            chunks += [[None]] * 3
        c_ret = len(chunks)
        w_o = w_in_odd[0]
        for h in range(RH):
            src = w_o[:, 0:2048].rearrange("(p k) (s n) -> p k s n", p=P, s=2)[:, :, :, h * RQ:(h + 1) * RQ]
            chunks.append([(lambda s, i=i: s.rearrange("p (k s n) -> p k s n", k=KT, s=2)[:, :, i, :], src[:, :, i, :]) for i in range(2)])
            for base in (2048, 4096):
                chunks.append([(lambda s: s.rearrange("p (k n) -> p k n", k=KT), k_rows(w_o, base + h * RV, base + (h + 1) * RV))])
            chunks.append([(lambda s: s.rearrange("p (k n) -> p k n", k=4),
                            w_out_odd[0, h * RV:(h + 1) * RV, :].rearrange("(p k) n -> p k n", p=P))])
        c_moe.append(len(chunks))
        for e in range(NE):
            chunks += [[None]] * 3

        def landed(c):
            return 16 * sum(len(chunks[d]) for d in range(c % RING, c + 1, RING))

        w_landed = [sem(f"w_landed{s}") for s in range(RING)]

        x_in, consts_in, params_in, odd_in, gain_in, router_in = (sem(s) for s in (
            "x_in", "consts_in", "params_in", "odd_in", "gain_in", "router_in"))
        mhalf_set = sem("mhalf_set")
        turns = sem("turns")
        resid = sem("resid")
        ss_done, rstd_done, xn_done, tr_done, tr_out_a, tr_out_d = (sem(s) for s in (
            "ss_done", "rstd_done", "xn_done", "tr_done", "tr_out_a", "tr_out_d"))
        act_step, dve_step, pool_step = sem("act_step"), sem("dve_step"), sem("pool_step")
        S = {}

        def sg(name):
            if name not in S:
                S[name] = sem(name)
            return S[name]

        class Steps:
            def __init__(self, eng, s):
                self.eng, self.sem, self.n = eng, s, 0

            def __call__(self, ins):
                ins.then_inc(self.sem, 1)
                self.n += 1

            def wait(self):
                self.eng.wait_ge(self.sem, self.n)

            def then(self, ins):
                self(ins)
                self.wait()

        def alone(eng):
            eng.sem_inc(turns, 1)

        R_EVEN, R_MOE0, R_ODD, R_MOE1 = 8, 12, 12 + 32, 12 + 32 + 4

        def x_wait(eng, ph, t):
            if ph == 0:
                eng.wait_ge(x_in, 16)
            else:
                eng.wait_ge(resid, [0, 2 * (t + 1), R_EVEN + t + 1, R_ODD - 8 + 2 * (t + 1)][ph])

        def norm_act(act, ph):
            if ph == 1:
                act.wait_ge(sg("m_tr"), 8)
            if ph == 3:
                act.wait_ge(sg("r_tr"), NT * RH)
            for t in range(NT):
                x_wait(act, ph, t)
                act.activation(XN[:, t, :], X[:, t, :], ACT.Square, accum_out=sumsq[:, t:t + 1]).then_inc(ss_done, 1)

        def norm_act_out(act, ph):
            for n in range(0, 8, 2):
                t, kk = n // 2, n % 2
                act.wait_ge(tr_done, 8 * ph + n + 1)
                act.copy(HT[:, 4 * kk:4 * kk + 4, t * P:(t + 1) * P], PB[n % 4][:, :].rearrange("p (k q) -> p k q", k=4)).then_inc(tr_out_a, 1)

        def norm_pool(pool, ph, step, tiles=range(NT)):
            for t in tiles:
                if ph and t == 0:
                    pool.wait_ge(xn_done, NT * ph)
                pool.wait_ge(ss_done, NT * ph + t + 1)
                step.then(pool.tensor_scalar(rstd[:, t:t + 1], sumsq[:, t:t + 1], 1.0 / D, EPS, ALU.mult, ALU.add))
                pool.tensor_tensor(rstd[:, t:t + 1], rstd[:, t:t + 1], mhalf[:, 0:1], ALU.pow).then_inc(rstd_done, 1)

        def gain_pool(pool, ph):
            if ph:
                pool.wait_ge(xn_done, NT * ph)
            pool.dma_start(gainB[:, :], gains[ph].to_broadcast([P, D])).then_inc(gain_in, 16)

        def norm_dve(dve, ph, t):
            if t < 0 or ph >= upto:
                return
            dve.wait_ge(rstd_done, NT * ph + t + 1)
            dve.wait_ge(gain_in, 16 * (ph + 1))
            x_wait(dve, ph, t)
            dve.scalar_tensor_tensor(XN[:, t, :].rearrange("p (a c) -> p c a", a=2), X[:, t, :].rearrange("p (c a) -> p c a", a=2),
                                     rstd[:, t:t + 1], gainB[:, :].rearrange("p (c a) -> p c a", a=2),
                                     ALU.mult, ALU.mult).then_inc(xn_done, 1)

        def norm_dve_out(dve, ph):
            for n in range(1, 8, 2):
                t, kk = n // 2, n % 2
                dve.wait_ge(tr_done, 8 * ph + n + 1)
                dve.tensor_copy(HT[:, 4 * kk:4 * kk + 4, t * P:(t + 1) * P], PB[n % 4][:, :].rearrange("p (k q) -> p k q", k=4)).then_inc(tr_out_d, 1)

        def norm_pe(pe, ph, between=None):
            if ph == 0:
                pe.wait_ge(consts_in, 16)
            for n in range(8):
                t, kk = n // 2, n % 2
                pe.wait_ge(xn_done, NT * ph + t + 1)
                if n >= 4:
                    pe.wait_ge((tr_out_a, tr_out_d)[n % 2], 4 * ph + (n - 4) // 2 + 1)
                for j in range(4):
                    k = 4 * kk + j
                    mm = pe.transpose(PB[n % 4][:, j * P:(j + 1) * P], XN[:, t, (k % 2) * 512 + k // 2:(k % 2 + 1) * 512:4], ident)
                mm.then_inc(tr_done, 1)
                if between and kk and t:
                    between(t - 1)
            pe.wait_ge(tr_out_a, 4 * (ph + 1))
            pe.wait_ge(tr_out_d, 4 * (ph + 1))
            if between:
                between(NT - 1)

        s_ = Carve(SCR, SCR_N)
        prm = s_(640 + 8 + 4 + 4 + 128)
        cwr, cw = s_(128), s_(48)
        qk_gain, sink_b, alog_b, dtb_b, gdn_gain = prm[:, 0:640], prm[:, 640:648], prm[:, 648:652], prm[:, 652:656], prm[:, 656:784]
        smalls = s_(400)
        sm_n = [0]

        def small(n):
            a = sm_n[0]
            sm_n[0] += n
            assert sm_n[0] <= 400
            return smalls[:, a:a + n]

        g_raw, g_abs, g_e, g_sp, g_val, beta, ea = (small(16) for _ in range(7))
        G_col, GL_col, kb_scale, kd_scale, eG = (small(16) for _ in range(5))
        mixed = s_.n
        A1 = s_(NT * 776).rearrange("p (t n) -> p t n", t=NT)
        qT = s_(4 * SEQ).rearrange("p (j n) -> p j n", j=4)
        kT = s_(SEQ)
        SC = s_(AH * 256).rearrange("p (h n) -> p h n", h=AH)
        PT = s_(AH * 256).rearrange("p (h n) -> p h n", h=AH)
        rt = s_(4 * 320).rearrange("p (a n) -> p a n", a=4)
        a_ss, a_rs = small(40), small(40)
        a_max, a_nmax, a_sum, a_sink, a_rec = (small(8) for _ in range(5))
        QKv = A1[:, :, 0:640]
        sq_tmp = SCR[:, mixed + NT * 776:mixed + NT * 776 + NT * 640].rearrange("p (t n) -> p t n", t=NT)

        def attn_pe(pe):
            for n in range(8):
                c, t = (c_kv, n) if n < 4 else (c_q, n - 4)
                if n % 4 == 0:
                    pe.wait_ge(w_landed[c % RING], landed(c))
                if n >= 4:
                    pe.wait_ge(sg("a_proj_out"), n - 3)
                width = 264 if n < 4 else 512
                w = slot_of(c)[:, 0:KT * width].rearrange("p (k n) -> p k n", k=KT)
                for k in range(KT):
                    mm = pe.matmul(PB[4 + n % 4][:, 0:width], HT[:, k, t * P:(t + 1) * P], w[:, k, :], start=(k == 0), stop=(k == KT - 1))
                mm.then_inc(sg("a_proj"), 1)
            pe.wait_ge(sg("g_gates"), 1)
            pe.wait_ge(params_in, PARAMS)
            pe.transpose(PB[2][:, 0:48], cwr[0:48, :], ident[0:48, 0:48]).then_inc(sg("d_cw"), 1)
            pe.matmul(PB[0][:, 0:16], const("cum"), g_val, start=True, stop=True)
            pe.matmul(PB[1][:, 0:16], const("chunk"), g_val, start=True, stop=True).then_inc(sg("g_cum"), 1)
            pe.wait_ge(sg("a_proj_out"), 8)
            for n in range(4):
                gproj_pe(pe, n)
            pe.wait_ge(sg("a_rope"), 1)
            pe.wait_ge(sg("d_conv_ready"), 1)
            for t in range(NT):
                b = PB[2 + t % 2]
                if t >= 2:
                    pe.wait_ge(sg("a_qt_out"), t - 1)
                for j in range(4):
                    pe.transpose(b[:, j * P:(j + 1) * P], QKv[:, t, j * P:(j + 1) * P], ident)
                pe.transpose(PB[6][:, t * P:(t + 1) * P], QKv[:, t, 512:640], ident).then_inc(sg("a_qt"), 1)
            for t in range(NT):
                if t == 0:
                    pe.wait_ge(sg("a_qt_out"), NT + 1)
                    pe.wait_ge(sg("g_left"), 1)
                lo = max(t - 1, 0) * P
                n = (t + 1) * P - lo
                if t:
                    pe.wait_ge(sg("a_masked"), 4 * t)
                for g in range(2):
                    for j in range(4):
                        h = 4 * g + j
                        mm = pe.matmul(PB[h // 2][:, (h % 2) * 256 + 256 - n:(h % 2) * 256 + 256], qT[64 * g:64 * g + 64, j, t * P:(t + 1) * P],
                                       kT[64 * g:64 * g + 64, lo:lo + n], start=True, stop=True)
                        if h % 2:
                            mm.then_inc(sg("a_scores"), 1)
                gproj_pe(pe, 4 + 3 * t)
                gproj_pe(pe, 5 + 3 * t)
                pe.wait_ge(sg("a_exp"), AH * (t + 1))
                for hp in range(4):
                    if t == 0 and hp < 2:
                        g_left_bank(pe, 2 - hp)
                    if hp >= 2:
                        pe.wait_ge(sg("a_pt_out"), 4 * t + hp - 1)
                    for h in (2 * hp, 2 * hp + 1):
                        for b in range(0 if t else 1, 2):
                            mm = pe.transpose(PB[4 + hp % 2][:, (h % 2) * 256 + b * P:(h % 2) * 256 + (b + 1) * P], SC[:, h, b * P:(b + 1) * P], ident)
                    mm.then_inc(sg("a_pt"), 1)
                for h in range(AH):
                    pe.wait_ge(sg("a_pt_out"), 4 * t + h // 2 + 1)
                    if t and h == 0:
                        pe.wait_ge(sg("a_y"), t)
                    for b in range(0 if t else 1, 2):
                        mm = pe.matmul(PB[6][:, h * 64:(h + 1) * 64], PT[:, h, b * P:(b + 1) * P],
                                       A1[:, t - 1 + b, 640 + 64 * (h // 4):704 + 64 * (h // 4)], start=(b == (0 if t else 1)), stop=(b == 1))
                mm.then_inc(sg("a_pv"), 1)
                gproj_pe(pe, 6 + 3 * t)

        def attn_act(act, step):
            for n in range(8):
                t = n % 4
                act.wait_ge(sg("a_proj"), n + 1)
                if n < 4:
                    act.copy(A1[:, t, 512:776], PB[4 + n % 4][:, 0:264]).then_inc(sg("a_proj_out"), 1)
                else:
                    act.copy(A1[:, t, 0:512].rearrange("p (j g d) -> p g j d", j=4, g=2),
                             PB[4 + n % 4][:, :].rearrange("p (g j d) -> p g j d", g=2, j=4)).then_inc(sg("a_proj_out"), 1)
                if n == 3:
                    act.wait_ge(params_in, PARAMS)
                    act.wait_ge(sg("g_pre"), 1)
                    act.activation(g_e, g_abs, ACT.Exp, scale=-1.0)
                    act.activation(ea[:, 0:4], alog_b, ACT.Exp)
                    act.activation(beta.rearrange("p (t h) -> p t h", t=NT), A1[:, :, 772:776], ACT.Exp, scale=-1.0).then_inc(sg("g_exp"), 1)
                    act.wait_ge(sg("g_one"), 1)
                    act.activation(g_sp, g_e, ACT.Ln).then_inc(sg("g_ln"), 1)
            act.wait_ge(sg("a_proj_out"), 8)
            act.activation(sq_tmp, QKv, ACT.Square).then_inc(sg("a_sq"), 1)
            for n in range(4):
                gproj_act(act, n)
            for t in range(NT):
                act.wait_ge(sg("a_qt"), t + 1)
                act.copy(qT[:, :, t * P:(t + 1) * P], PB[2 + t % 2][:, :].rearrange("p (j q) -> p j q", j=4)).then_inc(sg("a_qt_out"), 1)
            act.copy(kT, PB[6][:, :]).then_inc(sg("a_qt_out"), 1)
            for n in range(3):
                gsilu_act(act, n)
            for t in range(NT):
                act.wait_ge(sg("a_max"), t + 1)
                w = slice(0, 256) if t else slice(P, 256)
                for h in range(AH):
                    act.activation(SC[:, h, w], SC[:, h, w], ACT.Exp, bias=a_nmax[:, h:h + 1], accum_out=a_sum[:, h:h + 1]).then_inc(sg("a_exp"), 1)
                act.activation(a_sink, a_sink, ACT.Exp).then_inc(sg("a_sinkexp"), 1)
                if t:
                    gsilu_act(act, 3 + 3 * t)
                gproj_act(act, 4 + 3 * t)
                gproj_act(act, 5 + 3 * t)
                gsilu_act(act, 4 + 3 * t)
                for hp in range(4):
                    act.wait_ge(sg("a_pt"), 4 * t + hp + 1)
                    o = PT[:, 2 * hp:2 * hp + 2, w]
                    act.copy(o, PB[4 + hp % 2][:, :].rearrange("p (h n) -> p h n", h=2)[:, :, w]).then_inc(sg("a_pt_out"), 1)
                gsilu_act(act, 5 + 3 * t)
                gproj_act(act, 6 + 3 * t)
            gsilu_act(act, 3 + 3 * NT)

        def attn_pool(pool, step):
            pool.wait_ge(sg("a_sums"), 1)
            step.then(pool.tensor_scalar(a_rs, a_ss, 1.0 / ADH, EPS, ALU.mult, ALU.add))
            pool.tensor_tensor(a_rs, a_rs, mhalf[:, 0:40], ALU.pow).then_inc(sg("a_rstd"), 1)

        def attn_dve(dve, step):
            dve.wait_ge(params_in, PARAMS)
            dve.wait_ge(sg("a_proj_out"), 4)
            gv = lambda a: a.rearrange("p (t h) -> p t h", t=NT)
            bh = lambda a: a[:, None, :].to_broadcast([P, NT, 4])
            step.then(dve.tensor_tensor(gv(g_raw), A1[:, :, 768:772], bh(dtb_b), ALU.add))
            step.then(dve.tensor_scalar(g_val, g_raw, -1.0, None, ALU.mult))
            dve.tensor_tensor(g_abs, g_val, g_raw, ALU.max).then_inc(sg("g_pre"), 1)
            step.then(dve.tensor_scalar(g_raw, g_raw, 0.0, None, ALU.max))
            dve.wait_ge(sg("g_exp"), 1)
            dve.tensor_scalar(g_e, g_e, 1.0, None, ALU.add).then_inc(sg("g_one"), 1)
            step.then(dve.tensor_scalar(beta, beta, 1.0, None, ALU.add))
            step.then(dve.reciprocal(beta, beta))
            dve.wait_ge(sg("g_ln"), 1)
            step.then(dve.tensor_tensor(g_raw, g_raw, g_sp, ALU.add))
            dve.scalar_tensor_tensor(gv(g_val), gv(g_raw), -1.0, bh(ea[:, 0:4]), ALU.mult, ALU.mult).then_inc(sg("g_gates"), 1)
            dve.wait_ge(sg("d_cw"), 1)
            dve.tensor_copy(cw, PB[2][:, 0:48]).then_inc(sg("d_conv_ready"), 1)
            dve.wait_ge(sg("d_conv_ready"), 1)
            dve.wait_ge(sg("a_proj"), 8)
            dve.memset(xc[:, :, 0:3], 0.0).then_inc(sg("d_conv_ready"), 1)
            dve.wait_ge(sg("a_sq"), 1)
            dve.tensor_reduce(a_ss.rearrange("p (t h) -> p t h", t=NT), sq_tmp.rearrange("p t (h d) -> p t h d", d=ADH), AX, ALU.add).then_inc(sg("a_sums"), 1)
            dve.wait_ge(sg("a_rstd"), 1)
            dve.wait_ge(sg("a_proj_out"), 8)
            for t in range(NT):
                v = QKv[:, t, :].rearrange("p (h d) -> p h d", d=ADH)
                step(dve.tensor_tensor(v, v, a_rs[:, t * 10:(t + 1) * 10, None].to_broadcast([P, AQK, ADH]), ALU.mult))
            step.wait()
            step.then(dve.tensor_tensor(QKv, QKv, qk_gain[:, None, :].to_broadcast([P, NT, 640]), ALU.mult))
            x1 = [QKv[:, t, :].rearrange("p (h d) -> p h d", d=ADH)[:, :, 0:8] for t in range(NT)]
            x2 = [QKv[:, t, :].rearrange("p (h d) -> p h d", d=ADH)[:, :, 8:16] for t in range(NT)]
            rot = [[rt[:, a, t * 80:(t + 1) * 80].rearrange("p (h d) -> p h d", d=8) for t in range(NT)] for a in range(4)]
            for t in range(NT):
                cs = const("rcos")[:, None, t * 8:(t + 1) * 8].to_broadcast([P, AQK, 8])
                sn = const("rsin")[:, None, t * 8:(t + 1) * 8].to_broadcast([P, AQK, 8])
                step(dve.tensor_tensor(rot[0][t], x1[t], cs, ALU.mult))
                step(dve.tensor_tensor(rot[1][t], x2[t], sn, ALU.mult))
                step(dve.tensor_tensor(rot[2][t], x2[t], cs, ALU.mult))
                step(dve.tensor_tensor(rot[3][t], x1[t], sn, ALU.mult))
            step.wait()
            for t in range(NT):
                step(dve.tensor_tensor(x1[t], rot[0][t], rot[1][t], ALU.subtract))
                step(dve.tensor_tensor(x2[t], rot[2][t], rot[3][t], ALU.add))
            step.wait()
            dve.tensor_copy(rt[:, 0, 0:1], rt[:, 0, 0:1]).then_inc(sg("a_rope"), 1)
            dve.wait_ge(sg("g_cum"), 1)
            step(dve.tensor_copy(G_col, PB[0][:, 0:16]))
            step(dve.tensor_copy(GL_col, PB[1][:, 0:16]))
            step.wait()
            dve.tensor_tensor(GL_col, GL_col, G_col, ALU.subtract).then_inc(sg("g_left"), 1)
            for n in range(3):
                gconv_dve(dve, n, step)
            for t in range(NT):
                w = slice(0, 256) if t else slice(P, 256)
                n = 256 if t else P
                for b in range(4):
                    dve.wait_ge(sg("a_scores"), 4 * t + b + 1)
                    dve.scalar_tensor_tensor(SC[:, 2 * b:2 * b + 2, w], PB[b][:, :].rearrange("p (h n) -> p h n", h=2)[:, :, w], ADH ** -0.5,
                                             const("window")[:, None, w].to_broadcast([P, 2, n]), ALU.mult, ALU.add).then_inc(sg("a_masked"), 1)
                dve.wait_ge(sg("a_masked"), 4 * (t + 1))
                step.then(dve.tensor_reduce(a_max, SC[:, :, w], AX, ALU.max))
                step.then(dve.tensor_tensor(a_max, a_max, sink_b, ALU.max))
                step(dve.tensor_tensor(a_sink, sink_b, a_max, ALU.subtract))
                step.wait()
                dve.tensor_scalar(a_nmax, a_max, -1.0, None, ALU.mult).then_inc(sg("a_max"), 1)
                if t:
                    gconv_dve(dve, 3 + 3 * t, step)
                gconv_dve(dve, 4 + 3 * t, step)
                gconv_dve(dve, 5 + 3 * t, step)
                dve.wait_ge(sg("a_exp"), AH * (t + 1))
                dve.wait_ge(sg("a_sinkexp"), t + 1)
                step.then(dve.tensor_tensor(a_rec, a_sum, a_sink, ALU.add))
                step.then(dve.reciprocal(a_rec, a_rec))
                dve.wait_ge(sg("a_pv"), t + 1)
                dve.tensor_tensor(XN[:, t, 0:512].rearrange("p (h d) -> p h d", h=AH), PB[6][:, :].rearrange("p (h d) -> p h d", h=AH),
                                  a_rec[:, :, None].to_broadcast([P, AH, ADH]), ALU.mult).then_inc(sg("a_y"), 1)
            gconv_dve(dve, 3 + 3 * NT, step)

        t4 = lambda a: a.rearrange("p (t n) -> p t n", t=NT)
        r_ = Carve(ring[:, 0:2, :].rearrange("p a n -> p (a n)"), 2 * SLOT)
        CV = [r_(3 * 512).rearrange("p (s n) -> p s n", s=3) for _ in range(GH)]
        xc = r_(3 * 515).rearrange("p (s n) -> p s n", s=3)
        zs_at = lambda h: XN[:, :, 512 + h * GD:512 + (h + 1) * GD]

        def g_bank(n):
            return PB[(7, 5, 4, 7)[n] if n < 4 else 7]

        def g_left_bank(eng, n):
            eng.wait_ge(*((sg("d_zs"), n // 4 + 1) if n % 4 == 3 else (sg("d_x"), 3 * (n // 4) + n % 4 + 1)))

        def gproj_pe(pe, n):
            h, s = n // 4, n % 4
            c = c_gdn + h
            if s == 0:
                pe.wait_ge(w_landed[c % RING], landed(c))
            w = slot_of(c).rearrange("p (k s n) -> p k s n", k=KT, s=4)
            if n >= 3:
                g_left_bank(pe, n - 1 if n > 3 else 0)
            if s < 3:
                for k in range(KT):
                    mm = pe.matmul(g_bank(n)[:, :], w[:, k, s, :], HT[:, k, :], start=(k == 0), stop=(k == KT - 1))
                mm.then_inc(sg("d_proj"), 1)
            else:
                for t in range(NT):
                    for k in range(KT):
                        mm = pe.matmul(g_bank(n)[:, t * P:(t + 1) * P], HT[:, k, t * P:(t + 1) * P], w[:, k, 3, :], start=(k == 0), stop=(k == KT - 1))
                mm.then_inc(sg("d_z"), 1)

        def gproj_act(act, n):
            h, s = n // 4, n % 4
            if s < 3:
                act.wait_ge(sg("d_proj"), 3 * h + s + 1)
                if n == 0:
                    act.wait_ge(sg("d_conv_ready"), 2)
                if h:
                    act.wait_ge(sg("d_conv"), 3 * (h - 1) + s + 1)
                act.copy(xc[:, s, 3:515], g_bank(n)[:, :]).then_inc(sg("d_x"), 1)
            else:
                act.wait_ge(sg("d_z"), h + 1)
                act.activation(zs_at(h), t4(g_bank(n)[:, :]), ACT.Silu).then_inc(sg("d_zs"), 1)

        def gsilu_act(act, n):
            h, s = n // 4, n % 4
            if s < 3:
                act.wait_ge(sg("d_conv"), 3 * h + s + 1)
                act.activation(CV[h][:, s, :], CV[h][:, s, :], ACT.Silu).then_inc(sg("d_silu"), 1)

        def gconv_dve(dve, n, step):
            h, s = n // 4, n % 4
            if s == 3:
                return
            o = CV[h][:, s, :]
            dve.wait_ge(sg("d_x"), 3 * h + s + 1)
            tap = lambda i: cw[:, i * 12 + 4 * s + h:i * 12 + 4 * s + h + 1]
            step.then(dve.tensor_scalar(o, xc[:, s, 0:512], tap(0), None, ALU.mult))
            for i in (1, 2):
                step.then(dve.scalar_tensor_tensor(o, xc[:, s, i:i + 512], tap(i), o, ALU.mult, ALU.add))
            dve.scalar_tensor_tensor(o, xc[:, s, 3:515], tap(3), o, ALU.mult, ALU.add).then_inc(sg("d_conv"), 1)

        s_.n = mixed
        hb_ = Carve(HT[:, :, :].rearrange("p k n -> p (k n)"), KT * SEQ)
        heads = []
        for u in range(2):
            def b512(u=u):
                return t4((hb_ if u and hb_.n + 512 <= hb_.size else s_)(512))
            w = dict(N1=b512(), nwT=b512(), e_dec=b512(), e_decT=b512(), eGB=b512(), Tm=b512(), TTm=b512(), Cm=b512(),
                     qd=b512(), kbg=b512(), kd=b512(), vb=b512(), og=b512(), VN=s_(128), St=s_(128),
                     n_ss=small(8), n_rs=small(8), o_ss=small(4), o_rs=small(4), bank=[PB[4 * u + i] for i in range(4)])
            heads.append(type("Head", (), w))
        pairs = [(2 * g, 2 * g + 1) for g in range(GH // 2)]

        def nth(h, n=0, of=1):
            return 2 * of * (h // 2) + 2 * n + h % 2 + 1

        def set_free(eng, h):
            if h < 2:
                eng.wait_ge(sg("a_y"), NT)
                eng.wait_ge(sg("d_z"), GH)
            else:
                eng.wait_ge(sg("d_v"), nth(h - 2, 2 * NT - 1, 2 * NT))
                eng.wait_ge(sg("d_o"), nth(h - 2, 2 * NT - 1, 2 * NT))
                eng.wait_ge(sg("d_oss"), nth(h - 2))

        def gdn_pe(pe):
            for pair in pairs:
                for h in pair:
                    if h == 0:
                        pe.wait_ge(sg("a_masked"), 4 * NT)
                    elif h == 1:
                        pe.wait_ge(sg("a_pt_out"), 4 * NT)
                        pe.wait_ge(sg("a_y"), NT)
                        g_left_bank(pe, 4 * GH - 1)
                    else:
                        pe.wait_ge(sg("d_v_out"), nth(h - 2, 2 * NT - 1, 2 * NT))
                        pe.wait_ge(sg("d_o_out"), nth(h - 2, 2 * NT - 1, 2 * NT))
                        pe.wait_ge(sg("d_S"), nth(h - 2, 2 * NT, 2 * NT + 1))
                    for t in range(NT):
                        mm = pe.matmul(heads[h % 2].bank[0][:, t * P:(t + 1) * P], g_val[:, 4 * t + h:4 * t + h + 1].to_broadcast([P, P]), const("cum"), start=True, stop=True)
                    mm.then_inc(sg("d_gb"), 1)
                for h in pair:
                    H = heads[h % 2]
                    pe.wait_ge(sg("d_sq"), nth(h))
                    for s, sq in enumerate((H.N1, H.nwT)):
                        for t in range(NT):
                            mm = pe.matmul(H.bank[1][:, 4 * s + t:4 * s + t + 1], sq[:, t, :], ones[:, 0:1], start=True, stop=True)
                    mm.then_inc(sg("d_ss"), 1)
                for h in pair:
                    H = heads[h % 2]
                    pe.wait_ge(sg("d_rs"), nth(h))
                    for s in range(2):
                        for t in range(NT):
                            mm = pe.matmul(H.bank[2 + s][:, t * P:(t + 1) * P], H.n_rs[:, 4 * s + t:4 * s + t + 1].to_broadcast([P, P]), ident, start=True, stop=True)
                    mm.then_inc(sg("d_rb"), 1)
                for h in pair:
                    H, cv = heads[h % 2], CV[h]
                    pe.wait_ge(sg("d_qk"), nth(h))
                    pe.wait_ge(sg("d_egb"), nth(h))
                    pe.wait_ge(sg("d_ss_out"), nth(h))
                    for t in range(NT):
                        mm = pe.matmul(H.bank[t // 2][:, (t % 2) * 256:(t % 2) * 256 + 256], cv[:, 1, t * P:(t + 1) * P], cv[:, 0:2, t * P:(t + 1) * P],
                                       start=True, stop=True)
                    mm.then_inc(sg("d_kk"), 1)
                    for s in range(2):
                        for t in range(NT):
                            mm = pe.transpose(H.bank[2 + s][:, t * P:(t + 1) * P], cv[:, 1 + s, t * P:(t + 1) * P], ident)
                    mm.then_inc(sg("d_kv"), 1)
                for lv in range(LEVELS):
                    for h in pair:
                        H = heads[h % 2]
                        pe.wait_ge(sg("d_T"), nth(h, lv, LEVELS))
                        for t in range(NT):
                            mm = pe.matmul(H.bank[0][:, t * P:(t + 1) * P], H.Cm[:, t, :], H.TTm[:, t, :] if lv else ident, start=True, stop=True)
                        mm.then_inc(sg("d_n1"), 1)
                    for h in pair if lv else ():
                        H = heads[h % 2]
                        pe.wait_ge(sg("d_n1_out"), nth(h, lv - 1, LEVELS - 1))
                        pe.wait_ge(sg("d_Tm"), nth(h, lv - 1, LEVELS - 1))
                        for t in range(NT):
                            mm = pe.matmul(H.bank[1][:, t * P:(t + 1) * P], H.Tm[:, t, :], H.N1[:, t, :], start=True, stop=True)
                        mm.then_inc(sg("d_tt"), 1)
                        if lv < LEVELS - 1:
                            if lv == 1:
                                pe.wait_ge(sg("d_scaled"), nth(h))
                            for t in range(NT):
                                mm = pe.matmul(H.bank[2][:, t * P:(t + 1) * P], H.N1[:, t, :], H.Tm[:, t, :], start=True, stop=True)
                            mm.then_inc(sg("d_t"), 1)
                for h in pair:
                    H = heads[h % 2]
                    pe.wait_ge(sg("d_inv"), nth(h))
                    for t in range(NT):
                        mm = pe.matmul(H.bank[3][:, t * P:(t + 1) * P], H.kbg[:, t, :], H.TTm[:, t, :], start=True, stop=True)
                    mm.then_inc(sg("d_w"), 1)
                for h in pair:
                    pe.wait_ge(sg("d_w_out"), nth(h))
                    pe.wait_ge(sg("d_qd"), nth(h))
                for n in range(2 * NT):
                    t, half = n // 2, (n % 2) * CH
                    r, m = slice(half, half + CH), n % 2
                    for h in pair:
                        H = heads[h % 2]
                        pe.matmul(H.bank[3 * m][r, 0:GD], H.TTm[:, t, r], H.vb[:, t, :], start=True, stop=False)
                        pe.wait_ge(sg("d_S"), nth(h, n, 2 * NT + 1))
                        pe.matmul(H.bank[3 * m][r, 0:GD], H.nwT[:, t, r], H.St, start=False, stop=True).then_inc(sg("d_v"), 1)
                        if n >= 2:
                            pe.wait_ge(sg("d_o_out"), nth(h, n - 2, 2 * NT))
                        pe.matmul(H.bank[1][r, m * GD:(m + 1) * GD], H.qd[:, t, r], H.St, start=True, stop=False)
                    for h in pair:
                        H = heads[h % 2]
                        pe.wait_ge(sg("d_v_out"), nth(h, n, 2 * NT))
                        pe.matmul(H.bank[2][:, 0:GD], H.kd[r, t, :], H.VN[r, :], start=True, stop=True).then_inc(sg("d_kv_new"), 1)
                        pe.matmul(H.bank[1][r, m * GD:(m + 1) * GD], H.e_decT[r, t, r], H.VN[r, :], start=False, stop=True).then_inc(sg("d_o"), 1)

        def gdn_act(act, step):
            act.wait_ge(sg("g_left"), 1)
            act.activation(kd_scale, GL_col, ACT.Exp).then_inc(sg("d_eg"), 1)
            act.activation(eG, G_col, ACT.Exp).then_inc(sg("d_eg"), 1)
            act.wait_ge(sg("d_eg"), 2)
            for pair in pairs:
                for h in pair:
                    H = heads[h % 2]
                    act.wait_ge(sg("d_silu"), 3 * h + 3)
                    set_free(act, h)
                    step(act.activation(H.N1, t4(CV[h][:, 0, :]), ACT.Square))
                    step.wait()
                    act.activation(H.nwT, t4(CV[h][:, 1, :]), ACT.Square).then_inc(sg("d_sq"), 1)
                for h in pair:
                    H = heads[h % 2]
                    act.wait_ge(sg("d_diff"), nth(h))
                    act.activation(H.eGB, t4(H.bank[0][:, :]), ACT.Exp).then_inc(sg("d_egb"), 1)
                    step(act.activation(H.e_dec, H.e_dec, ACT.Exp))
                    step.wait()
                    act.activation(H.e_decT, H.e_decT, ACT.Exp, scale=-1.0).then_inc(sg("d_dec"), 1)
                for h in pair:
                    H = heads[h % 2]
                    act.wait_ge(sg("d_kv"), nth(h))
                    act.wait_ge(sg("d_kbs"), 1)
                    for t in range(NT):
                        c = slice(4 * t + h, 4 * t + h + 1)
                        step(act.activation(H.kbg[:, t, :], H.bank[2][:, t * P:(t + 1) * P], ACT.Copy, scale=kb_scale[:, c]))
                        step(act.activation(H.kd[:, t, :], H.bank[2][:, t * P:(t + 1) * P], ACT.Copy, scale=kd_scale[:, c]))
                        if t == NT - 1:
                            step.wait()
                        last = act.activation(H.vb[:, t, :], H.bank[3][:, t * P:(t + 1) * P], ACT.Copy, scale=beta[:, c])
                        if t < NT - 1:
                            step(last)
                    last.then_inc(sg("d_scaled"), 1)
                for lv in range(1, LEVELS):
                    for h in pair:
                        H = heads[h % 2]
                        act.wait_ge(sg("d_n1"), nth(h, lv, LEVELS))
                        act.copy(H.N1, t4(H.bank[0][:, :])).then_inc(sg("d_n1_out"), 1)
                for h in pair:
                    H = heads[h % 2]
                    act.wait_ge(sg("d_w"), nth(h))
                    act.activation(H.nwT, t4(H.bank[3][:, :]), ACT.Copy, scale=-1.0).then_inc(sg("d_w_out"), 1)
                for n in range(2 * NT):
                    t, half = n // 2, (n % 2) * CH
                    r, m = slice(half, half + CH), n % 2
                    for h in pair:
                        H = heads[h % 2]
                        act.wait_ge(sg("d_v"), nth(h, n, 2 * NT))
                        act.copy(H.VN[r, :], H.bank[3 * m][r, 0:GD]).then_inc(sg("d_v_out"), 1)
                    for h in pair:
                        H = heads[h % 2]
                        act.wait_ge(sg("d_o"), nth(h, n, 2 * NT))
                        act.copy(H.og[r, t, :], H.bank[1][r, m * GD:(m + 1) * GD]).then_inc(sg("d_o_out"), 1)
                for h in pair:
                    H = heads[h % 2]
                    act.wait_ge(sg("d_o_out"), nth(h, 2 * NT - 1, 2 * NT))
                    for t in range(NT):
                        last = act.activation(H.N1[:, t, :], H.og[:, t, :], ACT.Square, accum_out=H.o_ss[:, t:t + 1])
                        if t < NT - 1:
                            step(last)
                            step.wait()
                    last.then_inc(sg("d_oss"), 1)

        def gdn_pool(pool, step):
            for pair in pairs:
                for h in pair:
                    H = heads[h % 2]
                    pool.wait_ge(sg("d_ss_out"), nth(h))
                    if h >= 2:
                        pool.wait_ge(sg("d_rb"), nth(h - 2))
                    step.then(pool.tensor_scalar(H.n_rs, H.n_ss, 1.0, EPS, ALU.mult, ALU.add))
                    step.then(pool.tensor_tensor(H.n_rs, H.n_rs, mhalf[:, 0:8], ALU.pow))
                    pool.tensor_scalar(H.n_rs[:, 0:4], H.n_rs[:, 0:4], GD ** -0.5, None, ALU.mult).then_inc(sg("d_rs"), 1)
                for h in pair:
                    H = heads[h % 2]
                    pool.wait_ge(sg("d_oss"), nth(h))
                    step.then(pool.tensor_scalar(H.o_rs, H.o_ss, 1.0 / GD, EPS, ALU.mult, ALU.add))
                    pool.tensor_tensor(H.o_rs, H.o_rs, mhalf[:, 0:4], ALU.pow).then_inc(sg("d_ors"), 1)

        def gdn_dve(dve, step):
            bc = lambda name: const(name)[:, None, :].to_broadcast([P, NT, P])
            for pair in pairs:
                for h in pair:
                    H = heads[h % 2]
                    set_free(dve, h)
                    dve.wait_ge(sg("d_gb"), nth(h))
                    Gi = G_col.rearrange("p (t h) -> p t h", h=4)[:, :, h:h + 1].to_broadcast([P, NT, P])
                    step.then(dve.tensor_tensor(H.e_dec, Gi, t4(H.bank[0][:, :]), ALU.subtract))
                    step.then(dve.tensor_scalar(H.e_decT, H.e_dec, 0.0, None, ALU.max))
                    dve.tensor_scalar(H.e_dec, H.e_dec, 0.0, None, ALU.min).then_inc(sg("d_diff"), 1)
                for h in pair:
                    H = heads[h % 2]
                    dve.wait_ge(sg("d_ss"), nth(h))
                    dve.tensor_copy(H.n_ss, H.bank[1][:, 0:8]).then_inc(sg("d_ss_out"), 1)
                if pair[0] == 0:
                    dve.wait_ge(sg("d_eg"), 2)
                    dve.tensor_tensor(kb_scale, beta, eG, ALU.mult).then_inc(sg("d_kbs"), 1)
                for h in pair:
                    H, cv = heads[h % 2], CV[h]
                    dve.wait_ge(sg("d_rb"), nth(h))
                    step(dve.tensor_tensor(cv[:, 0, :], cv[:, 0, :], H.bank[2][:, :], ALU.mult))
                    step.wait()
                    dve.tensor_tensor(cv[:, 1, :], cv[:, 1, :], H.bank[3][:, :], ALU.mult).then_inc(sg("d_qk"), 1)
                for h in pair:
                    H = heads[h % 2]
                    dve.wait_ge(sg("d_dec"), nth(h))
                    for t in range(NT):
                        step(dve.scalar_tensor_tensor(H.e_dec[:, t, :], H.e_dec[:, t, :], beta[:, 4 * t + h:4 * t + h + 1], const("strict"), ALU.mult, ALU.mult))
                    step(dve.tensor_tensor(H.e_decT, H.e_decT, bc("inclT"), ALU.mult))
                for h in pair:
                    H = heads[h % 2]
                    step.wait()
                    dve.wait_ge(sg("d_kk"), nth(h))
                    for b in range(2):
                        kk = H.bank[b][:, :].rearrange("p (t s n) -> p t s n", t=2, s=2)
                        step(dve.tensor_tensor(H.e_dec[:, 2 * b:2 * b + 2, :], kk[:, :, 1, :], H.e_dec[:, 2 * b:2 * b + 2, :], ALU.mult))
                        step(dve.tensor_tensor(H.e_decT[:, 2 * b:2 * b + 2, :], kk[:, :, 0, :], H.e_decT[:, 2 * b:2 * b + 2, :], ALU.mult))
                    step.wait()
                    dve.tensor_tensor(H.Cm, H.e_dec, bc("level0"), ALU.mult).then_inc(sg("d_T"), 1)
                for h in pair:
                    H = heads[h % 2]
                    dve.wait_ge(sg("d_T"), nth(h, 0, LEVELS))
                    dve.tensor_tensor(H.Tm, bc("ident"), H.Cm, ALU.subtract).then_inc(sg("d_Tm"), 1)
                for lv in range(LEVELS):
                    for h in pair:
                        H = heads[h % 2]
                        dve.wait_ge(sg("d_n1"), nth(h, lv, LEVELS))
                        if lv == 0:
                            dve.wait_ge(sg("d_Tm"), nth(h, 0, LEVELS - 1))
                        if lv < LEVELS - 1:
                            step(dve.tensor_tensor(H.Cm, H.e_dec, bc(f"level{lv + 1}"), ALU.mult))
                    for h in pair:
                        H = heads[h % 2]
                        if lv:
                            dve.wait_ge(sg("d_tt"), nth(h, lv - 1, LEVELS - 1))
                            dve.wait_ge(sg("d_T"), nth(h, lv, LEVELS))
                        step.wait()
                        dve.tensor_tensor(H.TTm, H.TTm if lv else bc("ident"), t4(H.bank[1 if lv else 0][:, :]), ALU.subtract)\
                            .then_inc(sg("d_T" if lv < LEVELS - 1 else "d_inv"), 1)
                    for h in pair if 0 < lv < LEVELS - 1 else ():
                        H = heads[h % 2]
                        dve.wait_ge(sg("d_t"), nth(h, lv - 1, LEVELS - 2))
                        dve.wait_ge(sg("d_Tm"), nth(h, lv - 1, LEVELS - 1))
                        dve.tensor_tensor(H.Tm, H.Tm, t4(H.bank[2][:, :]), ALU.subtract).then_inc(sg("d_Tm"), 1)
                for h in pair:
                    H = heads[h % 2]
                    dve.tensor_tensor(H.qd, t4(CV[h][:, 0, :]), H.eGB, ALU.mult).then_inc(sg("d_qd"), 1)
                for h in pair:
                    dve.memset(heads[h % 2].St, 0.0).then_inc(sg("d_S"), 1)
                for n in range(2 * NT):
                    t, half = n // 2, (n % 2) * CH
                    for h in pair:
                        H = heads[h % 2]
                        dve.wait_ge(sg("d_S"), nth(h, n, 2 * NT + 1))
                        dve.wait_ge(sg("d_kv_new"), nth(h, n, 2 * NT))
                        dve.scalar_tensor_tensor(H.St, H.St, H.eGB[:, t, half + CH - 1:half + CH], H.bank[2][:, 0:GD], ALU.mult, ALU.add).then_inc(sg("d_S"), 1)
                for h in pair:
                    H = heads[h % 2]
                    dve.wait_ge(sg("d_ors"), nth(h))
                    dve.wait_ge(sg("d_zs"), h + 1)
                    for t in range(NT):
                        step(dve.scalar_tensor_tensor(H.og[:, t, :], H.og[:, t, :], H.o_rs[:, t:t + 1], gdn_gain, ALU.mult, ALU.mult))
                    step.wait()
                    dve.tensor_tensor(zs_at(h), H.og, zs_at(h), ALU.mult).then_inc(sg("d_y"), 1)


        def oute_pe(pe):
            pe.wait_ge(sg("d_y"), GH)
            for n in range(8):
                t, g = n // 2, n % 2
                if n >= 4:
                    pe.wait_ge(sg(("m_tr_a", "m_tr_d")[g]), (n - 4) // 2 + 1)
                for j in range(4):
                    mm = pe.transpose(PB[n % 4][:, j * P:(j + 1) * P], XN[:, t, g * 512 + j:(g + 1) * 512:4], ident)
                mm.then_inc(sg("m_tr"), 1)
            for g in range(2):
                pe.wait_ge(w_landed[(c_oute + g) % RING], landed(c_oute + g))
            for n in range(8):
                t, half = n // 2, n % 2
                pe.wait_ge(sg("m_tr_a"), t + 1)
                pe.wait_ge(sg("m_tr_d"), t + 1)
                if n >= 2:
                    pe.wait_ge(resid, n - 1)
                for g in range(2):
                    w = slot_of(c_oute + g).rearrange("p (k n) -> p k n", k=4)
                    for j in range(4):
                        mm = pe.matmul(PB[4 + n % 2][:, :], HT[:, 4 * g + j, t * P:(t + 1) * P], w[:, j, half * 512:(half + 1) * 512],
                                       start=(g + j == 0), stop=(g == 1 and j == 3))
                mm.then_inc(sg("m_out"), 1)

        def oute_act(act):
            for t in range(NT):
                act.wait_ge(sg("m_tr"), 2 * t + 1)
                act.copy(HT[:, 0:4, t * P:(t + 1) * P], PB[(2 * t) % 4][:, :].rearrange("p (k q) -> p k q", k=4)).then_inc(sg("m_tr_a"), 1)

        def oute_dve(dve):
            for t in range(NT):
                dve.wait_ge(sg("m_tr"), 2 * t + 2)
                dve.tensor_copy(HT[:, 4:8, t * P:(t + 1) * P], PB[(2 * t + 1) % 4][:, :].rearrange("p (k q) -> p k q", k=4)).then_inc(sg("m_tr_d"), 1)
            for n in range(8):
                t, half = n // 2, n % 2
                dve.wait_ge(sg("m_out"), n + 1)
                xs = X[:, t, half * 512:(half + 1) * 512]
                dve.tensor_tensor(xs, xs, PB[4 + n % 2][:, :], ALU.add).then_inc(resid, 1)
                if half:
                    norm_dve(dve, 1, t - 1)
            norm_dve(dve, 1, NT - 1)

        s_.n, s_.size = 0, CO_AT
        OH = [s_(NT * SLOTS).rearrange("p (t s) -> p t s", t=NT) for _ in range(2)]
        XG, XTt, SIL, HH = s_(512), s_(512), s_(512), s_(512)
        HHT = s_(4 * SLOTS)
        YS = [s_(512) for _ in range(2)]
        WOV = s_(SLOT)
        ROWS = WOV.rearrange("p (n d) -> p n d", n=4)
        OHG, OT = s_(512), s_(512)
        tg = lambda a: a.rearrange("p (t n) -> p t n", t=NT)
        LT = OT
        LG = tg(s_(NT * NR))
        dg, eg, selg, ohg = (tg(s_(16)) for _ in range(4))
        EL4 = s_(NT * 32).rearrange("p (t e g) -> p t e g", t=NT, g=NG)
        EL, EL2, dd, sel, oh1, oh2 = (tg(s_(NT * EPG)) for _ in range(6))
        gmax, vmax, m1, m2, e2, gate1, gate2, rsg, used1, used2 = (s_(NT) for _ in range(10))
        M1, M2, POS, POSM, T1, INR = (tg(s_(NT * NE)) for _ in range(6))
        MMz = s_((NT + 1) * NE)
        MM = tg(MMz[:, 0:NT * NE])
        dest_f = s_(2 * NT)
        cnt_f = s_(1)
        dest = sb("dest", [P, 2 * NT], I32)
        cnt = sb("cnt", [P, 1], I32)
        y_view = y_rows.rearrange("(e r) (h n) -> e r h n", e=NE, h=2)

        PER_LAYER = dict(logits=1, logitsT=1, logitsT_out=1, masks=1, counts=1, gdiff=1, ediff=1, rexp=2, routed=1, rows_stored=1, first_added=NT,
                         stored0=16 * NE, stored1=16 * NE,
                         **dict.fromkeys(("oh", "gat", "xg", "xt", "xt_out", "gu", "sil", "hh", "ht", "ht_out", "y", "y_out"), NE))

        def moe_sem(l, name):
            return sg(f"m_{name}" if name in PER_LAYER else f"m{l}_{name}")

        OVER = dict(pe=("v_gat", "v_xt", "v_g", "v_u", "v_ht", "v_y", "v_ot", "v_comb"), act=("v_xg", "v_sil", "v_ht_out"),
                    dve=("v_oh", "v_ohg", "v_xt_out", "v_hh", "v_y_out", "v_added"))

        def over_done(l, name):
            return next(sg(f"m{l}_over_{eng}") for eng, stages in OVER.items() if name in stages)

        def over_wait(l, name, n):
            stages = next(x for x in OVER.values() if name in x)
            return over_done(l, name), n * len(stages) + stages.index(name) + 1

        def moe_wait(l, name, value):
            return moe_sem(l, name), value + l * PER_LAYER.get(name, 0)

        def one_hot(dve, step, out_oh, diff):
            n = out_oh.shape[2]
            step.then(dve.tensor_scalar(out_oh, diff, 0.0, None, ALU.is_equal))
            step.then(dve.tensor_tensor(out_oh, out_oh, const("first")[:, None, 0:n].to_broadcast([P, NT, n]), ALU.mult))
            step.then(dve.tensor_reduce(vmax, out_oh, AX, ALU.max))
            step.then(dve.tensor_tensor(out_oh, out_oh, vmax[:, :, None].to_broadcast([P, NT, n]), ALU.is_equal))

        def route_pool(pool, l):
            if l:
                pool.wait_ge(*moe_wait(0, "logits", 1))
                pool.wait_ge(*moe_wait(0, "routed", 1))
            pool.dma_start(WR[:, :, 0:NG], k_rows(w_router_group[l], 0, NG)).then_inc(router_in, 16)
            pool.dma_start(WR[:, :, NG:NR], k_rows(w_router_expert[l], 0, NE)).then_inc(router_in, 16)
            pool.dma_start(br[:, 0:NG], b_router_group[l:l + 1, :].to_broadcast([P, NG])).then_inc(router_in, 16)
            pool.dma_start(br[:, NG:NR], b_router_expert[l:l + 1, :].to_broadcast([P, NE])).then_inc(router_in, 16)

        def logits_pe(pe, l, t):
            if t == 0:
                pe.wait_ge(router_in, 64 * (l + 1))
            pe.wait_ge(tr_out_a, 4 * (2 * l + 1) + t + 1)
            pe.wait_ge(tr_out_d, 4 * (2 * l + 1) + t + 1)
            for k in range(KT):
                mm = pe.matmul(PB[6][0:NR, t * P:(t + 1) * P], WR[:, k, :], HT[:, k, t * P:(t + 1) * P], start=(k == 0), stop=(k == KT - 1))
            if t == NT - 1:
                mm.then_inc(moe_sem(l, "logitsT"), 1)
            for u in range(NT) if t == NT - 1 else ():
                pe.wait_ge(*moe_wait(l, "logitsT_out", 1))
                mm = pe.transpose(PB[7][:, u * NR:(u + 1) * NR], LT[0:NR, u * P:(u + 1) * P], ident[0:NR, 0:NR])
            if t == NT - 1:
                mm.then_inc(moe_sem(l, "logits"), 1)

        def route_pe(pe, l):
            ms = lambda n: moe_sem(l, n)
            mw = lambda n, v: moe_wait(l, n, v)
            pe.wait_ge(*mw("masks", 1))
            pe.matmul(PB[5][:, 0:(NT + 1) * NE], const("before"), MMz, start=True, stop=False)
            for u in range(NT):
                mm = pe.matmul(PB[5][:, (u + 1) * NE:(NT + 1) * NE], ones, MM[:, u:u + 1, :].to_broadcast([P, NT - u, NE]), start=False, stop=(u == NT - 1))
            mm.then_inc(ms("counts"), 1)

        def route_act(act, l):
            ms = lambda n: moe_sem(l, n)
            mw = lambda n, v: moe_wait(l, n, v)
            act.wait_ge(*mw("gdiff", 1))
            act.activation(eg, dg, ACT.Exp).then_inc(ms("rexp"), 1)
            act.wait_ge(*mw("ediff", 1))
            act.activation(e2, m2, ACT.Exp).then_inc(ms("rexp"), 1)

        def route_dve(dve, l, step):
            ms = lambda n: moe_sem(l, n)
            mw = lambda n, v: moe_wait(l, n, v)
            bt = lambda a, n: a[:, :, None].to_broadcast([P, NT, n])
            dve.wait_ge(*mw("logitsT", 1))
            dve.tensor_copy(LT[0:NR, :], PB[6][0:NR, :]).then_inc(ms("logitsT_out"), 1)
            dve.wait_ge(*mw("logits", 1))
            dve.wait_ge(router_in, 64 * (l + 1))
            step.then(dve.tensor_tensor(LG, tg(PB[7][:, 0:NT * NR]), br[:, None, :].to_broadcast([P, NT, NR]), ALU.add))
            step.then(dve.tensor_reduce(gmax, LG[:, :, 0:NG], AX, ALU.max))
            dve.tensor_tensor(dg, LG[:, :, 0:NG], bt(gmax, NG), ALU.subtract).then_inc(ms("gdiff"), 1)
            dve.wait_ge(*mw("gdiff", 1))
            one_hot(dve, step, ohg, dg)
            step.then(dve.tensor_tensor(EL4, LG[:, :, NG:NR].rearrange("p t (g e) -> p t e g", g=NG),
                                        ohg[:, :, None, :].to_broadcast([P, NT, EPG, NG]), ALU.mult))
            step.then(dve.tensor_reduce(EL, EL4, AX, ALU.add))
            step.then(dve.tensor_reduce(m1, EL, AX, ALU.max))
            step.then(dve.tensor_tensor(dd, EL, bt(m1, EPG), ALU.subtract))
            one_hot(dve, step, oh1, dd)
            step.then(dve.scalar_tensor_tensor(EL2, oh1, -BIG, EL, ALU.mult, ALU.add))
            step.then(dve.tensor_reduce(m2, EL2, AX, ALU.max))
            step.then(dve.tensor_tensor(dd, EL2, bt(m2, EPG), ALU.subtract))
            one_hot(dve, step, oh2, dd)
            dve.tensor_tensor(m2, m2, m1, ALU.subtract).then_inc(ms("ediff"), 1)
            for M, oh in ((M1, oh1), (M2, oh2)):
                step(dve.tensor_tensor(M.rearrange("p t (g e) -> p t g e", g=NG), ohg[:, :, :, None].to_broadcast([P, NT, NG, EPG]),
                                       oh[:, :, None, :].to_broadcast([P, NT, NG, EPG]), ALU.mult))
            step(dve.memset(MMz[:, NT * NE:(NT + 1) * NE], 0.0))
            step.wait()
            dve.tensor_tensor(MM, M1, M2, ALU.add).then_inc(ms("masks"), 1)
            dve.wait_ge(*mw("counts", 1))
            dve.wait_ge(*mw("masks", 1))
            step.then(dve.tensor_copy(POS, tg(PB[5][:, 0:NT * NE])))
            step.then(dve.scalar_tensor_tensor(POSM, POS, 1.0, MM, ALU.add, ALU.mult))
            step.then(dve.tensor_scalar(POSM, POSM, -1.0, None, ALU.add))

        def gates_dve(dve, l, step):
            ms = lambda n: moe_sem(l, n)
            mw = lambda n, v: moe_wait(l, n, v)
            dve.wait_ge(*mw("rexp", 2))
            step.then(dve.tensor_reduce(rsg, eg, AX, ALU.add))
            step.then(dve.scalar_tensor_tensor(gate1, e2, 1.0, rsg, ALU.add, ALU.mult))
            step.then(dve.reciprocal(gate1, gate1))
            step.then(dve.tensor_tensor(gate2, gate1, e2, ALU.mult))
            step.then(dve.tensor_reduce(cnt_f, PB[5][:, NT * NE:(NT + 1) * NE], AX, ALU.max))
            step(dve.tensor_copy(cnt[:, :], cnt_f))
            step.then(dve.tensor_scalar(INR, POS, float(SLOTS), None, ALU.is_lt))
            step.then(dve.tensor_tensor(POS, POS, const("rowbase")[:, None, :].to_broadcast([P, NT, NE]), ALU.add))
            for k, (M, gate, used) in enumerate(((M1, gate1, used1), (M2, gate2, used2))):
                step.then(dve.tensor_tensor(T1, INR, M, ALU.mult))
                step.then(dve.tensor_reduce(used, T1, AX, ALU.add))
                step.then(dve.tensor_tensor(used, used, gate, ALU.mult))
                step.then(dve.tensor_tensor(T1, POS, T1, ALU.mult))
                step.then(dve.tensor_reduce(dest_f[:, k * NT:(k + 1) * NT], T1, AX, ALU.add))
            dve.tensor_copy(dest[:, :], dest_f).then_inc(ms("routed"), 1)
            dve.wait_ge(*mw("routed", 1))

        BX, BXT, BGU, BH, BY = PB[0], PB[1], PB[2], PB[3], PB[6]

        def gather_mm(pe, oh):
            for t in range(NT):
                for half in range(2):
                    mm = pe.matmul(BX[64 * half:64 * half + 64, :], oh[:, t, :], XN[:, t, half * 512:(half + 1) * 512], start=(t == 0), stop=(t == NT - 1))
            return mm

        def xt_mm(pe):
            for j in range(4):
                mm = pe.transpose(BXT[:, j * P:(j + 1) * P], XG[:, j:512:4], ident)
            return mm

        def x_tile(k):
            a = (k // 2) * P + (k % 2) * SLOTS
            return XTt[:, a:a + SLOTS]

        def ht_mm(pe):
            for j in range(4):
                mm = pe.transpose(BH[:, j * SLOTS:(j + 1) * SLOTS], HH[0:SLOTS, j:512:4], ident[0:SLOTS, 0:SLOTS])
            return mm

        def down_mm(pe, w):
            for j in range(4):
                for half in range(2):
                    mm = pe.matmul(BY[64 * half:64 * half + 64, :], HHT[:, j * SLOTS:(j + 1) * SLOTS], w[:, j, half * 512:(half + 1) * 512],
                                   start=(j == 0), stop=(j == 3))
            return mm

        def w_need(l, u, j, i):
            c = c_moe[l] + 3 * u + j
            return w_landed[c % RING], landed(c) + 16 * i

        def experts_pe(pe, l):
            ms = lambda n: moe_sem(l, n)
            mw = lambda n, v: moe_wait(l, n, v)

            def expert(i, u, last=False):
                e = 2 * i + u
                for j in range(2):
                    pe.wait_ge(*w_need(l, u, j, i))
                pe.wait_ge(*mw("xt_out", e + 1))
                wg, wu, wd = (slot_of(c_moe[l] + 3 * u + j).rearrange("p (k n) -> p k n", k=k) for j, k in ((0, KT), (1, KT), (2, 4)))
                for k in range(KT):
                    pe.matmul(BGU[0:SLOTS, :], x_tile(k), wg[:, k, :], start=(k == 0), stop=(k == KT - 1))
                    mm = pe.matmul(BGU[SLOTS:2 * SLOTS, :], x_tile(k), wu[:, k, :], start=(k == 0), stop=(k == KT - 1))
                mm.then_inc(ms("gu"), 1)
                if not last:
                    pe.wait_ge(*mw("oh", e + 2))
                    gather_mm(pe, OH[(u + 1) % 2]).then_inc(ms("gat"), 1)
                pe.wait_ge(*mw("hh", e + 1))
                if not last:
                    pe.wait_ge(*mw("xg", e + 2))
                    xt_mm(pe).then_inc(ms("xt"), 1)
                ht_mm(pe).then_inc(ms("ht"), 1)
                pe.wait_ge(*mw("ht_out", e + 1))
                pe.wait_ge(*w_need(l, u, 2, i))
                if not (isinstance(i, int) and i == 0 and u == 0):
                    pe.wait_ge(*mw("y_out", e))
                down_mm(pe, wd).then_inc(ms("y"), 1)

            pe.wait_ge(*mw("oh", 1))
            gather_mm(pe, OH[0]).then_inc(ms("gat"), 1)
            pe.wait_ge(*mw("xg", 1))
            xt_mm(pe).then_inc(ms("xt"), 1)
            expert(0, 0)
            expert(0, 1)
            with pe.Fori(1, NE // 2 - 1) as i:
                expert(i, 0)
                expert(i, 1)
            expert(NE // 2 - 1, 0)
            expert(NE // 2 - 1, 1, last=True)
            n_most = pe.value_load(cnt[0:1, 0:1], min_val=0, max_val=SEQ)
            with pe.If(n_most > SLOTS):
                with pe.Fori(1, SEQ // SLOTS) as b:
                    with pe.Fori(0, NE) as e:
                        n = (b - 1) * NE + e
                        pe.wait_ge(*over_wait(l, "v_oh", n))
                        gather_mm(pe, OH[0]).then_inc(over_done(l, "v_gat"), 1)
                        pe.wait_ge(*over_wait(l, "v_xg", n))
                        xt_mm(pe).then_inc(over_done(l, "v_xt"), 1)
                        pe.wait_ge(*over_wait(l, "v_xt_out", n))
                        for half, name in enumerate(("v_g", "v_u")):
                            pe.wait_ge(ms("v_w"), 16 * (3 * n + half + 1))
                            w = WOV.rearrange("p (k n) -> p k n", k=KT)
                            for k in range(KT):
                                mm = pe.matmul(BGU[SLOTS * half:SLOTS * half + SLOTS, :], x_tile(k), w[:, k, :], start=(k == 0), stop=(k == KT - 1))
                            mm.then_inc(over_done(l, name), 1)
                        pe.wait_ge(*over_wait(l, "v_hh", n))
                        alone(pe)
                        ht_mm(pe).then_inc(over_done(l, "v_ht"), 1)
                        pe.wait_ge(*over_wait(l, "v_ht_out", n))
                        pe.wait_ge(ms("v_w"), 16 * (3 * n + 3))
                        down_mm(pe, WOV.rearrange("p (k n) -> p k n", k=4)).then_inc(over_done(l, "v_y"), 1)
                        pe.wait_ge(*over_wait(l, "v_ohg", n))
                        alone(pe)
                        for t in range(NT):
                            mm = pe.transpose(PB[4][:, t * P:(t + 1) * P], OHG[:, t * P:(t + 1) * P], ident)
                        mm.then_inc(over_done(l, "v_ot"), 1)
                        pe.wait_ge(*over_wait(l, "v_y_out", n))
                        alone(pe)
                        for m in range(2 * NT):
                            t, r = m // 2, slice(64 * (m % 2), 64 * (m % 2) + 64)
                            mm = pe.matmul(PB[m][:, :], OT[r, t * P:(t + 1) * P], YS[0][r, :], start=True, stop=True)
                        mm.then_inc(over_done(l, "v_comb"), 1)
                        pe.wait_ge(*over_wait(l, "v_added", n))
                        alone(pe)

        def experts_act(act, l, step):
            ms = lambda n: moe_sem(l, n)
            mw = lambda n, v: moe_wait(l, n, v)

            def store(e, u, b, s):
                for half in range(2):
                    act.dma_start(y_view[bass.ds(e, 1) if not isinstance(e, int) else slice(e, e + 1), b:b + SLOTS, half, :],
                                  YS[u][64 * half:64 * half + 64, :]).then_inc(s, 16)

            def expert(i, u, last=False):
                e = 2 * i + u
                act.wait_ge(*mw("gu", e + 1))
                act.activation(SIL[0:SLOTS, :], BGU[0:SLOTS, :], ACT.Silu).then_inc(ms("sil"), 1)
                if not last:
                    act.wait_ge(*mw("gat", e + 2))
                    act.copy(XG, BX[:, :]).then_inc(ms("xg"), 1)
                act.wait_ge(*mw("ht", e + 1))
                act.copy(HHT, BH[:, 0:4 * SLOTS]).then_inc(ms("ht_out"), 1)
                act.wait_ge(*mw("y_out", e + 1))
                store(e, u, 0, ms(f"stored{u}"))

            act.wait_ge(*mw("gat", 1))
            act.copy(XG, BX[:, :]).then_inc(ms("xg"), 1)
            expert(0, 0)
            expert(0, 1)
            with act.Fori(1, NE // 2 - 1) as i:
                expert(i, 0)
                expert(i, 1)
            expert(NE // 2 - 1, 0)
            expert(NE // 2 - 1, 1, last=True)
            n_most = act.value_load(cnt[0:1, 0:1], min_val=0, max_val=SEQ)
            with act.If(n_most > SLOTS):
                with act.Fori(1, SEQ // SLOTS) as b:
                    with act.Fori(0, NE) as e:
                        n = (b - 1) * NE + e
                        act.wait_ge(*over_wait(l, "v_gat", n))
                        act.copy(XG, BX[:, :]).then_inc(over_done(l, "v_xg"), 1)
                        act.wait_ge(*over_wait(l, "v_g", n))
                        act.wait_ge(*over_wait(l, "v_u", n))
                        act.activation(SIL[0:SLOTS, :], BGU[0:SLOTS, :], ACT.Silu).then_inc(over_done(l, "v_sil"), 1)
                        act.wait_ge(*over_wait(l, "v_ht", n))
                        act.copy(HHT, BH[:, 0:4 * SLOTS]).then_inc(over_done(l, "v_ht_out"), 1)

        def experts_dve(dve, l, step):
            ms = lambda n: moe_sem(l, n)
            mw = lambda n, v: moe_wait(l, n, v)

            def one_hots(e, buf):
                col = POSM[:, :, bass.ds(e, 1) if not isinstance(e, int) else slice(e, e + 1)]
                dve.tensor_tensor(OH[buf], const("slot")[:, None, :].to_broadcast([P, NT, SLOTS]), col.to_broadcast([P, NT, SLOTS]),
                                  ALU.is_equal).then_inc(ms("oh"), 1)

            def x_out(e):
                dve.wait_ge(*mw("xt", e + 1))
                dve.tensor_copy(XTt, BXT[:, :]).then_inc(ms("xt_out"), 1)

            def expert(i, u, last=False):
                e = 2 * i + u
                dve.wait_ge(*mw("sil", e + 1))
                dve.tensor_tensor(HH[0:SLOTS, :], SIL[0:SLOTS, :], BGU[SLOTS:2 * SLOTS, :], ALU.mult).then_inc(ms("hh"), 1)
                if not last:
                    x_out(e + 1)
                dve.wait_ge(*mw("y", e + 1))
                if not (isinstance(i, int) and i == 0):
                    dve.wait_ge(*mw(f"stored{u}", 32 * i))
                dve.tensor_copy(YS[u], BY[:, :]).then_inc(ms("y_out"), 1)

            def ahead(e, u):
                dve.wait_ge(*mw("gat", e + 1))
                one_hots(e + 2, u)

            one_hots(0, 0)
            one_hots(1, 1)
            gates_dve(dve, l, step)
            x_out(0)
            ahead(0, 0)
            expert(0, 0)
            ahead(1, 1)
            expert(0, 1)
            with dve.Fori(1, NE // 2 - 1) as i:
                for u in range(2):
                    ahead(2 * i + u, u)
                    expert(i, u)
            expert(NE // 2 - 1, 0)
            expert(NE // 2 - 1, 1, last=True)
            n_most = dve.value_load(cnt[0:1, 0:1], min_val=0, max_val=SEQ)
            with dve.If(n_most > SLOTS):
                for u in range(2):
                    dve.wait_ge(*mw(f"stored{u}", 32 * (NE // 2)))
                for M, gate in ((M1, gate1), (M2, gate2)):
                    dve.tensor_tensor(M, M, gate[:, :, None].to_broadcast([P, NT, NE]), ALU.mult).then_inc(ms("v_gates"), 1)
                dve.wait_ge(ms("v_gates"), 2)
                dve.tensor_tensor(M1, M1, M2, ALU.add).then_inc(ms("v_gates"), 1)
                dve.wait_ge(ms("v_gates"), 3)
                with dve.Fori(1, SEQ // SLOTS) as b:
                    dve.tensor_scalar(POSM, POSM, -float(SLOTS), None, ALU.add).then_inc(ms("v_pos"), 1)
                    dve.wait_ge(ms("v_pos"), b)
                    alone(dve)
                    with dve.Fori(0, NE) as e:
                        n = (b - 1) * NE + e
                        dve.tensor_tensor(OH[0], const("slot")[:, None, :].to_broadcast([P, NT, SLOTS]),
                                          POSM[:, :, bass.ds(e, 1)].to_broadcast([P, NT, SLOTS]), ALU.is_equal).then_inc(over_done(l, "v_oh"), 1)
                        dve.wait_ge(*over_wait(l, "v_oh", n))
                        dve.tensor_tensor(OHG.rearrange("p (t a s) -> p t a s", t=NT, a=2), OH[0][:, :, None, :].to_broadcast([P, NT, 2, SLOTS]),
                                          M1[:, :, bass.ds(e, 1), None].to_broadcast([P, NT, 2, SLOTS]), ALU.mult).then_inc(over_done(l, "v_ohg"), 1)
                        dve.wait_ge(*over_wait(l, "v_xt", n))
                        dve.tensor_copy(XTt, BXT[:, :]).then_inc(over_done(l, "v_xt_out"), 1)
                        dve.wait_ge(*over_wait(l, "v_sil", n))
                        dve.tensor_tensor(HH[0:SLOTS, :], SIL[0:SLOTS, :], BGU[SLOTS:2 * SLOTS, :], ALU.mult).then_inc(over_done(l, "v_hh"), 1)
                        dve.wait_ge(*over_wait(l, "v_ot", n))
                        dve.tensor_copy(OT, PB[4][:, :])
                        dve.wait_ge(*over_wait(l, "v_y", n))
                        dve.tensor_copy(YS[0], BY[:, :]).then_inc(over_done(l, "v_y_out"), 1)
                        dve.wait_ge(*over_wait(l, "v_comb", n))
                        for m in range(2 * NT):
                            xs = X[:, m // 2, (m % 2) * 512:(m % 2) * 512 + 512]
                            dve.tensor_tensor(xs, xs, PB[m][:, :], ALU.add).then_inc(ms("v_add") if m < 2 * NT - 1 else over_done(l, "v_added"), 1)
                        dve.wait_ge(*over_wait(l, "v_added", n))
                        alone(dve)
            for u in range(2):
                dve.wait_ge(*mw(f"stored{u}", 32 * (NE // 2)))
            dve.tensor_copy(cnt_f, cnt_f).then_inc(ms("rows_stored"), 1)
            base = (R_EVEN, R_ODD)[l]
            for n in range(2 * NT):
                t, k = n // 2, n % 2
                dve.wait_ge(sg(f"fetched{n % 4}"), 16 * (2 * l + n // 4 + 1))
                if k:
                    dve.wait_ge(*mw("first_added", t + 1))
                ins = dve.scalar_tensor_tensor(X[:, t, :], ROWS[:, n % 4, :], (used1, used2)[k][:, t:t + 1], X[:, t, :], ALU.mult, ALU.add)
                ins.then_inc(resid if k else ms("first_added"), 1)
                if k and l == 0:
                    norm_dve(dve, 2, t - 1)
            if l == 0:
                norm_dve(dve, 2, NT - 1)

        def experts_sp(sp, l):
            ms = lambda n: moe_sem(l, n)
            mw = lambda n, v: moe_wait(l, n, v)
            mats = (w_gate[l], w_up[l], w_down[l])

            def load(i, u, j):
                e = 2 * i + u
                c = c_moe[l] + 3 * u + j
                if isinstance(i, int) and i == 0:
                    sp.wait_ge(*released[c - RING])
                else:
                    sp.wait_ge(*mw("gu" if j < 2 else "y", e - 1))
                src = mats[j].rearrange("e (p k) n -> p e (k n)", p=P)[:, bass.ds(e, 1) if not isinstance(e, int) else slice(e, e + 1), :]
                sp.dma_start(slot_of(c), src.rearrange("p e n -> p (e n)"), max_dma_last_dim=4096).then_inc(w_landed[c % RING], 16)

            for u in range(2):
                for j in range(3):
                    load(0, u, j)
            with sp.Fori(1, NE // 2) as i:
                for u in range(2):
                    for j in range(3):
                        load(i, u, j)

        def overflow_sp(sp, l):
            ms = lambda n: moe_sem(l, n)
            mw = lambda n, v: moe_wait(l, n, v)
            sp.wait_ge(*mw("routed", 1))
            n_most = sp.value_load(cnt[0:1, 0:1], min_val=0, max_val=SEQ)
            with sp.If(n_most > SLOTS):
                with sp.Fori(1, SEQ // SLOTS) as b:
                    with sp.Fori(0, NE) as e:
                        n = (b - 1) * NE + e
                        for j, name in enumerate(("v_g", "v_u", "v_y")):
                            src = (w_gate[l], w_up[l], w_down[l])[j].rearrange("e (p k) n -> p e (k n)", p=P)[:, bass.ds(e, 1), :]
                            sp.dma_start(WOV, src.rearrange("p e n -> p (e n)"), max_dma_last_dim=4096).then_inc(ms("v_w"), 16)
                            sp.wait_ge(*over_wait(l, name, n))
                        alone(sp)

        def combine_pool(pool, l, step):
            ms = lambda n: moe_sem(l, n)
            mw = lambda n, v: moe_wait(l, n, v)
            base = (R_EVEN, R_ODD)[l]
            pool.wait_ge(*mw("rows_stored", 1))
            for n in range(2 * NT):
                t, k = n // 2, n % 2
                if n >= 4:
                    pool.wait_ge(*((resid, base + t - 1) if k else mw("first_added", t - 1)))
                pool.indirect_dma_start(ROWS[:, n % 4, :], None, y_rows, bass.IndirectOffsetOnAxis(ap=dest[:, k * NT + t:k * NT + t + 1], axis=0))\
                    .then_inc(sg(f"fetched{n % 4}"), 16)
                if l == 0 and upto > 2 and k and t >= 2:
                    norm_pool(pool, 2, step, [t - 2])

        def const_odd_(name):
            a, b = co[name]
            return SCR[:, CO_AT + a:CO_AT + b]

        s_.n = 0
        two = lambda a: a.rearrange("p (m n) -> p m n", m=2)
        QR, KR, QX, Sr = (two(s_(1024)) for _ in range(4))
        ATr = t4(s_(512))
        KZ = s_(3 * 256).rearrange("p (t m n) -> p t m n", t=3, m=2)
        rtmp = [s_(512) for _ in range(4)]
        YTr = s_(2048).rearrange("p (j n) -> p j n", j=4)
        r_ss, r_rs = s_(NT), s_(NT)
        rjunk = s_(512)
        VO = XN[:, 0:2, :].rearrange("p a (b n) -> p (a b) n", b=2)
        ZS = XN[:, 2:4, :].rearrange("p a (b n) -> p (a b) n", b=2)

        def ret_qk_pe(pe, h):
            c = c_ret + 4 * h
            pe.wait_ge(w_landed[c % RING], landed(c))
            w = slot_of(c).rearrange("p (k s n) -> p k s n", k=KT, s=2)
            if h:
                pe.wait_ge(sg("r_o_out"), NT * h)
                pe.wait_ge(sg("r_S"), 6 * h)
            for s in range(2):
                for par in range(2):
                    for k in range(KT):
                        mm = pe.matmul(PB[2 * s + par][:, :], w[:, k, s, par:RQ:2], HT[:, k, :], start=(k == 0), stop=(k == KT - 1))
                mm.then_inc(sg("r_qk"), 1)

        def ret_pe(pe):
            ret_qk_pe(pe, 0)
            for h in range(RH):
                c = c_ret + 4 * h
                c += 1
                pe.wait_ge(w_landed[c % RING], landed(c))
                w = slot_of(c).rearrange("p (k n) -> p k n", k=KT)
                for t in range(NT):
                    if t >= 2:
                        pe.wait_ge(sg("r_v_out"), NT * h + t - 1)
                    elif h:
                        pe.wait_ge(resid, R_MOE0 + 8 * h - 1 + t)
                    for k in range(KT):
                        mm = pe.matmul(PB[4 + t % 2][:, :], HT[:, k, t * P:(t + 1) * P], w[:, k, :], start=(k == 0), stop=(k == KT - 1))
                    mm.then_inc(sg("r_v"), 1)
                pe.wait_ge(sg("r_rot"), 2 * h + 2)
                for t in range(NT):
                    for m in range(2):
                        mm = pe.matmul(PB[0][:, t * P:(t + 1) * P], KR[:, m, t * P:(t + 1) * P], QR[:, m, t * P:(t + 1) * P], start=(m == 0), stop=(m == 1))
                mm.then_inc(sg("r_in"), 1)
                for t in range(NT - 1):
                    for m in range(2):
                        mm = pe.transpose(PB[6 + t // 2][:, (2 * (t % 2) + m) * P:(2 * (t % 2) + m + 1) * P], KR[:, m, t * P:(t + 1) * P], ident)
                mm.then_inc(sg("r_kt"), 1)
                c += 1
                pe.wait_ge(w_landed[c % RING], landed(c))
                w = slot_of(c).rearrange("p (k n) -> p k n", k=KT)
                for t in range(NT):
                    if t < 2:
                        pe.wait_ge(sg("r_v_out"), NT * h + t + 3)
                    else:
                        pe.wait_ge(sg("r_zs"), NT * h + t - 1)
                    for k in range(KT):
                        mm = pe.matmul(PB[4 + t % 2][:, :], HT[:, k, t * P:(t + 1) * P], w[:, k, :], start=(k == 0), stop=(k == KT - 1))
                    mm.then_inc(sg("r_z"), 1)
                pe.wait_ge(sg("r_at"), h + 1)
                pe.wait_ge(sg("r_kz"), h + 1)
                for t in range(NT):
                    b = PB[1 + t % 2]
                    if t >= 2:
                        pe.wait_ge(sg("r_o_out"), NT * h + t - 1)
                    mm = pe.matmul(b[:, :], ATr[:, t, :], VO[:, t, :], start=True, stop=(t == 0))
                    if t:
                        pe.wait_ge(sg("r_S"), 6 * h + 2 * t)
                        for m in range(2):
                            mm = pe.matmul(b[:, :], QX[:, m, t * P:(t + 1) * P], Sr[:, m, :], start=False, stop=(m == 1))
                    mm.then_inc(sg("r_o"), 1)
                    if t < NT - 1:
                        for m in range(2):
                            pe.matmul(PB[(3, 7)[m]][:, :], KZ[:, t, m, :], VO[:, t, :], start=True, stop=True).then_inc(sg("r_su"), 1)
                if h < RH - 1:
                    ret_qk_pe(pe, h + 1)
                pe.wait_ge(sg("r_y"), NT * (h + 1))
                pe.wait_ge(sg("r_S"), 6 * (h + 1))
                for t in range(NT):
                    if t >= 2:
                        pe.wait_ge(sg("r_yt"), NT * h + t - 1)
                    for j in range(4):
                        mm = pe.transpose(PB[6 + t % 2][:, j * P:(j + 1) * P], VO[:, t, j:512:4], ident)
                    mm.then_inc(sg("r_tr"), 1)
                c += 1
                pe.wait_ge(w_landed[c % RING], landed(c))
                w = slot_of(c).rearrange("p (k n) -> p k n", k=4)
                pe.wait_ge(sg("r_zs"), NT * (h + 1))
                for n in range(8):
                    t, half = n // 2, n % 2
                    pe.wait_ge(sg("r_yt"), NT * h + t + 1)
                    if n >= 2:
                        pe.wait_ge(resid, R_MOE0 + 8 * h + n - 1)
                    for j in range(4):
                        mm = pe.matmul(PB[4 + n % 2][:, :], YTr[:, j, t * P:(t + 1) * P], w[:, j, half * 512:(half + 1) * 512], start=(j == 0), stop=(j == 3))
                    mm.then_inc(sg("r_out"), 1)

        def ret_act(act, step):
            act.wait_ge(odd_in, 16)
            for h in range(RH):
                for t in range(NT):
                    act.wait_ge(sg("r_v"), NT * h + t + 1)
                    act.copy(VO[:, t, :], PB[4 + t % 2][:, :]).then_inc(sg("r_v_out"), 1)
                act.wait_ge(sg("r_kt"), h + 1)
                for t in range(NT - 1):
                    ins = act.activation(KZ[:, t, :, :], PB[6 + t // 2][:, (t % 2) * 256:(t % 2) * 256 + 256].rearrange("p (m n) -> p m n", m=2), ACT.Copy,
                                         scale=const_odd_("zeta")[:, h:h + 1])
                    if t == NT - 2:
                        ins.then_inc(sg("r_kz"), 1)
                for t in range(NT):
                    act.wait_ge(sg("r_z"), NT * h + t + 1)
                    act.activation(ZS[:, t, :], PB[4 + t % 2][:, :], ACT.Silu).then_inc(sg("r_zs"), 1)
                for t in range(NT):
                    act.wait_ge(sg("r_o"), NT * h + t + 1)
                    step.then(act.activation(rjunk, PB[1 + t % 2][:, :], ACT.Square, accum_out=r_ss[:, t:t + 1]))
                    if t < NT - 1:
                        act.wait_ge(sg("r_su"), 6 * h + 2 * t + 2)
                    act.copy(VO[:, t, :], PB[1 + t % 2][:, :]).then_inc(sg("r_o_out"), 1)
                for t in range(NT):
                    act.wait_ge(sg("r_tr"), NT * h + t + 1)
                    act.copy(YTr[:, :, t * P:(t + 1) * P], PB[6 + t % 2][:, :].rearrange("p (j q) -> p j q", j=4)).then_inc(sg("r_yt"), 1)

        def ret_pool(pool, step):
            for h in range(RH):
                pool.wait_ge(sg("r_o_out"), NT * (h + 1))
                step.then(pool.tensor_scalar(r_rs, r_ss, 1.0 / RV, EPS, ALU.mult, ALU.add))
                pool.tensor_tensor(r_rs, r_rs, mhalf[:, 0:NT], ALU.pow).then_inc(sg("r_rstd"), 1)

        def ret_dve(dve, step):
            dve.wait_ge(odd_in, 16)
            cs, sn = const_odd_("xcos"), const_odd_("xsin")

            def rotate(h):
                for s, R in enumerate((QR, KR)):
                    dve.wait_ge(sg("r_qk"), 2 * h + s + 1)
                    e_, o_ = PB[2 * s][:, :], PB[2 * s + 1][:, :]
                    step(dve.tensor_tensor(rtmp[0], e_, cs, ALU.mult))
                    step(dve.tensor_tensor(rtmp[1], o_, sn, ALU.mult))
                    step(dve.tensor_tensor(rtmp[2], o_, cs, ALU.mult))
                    step(dve.tensor_tensor(rtmp[3], e_, sn, ALU.mult))
                    step.wait()
                    step(dve.tensor_tensor(R[:, 0, :], rtmp[0], rtmp[1], ALU.subtract))
                    dve.tensor_tensor(R[:, 1, :], rtmp[2], rtmp[3], ALU.add).then_inc(sg("r_rot"), 1)
                    step.wait()
                    dve.wait_ge(sg("r_rot"), 2 * h + s + 1)

            rotate(0)
            for h in range(RH):
                for m in range(2):
                    step(dve.tensor_tensor(t4(QX[:, m, :]), t4(QR[:, m, :]), const_odd_(f"xi{h}")[:, None, :].to_broadcast([P, NT, P]), ALU.mult))
                dve.wait_ge(sg("r_in"), h + 1)
                step.wait()
                dve.tensor_tensor(ATr, t4(PB[0][:, :]), const_odd_(f"decay{h}")[:, None, :].to_broadcast([P, NT, P]), ALU.mult).then_inc(sg("r_at"), 1)
                for t in range(NT - 1):
                    for m in range(2):
                        dve.wait_ge(sg("r_su"), 6 * h + 2 * t + m + 1)
                        b = PB[(3, 7)[m]][:, :]
                        if t:
                            dve.wait_ge(sg("r_S"), 6 * h + 2 * (t - 1) + m + 1)
                            dve.wait_ge(sg("r_o"), NT * h + t + 1)
                            ins = dve.scalar_tensor_tensor(Sr[:, m, :], Sr[:, m, :], gamma[h], b, ALU.mult, ALU.add)
                        else:
                            ins = dve.tensor_copy(Sr[:, m, :], b)
                        ins.then_inc(sg("r_S"), 1)
                dve.wait_ge(sg("r_rstd"), h + 1)
                dve.wait_ge(sg("r_zs"), NT * (h + 1))
                for t in range(NT):
                    dve.scalar_tensor_tensor(VO[:, t, :], VO[:, t, :], r_rs[:, t:t + 1], ZS[:, t, :], ALU.mult, ALU.mult).then_inc(sg("r_y"), 1)
                if h < RH - 1:
                    dve.wait_ge(sg("r_o"), NT * (h + 1))
                    rotate(h + 1)
                for n in range(8):
                    t, half = n // 2, n % 2
                    dve.wait_ge(sg("r_out"), 8 * h + n + 1)
                    xs = X[:, t, half * 512:(half + 1) * 512]
                    dve.wait_ge(resid, R_MOE0 + 8 * h)
                    dve.tensor_tensor(xs, xs, PB[4 + n % 2][:, :], ALU.add).then_inc(resid, 1)
                    if half and h == RH - 1:
                        norm_dve(dve, 3, t - 1)
            norm_dve(dve, 3, NT - 1)

        released = {c_kv: (sg("a_proj"), 4), c_q: (sg("a_proj"), 8)}
        for h in range(GH):
            released[c_gdn + h] = (sg("d_z"), h + 1)
        for g in range(2):
            released[c_oute + g] = (sg("m_out"), 8)
        for l in range(2):
            for e in range(NE):
                released[c_moe[l] + 3 * e] = released[c_moe[l] + 3 * e + 1] = moe_wait(l, "gu", e + 1)
                released[c_moe[l] + 3 * e + 2] = moe_wait(l, "y", e + 1)
        for h in range(RH):
            for j, s in enumerate((("r_qk", 2 * h + 2), ("r_v", NT * (h + 1)), ("r_z", NT * (h + 1)), ("r_out", 8 * (h + 1)))):
                released[c_ret + 4 * h + j] = (sg(s[0]), s[1])

        stored = sem("stored")
        R_END = (0, R_EVEN, R_MOE0, R_ODD, R_MOE1)[upto]
        block = ctx.enter_context(nc.Block())

        @block.sync
        def _(sp):
            sp.dma_start(X[:, :, :], x[0].rearrange("(t p) d -> p t d", p=P)).then_inc(x_in, 16)
            sp.dma_start(CE[:, :], const_even).then_inc(consts_in, 16)

            def load(c):
                if c in (c_oute, c_oute + 1):
                    sp.wait_ge(sg("d_kv"), GH)
                    sp.wait_ge(sg("d_qd"), GH)
                elif c >= RING:
                    sp.wait_ge(*released[c - RING])
                for dst, src in chunks[c]:
                    sp.dma_start(dst(slot_of(c)), src).then_inc(w_landed[c % RING], 16)

            for c in range(c_moe[0]):
                load(c)
            if upto > 1:
                experts_sp(sp, 0)
                overflow_sp(sp, 0)
            if upto > 2:
                for c in range(c_ret, c_moe[1]):
                    if c == c_ret + 1:
                        sp.wait_ge(sg("fetched3"), 32)
                    load(c)
            if upto > 3:
                experts_sp(sp, 1)
                overflow_sp(sp, 1)
            for t in range(NT):
                sp.wait_ge(resid, R_END - NT + t + 1 if upto == 4 else R_END)
                sp.dma_start(out[0].rearrange("(t p) d -> p t d", p=P)[:, t, :], X[:, t, :]).then_inc(stored, 16)
            sp.wait_ge(stored, 16 * NT)

        @block.gpsimd
        def _(pool):
            step = Steps(pool, pool_step)
            pool.memset(mhalf[:, :], -0.5).then_inc(mhalf_set, 1)
            gain_pool(pool, 0)
            for dst, src in ((qk_gain[:, 0:512].rearrange("p (h d) -> p h d", h=AH), q_gain_even[0:1, None, :].to_broadcast([P, AH, ADH])),
                             (qk_gain[:, 512:640].rearrange("p (h d) -> p h d", h=AKV), k_gain_even[0:1, None, :].to_broadcast([P, AKV, ADH])),
                             (sink_b, sinks_even[0:1, :].to_broadcast([P, AH])),
                             (alog_b, a_log_even[0:1, :].to_broadcast([P, GH])),
                             (dtb_b, dt_bias_even[0:1, :].to_broadcast([P, GH])),
                             (gdn_gain, gdn_gain_even[0:1, :].to_broadcast([P, GD]))):
                pool.dma_start(dst, src).then_inc(params_in, 16)
            pool.dma_start(cwr[0:48, :], conv_w_even[0].rearrange("i (c n) -> (i c) n", n=P)).then_inc(params_in, 16)
            pool.wait_ge(mhalf_set, 1)
            if upto > 1:
                route_pool(pool, 0)
            norm_pool(pool, 0, step)
            if upto > 1:
                gain_pool(pool, 1)
            attn_pool(pool, step)
            gdn_pool(pool, step)
            if upto > 1:
                norm_pool(pool, 1, step)
                pool.wait_ge(resid, R_EVEN)
                pool.dma_start(SCR[:, CO_AT:SCR_N], const_odd).then_inc(odd_in, 16)
                if upto > 2:
                    gain_pool(pool, 2)
                combine_pool(pool, 0, step)
            if upto > 2:
                if upto > 3:
                    route_pool(pool, 1)
                norm_pool(pool, 2, step, range(2, NT))
                if upto > 3:
                    gain_pool(pool, 3)
                ret_pool(pool, step)
            if upto > 3:
                norm_pool(pool, 3, step)
                combine_pool(pool, 1, step)

        @block.scalar
        def _(act):
            step = Steps(act, act_step)
            norm_act(act, 0)
            norm_act_out(act, 0)
            attn_act(act, step)
            gdn_act(act, step)
            oute_act(act)
            for l in range(2):
                if upto > 2 * l + 1:
                    norm_act(act, 2 * l + 1)
                    norm_act_out(act, 2 * l + 1)
                    route_act(act, l)
                    experts_act(act, l, step)
                if l == 0 and upto > 2:
                    norm_act(act, 2)
                    norm_act_out(act, 2)
                    ret_act(act, step)

        @block.vector
        def _(dve):
            step = Steps(dve, dve_step)
            for t in range(NT):
                norm_dve(dve, 0, t)
            norm_dve_out(dve, 0)
            attn_dve(dve, step)
            gdn_dve(dve, step)
            oute_dve(dve)
            for l in range(2):
                if upto > 2 * l + 1:
                    norm_dve_out(dve, 2 * l + 1)
                    route_dve(dve, l, step)
                    experts_dve(dve, l, step)
                if l == 0 and upto > 2:
                    norm_dve_out(dve, 2)
                    ret_dve(dve, step)

        @block.tensor
        def _(pe):
            norm_pe(pe, 0)
            attn_pe(pe)
            gdn_pe(pe)
            oute_pe(pe)
            for l in range(2):
                if upto > 2 * l + 1:
                    norm_pe(pe, 2 * l + 1, lambda t, l=l: logits_pe(pe, l, t))
                    route_pe(pe, l)
                    experts_pe(pe, l)
                if l == 0 and upto > 2:
                    norm_pe(pe, 2)
                    ret_pe(pe)


_INS = ['x', 'ln_mix_even', 'w_in_even', 'conv_w_even', 'a_log_even', 'dt_bias_even', 'q_gain_even', 'k_gain_even',
        'sinks_even', 'gdn_gain_even', 'w_out_even', 'ln_mix_odd', 'w_in_odd', 'w_out_odd', 'ln_ffn',
        'w_router_group', 'b_router_group', 'w_router_expert', 'b_router_expert', 'w_gate', 'w_up', 'w_down']


def packed(tables):
    return np.ascontiguousarray(np.concatenate([np.asarray(a, np.float32) for a in tables.values()], axis=1))


def kernel(**inputs):
    import concourse.bacc as bacc
    from concourse.bass_utils import run_bass_kernel_spmd

    nc = bacc.Bacc("TRN2", target_bir_lowering=False, num_devices=1)
    arrays, args = {}, []
    tab_even, tab_odd, _ = constants()
    for name, a in [(n, inputs[n]) for n in _INS] + [("const_even", packed(tab_even)), ("const_odd", packed(tab_odd))]:
        a = np.ascontiguousarray(a)
        arrays[f"in_{name}_dram"] = a
        args.append(nc.dram_tensor(f"in_{name}_dram", a.shape, mybir.dt.from_np(a.dtype), kind="ExternalInput").ap())
    args.append(nc.dram_tensor("out_0_dram", (1, SEQ, D), F32, kind="ExternalOutput").ap())
    program(nc, *args)
    r = run_bass_kernel_spmd(nc, [arrays], core_ids=[0])
    return r.results[0]["out_0_dram"]
```

```python
from contextlib import ExitStack

import numpy as np
import concourse.bass as bass
from concourse import mybir

F32 = mybir.dt.float32
F32R = mybir.dt.float32r
I32 = mybir.dt.int32
ALU = mybir.AluOpType
ACT = mybir.ActivationFunctionType
AX = mybir.AxisListType.X

P = 128
D = 1024
SEQ = 512
NT = SEQ // P
KT = D // P
EPS = 1e-6
BIG = 1e30
RING = 6
SLOT = 4096
AH, AKV, ADH = 8, 2, 64
AQK = AH + AKV
GH, GD, CONV, CH = 4, 128, 4, 64
LEVELS = 6
RH, RQ, RV = 4, 256, 512
NG, EPG, NE, DE = 4, 8, 32, 512
SLOTS = 64
NR = NG + NE


def constants():
    i = np.arange(P)
    same = (i[:, None] // CH) == (i[None, :] // CH)
    even = {
        "ident": np.eye(P),
        "ones": np.ones((P, P)),
        "before": i[:, None] < i[None, :],
        "cum": same & (i[:, None] <= i[None, :]),
        "chunk": same,
        "strict": same & (i[:, None] > i[None, :]),
        "inclT": same & (i[:, None] <= i[None, :]),
    }
    for lv in range(LEVELS):
        b = 1 << lv
        even[f"level{lv}"] = ((i[:, None] // (2 * b)) == (i[None, :] // (2 * b))) & \
            ((i[:, None] // b) % 2 == 1) & ((i[None, :] // b) % 2 == 0)
    q, k = i[:, None], np.arange(2 * P)[None, :] - P
    even["window"] = np.where((q - k >= 0) & (q - k < P), 0.0, -BIG)
    half = ADH // 8
    inv = (np.float32(1.0) / np.float32(500000.0) ** (np.arange(half, dtype=np.float32) * np.float32(2.0) / np.float32(16))).astype(np.float32)
    ang = (np.arange(SEQ, dtype=np.float32)[:, None] * inv[None, :]).astype(np.float32)
    ang = ang.reshape(NT, P, half).transpose(1, 0, 2).reshape(P, NT * half).astype(np.float64)
    even["rcos"], even["rsin"] = np.cos(ang), np.sin(ang)
    even["slot"] = np.broadcast_to(np.arange(SLOTS), (P, SLOTS))
    even["first"] = np.broadcast_to(16 - np.arange(EPG), (P, EPG))
    odd = {}
    freq = (np.float32(1.0) / np.float32(10000.0) ** np.linspace(0.0, 1.0, RQ // 2, dtype=np.float32)).astype(np.float32)
    ang = (np.arange(SEQ, dtype=np.float32)[None, :] * freq[:, None]).astype(np.float32).astype(np.float64)
    odd["xcos"], odd["xsin"] = np.cos(ang), np.sin(ang)
    lg = np.log(1.0 - 2.0 ** (-5.0 - np.arange(RH)))
    kscale = RQ ** -0.5
    for h in range(RH):
        rel = i[None, :] - i[:, None]
        odd[f"decay{h}"] = np.where(rel >= 0, np.exp(np.maximum(rel, 0) * lg[h]), 0.0) * kscale
        odd[f"xi{h}"] = np.broadcast_to(np.exp((i + 1) * lg[h]), (P, P))
    odd["zeta"] = np.exp((P - 1 - i)[:, None] * lg[None, :]) * kscale
    return even, odd, [float(np.exp(P * x)) for x in lg]


def columns(tables):
    at, n = {}, 0
    for name, a in tables.items():
        at[name] = (n, n + a.shape[1])
        n += a.shape[1]
    return at, n


def program(nc, x, ln_mix_even, w_in_even, conv_w_even, a_log_even, dt_bias_even, q_gain_even, k_gain_even,
            sinks_even, gdn_gain_even, w_out_even, ln_mix_odd, w_in_odd, w_out_odd, ln_ffn,
            w_router_group, b_router_group, w_router_expert, b_router_expert, w_gate, w_up, w_down,
            const_even, const_odd, out, upto=4):
    tab_even, tab_odd, gamma = constants()
    ce, n_even = columns(tab_even)
    co, n_odd = columns(tab_odd)
    gains = [ln_mix_even[0:1, :], ln_ffn[0:1, :], ln_mix_odd[0:1, :], ln_ffn[1:2, :]]
    ctx = ExitStack()
    with ctx:
        def sb(name, shape, dt=F32):
            return ctx.enter_context(nc.sbuf_tensor(name, shape, dt))

        def sem(name):
            return ctx.enter_context(nc.semaphore(name))

        def sb_twin(name, shape):
            at = -(-nc.sbuf_base // 32) * 32
            t = sb(name, shape)
            return t, nc.alloc_sbuf_tensor_at(name + "_r", shape, F32R, offset=at)

        ring, ring_r = sb_twin("ring", [P, RING, SLOT])
        X = sb("X", [P, NT, D])
        XN, XN_r = sb_twin("XN", [P, NT, D])
        HT, HT_r = sb_twin("HT", [P, KT, SEQ])
        CE = sb("CE", [P, n_even])
        gainB = sb("gainB", [P, D])
        sumsq = sb("sumsq", [P, NT])
        rstd = sb("rstd", [P, NT])
        mhalf = sb("mhalf", [P, 64])
        WR = sb("WR", [P, KT, NR])
        br = sb("br", [P, NR])
        SCR_N = 12600
        CO_AT = SCR_N - n_odd
        SCR, SCR_r = sb_twin("SCR", [P, SCR_N])
        PARAMS = 16 * 7
        PB = [ctx.enter_context(nc.psum_tensor(f"bank{i}", [P, 512], F32)) for i in range(8)]

        def const(name):
            a, b = ce[name]
            return CE[:, a:b]

        ident, ones = const("ident"), const("ones")

        HTU = ring_r[:, 1, :].rearrange("p (k n) -> p k n", k=KT)
        HTU0 = ring_r[:, 4, :].rearrange("p (k n) -> p k n", k=KT)
        WU0 = ring_r[:, 5, :]
        WU = [ring_r[:, 5, :], ring_r[:, 0, :]]

        def split_mm(pe, out, lhs, rhs, first, last):
            for i, (a, b) in enumerate(((0, 0), (0, 1), (1, 0))):
                mm = pe.matmul(out, lhs[a], rhs[b], start=(first and i == 0), stop=(last and i == 2))
            return mm

        class Carve:
            def __init__(self, tensor, size):
                self.t, self.n, self.size = tensor, 0, size

            def __call__(self, n):
                a = self.n
                self.n += n
                assert self.n <= self.size, (self.n, self.size)
                return self.t[:, a:a + n]

        chunks = []

        def slot_of(c):
            return ring[:, c % RING, :]

        def k_rows(w, a, b):
            return w[:, a:b].rearrange("(p k) n -> p k n", p=P)

        w_e = w_in_even[0]
        c_kv = len(chunks)
        chunks.append([(lambda s: s[:, 0:KT * 264].rearrange("p (k n) -> p k n", k=KT)[:, :, 0:256], k_rows(w_e, 512, 768)),
                       (lambda s: s[:, 0:KT * 264].rearrange("p (k n) -> p k n", k=KT)[:, :, 256:264], k_rows(w_e, 2816, 2824))])
        c_q = len(chunks)
        chunks.append([(lambda s: s.rearrange("p (k n) -> p k n", k=KT), k_rows(w_e, 0, 512))])
        gdn_at = []
        for h in range(GH):
            if h == 2:
                chunks += [[]] * 4
            gdn_at.append(len(chunks))
            src = w_e[:, 768:2816].rearrange("(p k) (s n) -> p k s n", p=P, s=4)[:, :, :, h * GD:(h + 1) * GD]
            chunks.append([(lambda s, i=i: s.rearrange("p (k s n) -> p k s n", k=KT, s=4)[:, :, i, :], src[:, :, i, :]) for i in range(4)])
        chunks += [[]] * 2
        c_oute = len(chunks)
        for g in range(2):
            chunks.append([(lambda s: s.rearrange("p (k n) -> p k n", k=4),
                            w_out_even[0, g * 512:(g + 1) * 512, :].rearrange("(p k) n -> p k n", p=P))])
        c_moe = [len(chunks)]
        for e in range(NE):
            chunks += [[None]] * 3
        w_o = w_in_odd[0]
        odd_w = {}
        for h in range(RH):
            src = w_o[:, 0:2048].rearrange("(p k) (s n) -> p k s n", p=P, s=2)[:, :, :, h * RQ:(h + 1) * RQ]
            odd_w["qk", h] = [(lambda s, i=i: s.rearrange("p (k s n) -> p k s n", k=KT, s=2)[:, :, i, :], src[:, :, i, :]) for i in range(2)]
            for name, base in (("v", 2048), ("z", 4096)):
                odd_w[name, h] = [(lambda s: s.rearrange("p (k n) -> p k n", k=KT), k_rows(w_o, base + h * RV, base + (h + 1) * RV))]
            odd_w["out", h] = [(lambda s: s.rearrange("p (k n) -> p k n", k=4),
                                w_out_odd[0, h * RV:(h + 1) * RV, :].rearrange("(p k) n -> p k n", p=P))]
        odd_order = [("qk", 0)]
        for h in range(RH):
            odd_order += [("v", h), ("z", h)] + ([("qk", h + 1)] if h < RH - 1 else []) + [("out", h)]
        odd_at = {}
        RAW = RING // 2
        for j, name in enumerate(odd_order):
            if j and j % RAW == 0:
                chunks += [[]] * (RING - RAW)
            odd_at[name] = (j, len(chunks))
            chunks.append(odd_w[name])
        c_moe.append(len(chunks))
        for e in range(NE):
            chunks += [[None]] * 3

        def landed(c):
            return 16 * sum(len(chunks[d]) for d in range(c % RING, c + 1, RING))

        w_landed = [sem(f"w_landed{s}") for s in range(RING)]

        x_in, consts_in, params_in, odd_in, gain_in, router_in = (sem(s) for s in (
            "x_in", "consts_in", "params_in", "odd_in", "gain_in", "router_in"))
        mhalf_set = sem("mhalf_set")
        turns = sem("turns")
        resid = sem("resid")
        ss_done, rstd_done, xn_done, tr_done, tr_out_a, tr_out_d = (sem(s) for s in (
            "ss_done", "rstd_done", "xn_done", "tr_done", "tr_out_a", "tr_out_d"))
        act_step, dve_step, pool_step = sem("act_step"), sem("dve_step"), sem("pool_step")
        S = {}

        def sg(name):
            if name not in S:
                S[name] = sem(name)
            return S[name]

        class Steps:
            def __init__(self, eng, s):
                self.eng, self.sem, self.n = eng, s, 0

            def __call__(self, ins):
                ins.then_inc(self.sem, 1)
                self.n += 1

            def wait(self):
                self.eng.wait_ge(self.sem, self.n)

            def then(self, ins):
                self(ins)
                self.wait()

        def alone(eng):
            eng.sem_inc(turns, 1)

        R_EVEN, R_MOE0, R_ODD, R_MOE1 = 8, 12, 12 + 32, 12 + 32 + 4

        TR_OUT = (0, 8, 12, 20, 24)

        def x_wait(eng, ph, t):
            if ph == 0:
                eng.wait_ge(x_in if t < 2 else sg("x_in_late"), 16)
            else:
                eng.wait_ge(resid, [0, 2 * (t + 1), R_EVEN + t + 1, R_ODD - 8 + 2 * (t + 1)][ph])

        def norm_act(act, ph):
            if ph == 1:
                act.wait_ge(sg("m_tr"), 8)
            if ph == 3:
                act.wait_ge(sg("r_tr"), NT * RH)
            for t in range(NT):
                x_wait(act, ph, t)
                act.activation(XN[:, t, :], X[:, t, :], ACT.Square, accum_out=sumsq[:, t:t + 1]).then_inc(ss_done, 1)

        def norm_act_out(act, ph, after=lambda n: None):
            if ph in (0, 2):
                if ph:
                    act.wait_ge(*moe_wait(0, "gu", NE))
                for n in range(8):
                    t, kk = n // 2, n % 2
                    act.wait_ge(tr_done, 8 * ph + n + 1)
                    act.copy((HTU if ph else HTU0)[:, 4 * kk:4 * kk + 4, t * P:(t + 1) * P], PB[n % 4][:, :].rearrange("p (k q) -> p k q", k=4)).then_inc(tr_out_a, 1)
                    after(n)
                return
            for n in range(0, 8, 2):
                t, kk = n // 2, n % 2
                act.wait_ge(tr_done, 8 * ph + n + 1)
                act.copy(HT[:, 4 * kk:4 * kk + 4, t * P:(t + 1) * P], PB[n % 4][:, :].rearrange("p (k q) -> p k q", k=4)).then_inc(tr_out_a, 1)

        def norm_pool(pool, ph, step, tiles=range(NT)):
            for t in tiles:
                if ph and t == 0:
                    pool.wait_ge(xn_done, NT * ph)
                pool.wait_ge(ss_done, NT * ph + t + 1)
                step.then(pool.tensor_scalar(rstd[:, t:t + 1], sumsq[:, t:t + 1], 1.0 / D, EPS, ALU.mult, ALU.add))
                pool.tensor_tensor(rstd[:, t:t + 1], rstd[:, t:t + 1], mhalf[:, 0:1], ALU.pow).then_inc(rstd_done, 1)

        def gain_pool(pool, ph):
            if ph:
                pool.wait_ge(xn_done, NT * ph)
            pool.dma_start(gainB[:, :], gains[ph].to_broadcast([P, D])).then_inc(gain_in, 16)

        def norm_dve(dve, ph, t):
            if t < 0 or ph >= upto:
                return
            dve.wait_ge(rstd_done, NT * ph + t + 1)
            dve.wait_ge(gain_in, 16 * (ph + 1))
            x_wait(dve, ph, t)
            dve.scalar_tensor_tensor(XN[:, t, :].rearrange("p (a c) -> p c a", a=2), X[:, t, :].rearrange("p (c a) -> p c a", a=2),
                                     rstd[:, t:t + 1], gainB[:, :].rearrange("p (c a) -> p c a", a=2),
                                     ALU.mult, ALU.mult).then_inc(xn_done, 1)

        def norm_dve_out(dve, ph):
            if ph in (0, 2):
                for n in range(8):
                    t, kk = n // 2, n % 2
                    dve.wait_ge(tr_out_a, TR_OUT[ph] + n + 1)
                    at = (slice(None), slice(4 * kk, 4 * kk + 4), slice(t * P, (t + 1) * P))
                    dve.tensor_tensor(HT_r[at], PB[n % 4][:, :].rearrange("p (k q) -> p k q", k=4), (HTU if ph else HTU0)[at].bitcast(F32), ALU.subtract).then_inc(tr_out_d, 1)
                return
            for n in range(1, 8, 2):
                t, kk = n // 2, n % 2
                dve.wait_ge(tr_done, 8 * ph + n + 1)
                dve.tensor_copy(HT[:, 4 * kk:4 * kk + 4, t * P:(t + 1) * P], PB[n % 4][:, :].rearrange("p (k q) -> p k q", k=4)).then_inc(tr_out_d, 1)

        def norm_pe(pe, ph, between=None):
            if ph == 0:
                pe.wait_ge(consts_in, 16)
            for n in range(8):
                t, kk = n // 2, n % 2
                pe.wait_ge(xn_done, NT * ph + t + 1)
                if n >= 4:
                    pe.wait_ge((tr_out_a, tr_out_d)[1 if ph in (0, 2) else n % 2], TR_OUT[ph] + (n - 4 if ph in (0, 2) else (n - 4) // 2) + 1)
                for j in range(4):
                    k = 4 * kk + j
                    mm = pe.transpose(PB[n % 4][:, j * P:(j + 1) * P], XN[:, t, (k % 2) * 512 + k // 2:(k % 2 + 1) * 512:4], ident)
                mm.then_inc(tr_done, 1)
                if between and kk and t:
                    between(t - 1)
            pe.wait_ge(tr_out_a, TR_OUT[ph + 1])
            pe.wait_ge(tr_out_d, TR_OUT[ph + 1])
            if between:
                between(NT - 1)

        s_ = Carve(SCR, SCR_N)
        prm = s_(640 + 8 + 4 + 4 + 128)
        cwr, cw = s_(128), s_(48)
        qk_gain, sink_b, alog_b, dtb_b, gdn_gain = prm[:, 0:640], prm[:, 640:648], prm[:, 648:652], prm[:, 652:656], prm[:, 656:784]
        smalls = s_(400)
        sm_n = [0]

        def small(n):
            a = sm_n[0]
            sm_n[0] += n
            assert sm_n[0] <= 400
            return smalls[:, a:a + n]

        g_raw, g_abs, g_e, g_sp, g_val, beta, ea = (small(16) for _ in range(7))
        G_col, GL_col, kb_scale, kd_scale, eG = (small(16) for _ in range(5))
        mixed = s_.n
        A1 = s_(NT * 776).rearrange("p (t n) -> p t n", t=NT)
        qT = s_(4 * SEQ).rearrange("p (j n) -> p j n", j=4)
        kT = s_(SEQ)
        SC = s_(AH * 256).rearrange("p (h n) -> p h n", h=AH)
        PT = s_(AH * 256).rearrange("p (h n) -> p h n", h=AH)
        rt = s_(4 * 320).rearrange("p (a n) -> p a n", a=4)
        a_ss, a_rs = small(40), small(40)
        a_max, a_nmax, a_sum, a_sink, a_rec = (small(8) for _ in range(5))
        QKv = A1[:, :, 0:640]
        sq_tmp = SCR[:, mixed + NT * 776:mixed + NT * 776 + NT * 640].rearrange("p (t n) -> p t n", t=NT)

        G_STAGES = dict(g_by_dve=("g_pre", "g_one", "g_gates", "g_left"), g_by_act=("g_exp", "g_ln"))

        def g_stage(name):
            by = next(k for k, v in G_STAGES.items() if name in v)
            return sg(by), G_STAGES[by].index(name) + 1

        WUQ = ring_r[:, 3, :]
        E_GDN, E_OUT = 6, 6 + 4 * GH

        def kvq_part(i):
            if i < 2:
                return c_kv, WU0, slice(i * KT * 132, (i + 1) * KT * 132)
            return c_q, WUQ, slice((i - 2) * SLOT // 4, (i - 1) * SLOT // 4)

        def split_kvq_act(act, i):
            c, up, a = kvq_part(i)
            act.wait_ge(w_landed[c], landed(c))
            act.copy(up[:, a], slot_of(c)[:, a]).then_inc(sg("e_upper"), 1)

        def split_kvq_pool(pool):
            for i in range(6):
                c, up, a = kvq_part(i)
                pool.wait_ge(sg("e_upper"), i + 1)
                pool.tensor_tensor(ring_r[:, c, a], slot_of(c)[:, a], up[:, a].bitcast(F32), ALU.subtract).then_inc(sg("e_lower"), 1)

        def gdn_part(a, n):
            return a.rearrange("p (k s n) -> p k s n", k=KT, s=4)[:, :, n % 4, :]

        def split_gdn_act(act, n):
            if n >= 4 * GH:
                return
            h, i = n // 4, n % 4
            c = gdn_at[h]
            act.wait_ge(w_landed[c % RING], landed(c))
            if n < 4:
                act.wait_ge(sg("a_proj"), 4)
            else:
                act.wait_ge(*((sg("d_z"), h) if i == 3 else (sg("d_proj"), 3 * (h - 1) + i + 1)))
            act.copy(gdn_part(WU0, n), gdn_part(slot_of(c), n)).then_inc(sg("e_upper"), 1)

        def split_gdn_pool(pool, n):
            c = gdn_at[n // 4]
            pool.wait_ge(sg("e_upper"), E_GDN + n + 1)
            pool.tensor_tensor(gdn_part(ring_r[:, c % RING, :], n), gdn_part(slot_of(c), n), gdn_part(WU0, n).bitcast(F32), ALU.subtract).then_inc(sg("e_lower"), 1)

        def oute_part(i):
            return c_oute + i // 4, slice(i % 4 * SLOT // 4, (i % 4 + 1) * SLOT // 4)

        def split_oute_act(act, i):
            c, a = oute_part(i)
            act.wait_ge(sg("d_z"), GH)
            act.wait_ge(w_landed[c % RING], landed(c))
            act.copy(ring_r[:, 4 + i // 4, a], slot_of(c)[:, a]).then_inc(sg("e_upper"), 1)

        def split_oute_pool(pool):
            for i in range(8):
                c, a = oute_part(i)
                pool.wait_ge(sg("e_upper"), E_OUT + i + 1)
                pool.tensor_tensor(ring_r[:, c % RING, a], slot_of(c)[:, a], ring_r[:, 4 + i // 4, a].bitcast(F32), ALU.subtract).then_inc(sg("e_lower"), 1)

        def attn_pe(pe):
            for n in range(8):
                c, t = (c_kv, n) if n < 4 else (c_q, n - 4)
                if n >= 4:
                    pe.wait_ge(sg("a_proj_out"), n - 3)
                width = 264 if n < 4 else 512
                w = [a[:, 0:KT * width].rearrange("p (k n) -> p k n", k=KT) for a in (WU0 if n < 4 else WUQ, ring_r[:, c, :])]
                for k in range(KT):
                    if n % 4 == 0 and k % 2 == 0:
                        pe.wait_ge(sg("e_lower"), 1 + k // 4 if n == 0 else 3 + k // 2)
                    mm = split_mm(pe, PB[4 + n % 4][:, 0:width], [a[:, k, t * P:(t + 1) * P] for a in (HTU0, HT_r)], [a[:, k, :] for a in w], k == 0, k == KT - 1)
                mm.then_inc(sg("a_proj"), 1)
            pe.wait_ge(*g_stage("g_gates"))
            pe.wait_ge(params_in, PARAMS)
            pe.transpose(PB[2][:, 0:48], cwr[0:48, :], ident[0:48, 0:48]).then_inc(sg("d_cw"), 1)
            pe.matmul(PB[0][:, 0:16], const("cum"), g_val, start=True, stop=True)
            pe.matmul(PB[1][:, 0:16], const("chunk"), g_val, start=True, stop=True).then_inc(sg("g_cum"), 1)
            pe.wait_ge(sg("a_proj_out"), 8)
            for n in range(5):
                gproj_pe(pe, n)
            pe.wait_ge(sg("a_rope"), 1)
            pe.wait_ge(sg("d_conv_ready"), 1)
            for t in range(NT):
                b = PB[2 + t % 2]
                if t >= 2:
                    pe.wait_ge(sg("a_qt_out"), t - 1)
                for j in range(4):
                    pe.transpose(b[:, j * P:(j + 1) * P], QKv[:, t, j * P:(j + 1) * P], ident)
                pe.transpose(PB[6][:, t * P:(t + 1) * P], QKv[:, t, 512:640], ident).then_inc(sg("a_qt"), 1)
            for t in range(NT):
                if t == 0:
                    pe.wait_ge(sg("a_qt_out"), NT + 1)
                    pe.wait_ge(*g_stage("g_left"))
                lo = max(t - 1, 0) * P
                n = (t + 1) * P - lo
                if t:
                    pe.wait_ge(sg("a_masked"), 4 * t)
                for g in range(2):
                    for j in range(4):
                        h = 4 * g + j
                        mm = pe.matmul(PB[h // 2][:, (h % 2) * 256 + 256 - n:(h % 2) * 256 + 256], qT[64 * g:64 * g + 64, j, t * P:(t + 1) * P],
                                       kT[64 * g:64 * g + 64, lo:lo + n], start=True, stop=True)
                        if h % 2:
                            mm.then_inc(sg("a_scores"), 1)
                gproj_pe(pe, 5 + 3 * t)
                gproj_pe(pe, 6 + 3 * t)
                pe.wait_ge(sg("a_exp"), AH * (t + 1))
                for hp in range(4):
                    if hp == 1 or t + hp == 0:
                        g_left_bank(pe, 6 + 3 * t if hp else 2)
                    if hp >= 2:
                        pe.wait_ge(sg("a_pt_out"), 4 * t + hp - 1)
                    for h in (2 * hp, 2 * hp + 1):
                        for b in range(0 if t else 1, 2):
                            mm = pe.transpose(PB[4 + hp % 2][:, (h % 2) * 256 + b * P:(h % 2) * 256 + (b + 1) * P], SC[:, h, b * P:(b + 1) * P], ident)
                    mm.then_inc(sg("a_pt"), 1)
                for h in range(AH):
                    pe.wait_ge(sg("a_pt_out"), 4 * t + h // 2 + 1)
                    if t and h == 0:
                        pe.wait_ge(sg("a_y"), t)
                    for b in range(0 if t else 1, 2):
                        mm = pe.matmul(PB[6][:, h * 64:(h + 1) * 64], PT[:, h, b * P:(b + 1) * P],
                                       A1[:, t - 1 + b, 640 + 64 * (h // 4):704 + 64 * (h // 4)], start=(b == (0 if t else 1)), stop=(b == 1))
                mm.then_inc(sg("a_pv"), 1)
                gproj_pe(pe, 7 + 3 * t)

        def attn_act(act, step):
            for n in range(8):
                t = n % 4
                act.wait_ge(sg("a_proj"), n + 1)
                if n < 4:
                    act.copy(A1[:, t, 512:776], PB[4 + n % 4][:, 0:264]).then_inc(sg("a_proj_out"), 1)
                else:
                    act.copy(A1[:, t, 0:512].rearrange("p (j g d) -> p g j d", j=4, g=2),
                             PB[4 + n % 4][:, :].rearrange("p (g j d) -> p g j d", g=2, j=4)).then_inc(sg("a_proj_out"), 1)
                if n == 3:
                    for i in range(4):
                        split_gdn_act(act, i)
                    act.wait_ge(params_in, PARAMS)
                    act.wait_ge(*g_stage("g_pre"))
                    act.activation(g_e, g_abs, ACT.Exp, scale=-1.0)
                    act.activation(ea[:, 0:4], alog_b, ACT.Exp)
                    act.activation(beta.rearrange("p (t h) -> p t h", t=NT), A1[:, :, 772:776], ACT.Exp, scale=-1.0).then_inc(sg("g_by_act"), 1)
                    act.wait_ge(*g_stage("g_one"))
                    act.activation(g_sp, g_e, ACT.Ln).then_inc(sg("g_by_act"), 1)
            act.wait_ge(sg("a_proj_out"), 8)
            act.activation(sq_tmp, QKv, ACT.Square).then_inc(sg("a_sq"), 1)
            for n in range(5):
                gproj_act(act, n)
            for t in range(NT):
                act.wait_ge(sg("a_qt"), t + 1)
                act.copy(qT[:, :, t * P:(t + 1) * P], PB[2 + t % 2][:, :].rearrange("p (j q) -> p j q", j=4)).then_inc(sg("a_qt_out"), 1)
            act.copy(kT, PB[6][:, :]).then_inc(sg("a_qt_out"), 1)
            split_gdn_act(act, 8)
            for n in range(3):
                gsilu_act(act, n)
            for t in range(NT):
                act.wait_ge(sg("a_max"), t + 1)
                w = slice(0, 256) if t else slice(P, 256)
                for h in range(AH):
                    act.activation(SC[:, h, w], SC[:, h, w], ACT.Exp, bias=a_nmax[:, h:h + 1], accum_out=a_sum[:, h:h + 1]).then_inc(sg("a_exp"), 1)
                act.activation(a_sink, a_sink, ACT.Exp).then_inc(sg("a_sinkexp"), 1)
                gproj_act(act, 5 + 3 * t)
                gproj_act(act, 6 + 3 * t)
                for hp in range(4):
                    act.wait_ge(sg("a_pt"), 4 * t + hp + 1)
                    o = PT[:, 2 * hp:2 * hp + 2, w]
                    act.copy(o, PB[4 + hp % 2][:, :].rearrange("p (h n) -> p h n", h=2)[:, :, w]).then_inc(sg("a_pt_out"), 1)
                gsilu_act(act, 4 + 3 * t)
                gsilu_act(act, 5 + 3 * t)
                gsilu_act(act, 6 + 3 * t)
                gproj_act(act, 7 + 3 * t)

        def attn_pool(pool, step):
            pool.wait_ge(sg("a_sums"), 1)
            step.then(pool.tensor_scalar(a_rs, a_ss, 1.0 / ADH, EPS, ALU.mult, ALU.add))
            pool.tensor_tensor(a_rs, a_rs, mhalf[:, 0:40], ALU.pow).then_inc(sg("a_rstd"), 1)

        def attn_dve(dve, step):
            dve.wait_ge(params_in, PARAMS)
            dve.wait_ge(sg("a_proj_out"), 4)
            gv = lambda a: a.rearrange("p (t h) -> p t h", t=NT)
            bh = lambda a: a[:, None, :].to_broadcast([P, NT, 4])
            step.then(dve.tensor_tensor(gv(g_raw), A1[:, :, 768:772], bh(dtb_b), ALU.add))
            step.then(dve.tensor_scalar(g_val, g_raw, -1.0, None, ALU.mult))
            dve.tensor_tensor(g_abs, g_val, g_raw, ALU.max).then_inc(sg("g_by_dve"), 1)
            step.then(dve.tensor_scalar(g_raw, g_raw, 0.0, None, ALU.max))
            dve.wait_ge(*g_stage("g_exp"))
            dve.tensor_scalar(g_e, g_e, 1.0, None, ALU.add).then_inc(sg("g_by_dve"), 1)
            step.then(dve.tensor_scalar(beta, beta, 1.0, None, ALU.add))
            step.then(dve.reciprocal(beta, beta))
            dve.wait_ge(*g_stage("g_ln"))
            step.then(dve.tensor_tensor(g_raw, g_raw, g_sp, ALU.add))
            dve.scalar_tensor_tensor(gv(g_val), gv(g_raw), -1.0, bh(ea[:, 0:4]), ALU.mult, ALU.mult).then_inc(sg("g_by_dve"), 1)
            dve.wait_ge(sg("d_cw"), 1)
            dve.tensor_copy(cw, PB[2][:, 0:48]).then_inc(sg("d_conv_ready"), 1)
            dve.wait_ge(sg("d_conv_ready"), 1)
            dve.wait_ge(sg("a_proj"), 8)
            dve.memset(xc[:, :, 0:3], 0.0).then_inc(sg("d_conv_ready"), 1)
            dve.wait_ge(sg("a_sq"), 1)
            dve.tensor_reduce(a_ss.rearrange("p (t h) -> p t h", t=NT), sq_tmp.rearrange("p t (h d) -> p t h d", d=ADH), AX, ALU.add).then_inc(sg("a_sums"), 1)
            dve.wait_ge(sg("a_rstd"), 1)
            dve.wait_ge(sg("a_proj_out"), 8)
            for t in range(NT):
                v = QKv[:, t, :].rearrange("p (h d) -> p h d", d=ADH)
                step(dve.tensor_tensor(v, v, a_rs[:, t * 10:(t + 1) * 10, None].to_broadcast([P, AQK, ADH]), ALU.mult))
            step.wait()
            step.then(dve.tensor_tensor(QKv, QKv, qk_gain[:, None, :].to_broadcast([P, NT, 640]), ALU.mult))
            x1 = [QKv[:, t, :].rearrange("p (h d) -> p h d", d=ADH)[:, :, 0:8] for t in range(NT)]
            x2 = [QKv[:, t, :].rearrange("p (h d) -> p h d", d=ADH)[:, :, 8:16] for t in range(NT)]
            rot = [[rt[:, a, t * 80:(t + 1) * 80].rearrange("p (h d) -> p h d", d=8) for t in range(NT)] for a in range(4)]
            for t in range(NT):
                cs = const("rcos")[:, None, t * 8:(t + 1) * 8].to_broadcast([P, AQK, 8])
                sn = const("rsin")[:, None, t * 8:(t + 1) * 8].to_broadcast([P, AQK, 8])
                step(dve.tensor_tensor(rot[0][t], x1[t], cs, ALU.mult))
                step(dve.tensor_tensor(rot[1][t], x2[t], sn, ALU.mult))
                step(dve.tensor_tensor(rot[2][t], x2[t], cs, ALU.mult))
                step(dve.tensor_tensor(rot[3][t], x1[t], sn, ALU.mult))
            step.wait()
            for t in range(NT):
                step(dve.tensor_tensor(x1[t], rot[0][t], rot[1][t], ALU.subtract))
                step(dve.tensor_tensor(x2[t], rot[2][t], rot[3][t], ALU.add))
            step.wait()
            dve.tensor_copy(rt[:, 0, 0:1], rt[:, 0, 0:1]).then_inc(sg("a_rope"), 1)
            dve.wait_ge(sg("g_cum"), 1)
            step(dve.tensor_copy(G_col, PB[0][:, 0:16]))
            step(dve.tensor_copy(GL_col, PB[1][:, 0:16]))
            step.wait()
            dve.tensor_tensor(GL_col, GL_col, G_col, ALU.subtract).then_inc(sg("g_by_dve"), 1)
            for n in range(3):
                gconv_dve(dve, n, step)
            for t in range(NT):
                w = slice(0, 256) if t else slice(P, 256)
                n = 256 if t else P
                for b in range(4):
                    dve.wait_ge(sg("a_scores"), 4 * t + b + 1)
                    dve.scalar_tensor_tensor(SC[:, 2 * b:2 * b + 2, w], PB[b][:, :].rearrange("p (h n) -> p h n", h=2)[:, :, w], ADH ** -0.5,
                                             const("window")[:, None, w].to_broadcast([P, 2, n]), ALU.mult, ALU.add).then_inc(sg("a_masked"), 1)
                dve.wait_ge(sg("a_masked"), 4 * (t + 1))
                step.then(dve.tensor_reduce(a_max, SC[:, :, w], AX, ALU.max))
                step.then(dve.tensor_tensor(a_max, a_max, sink_b, ALU.max))
                step(dve.tensor_tensor(a_sink, sink_b, a_max, ALU.subtract))
                step.wait()
                dve.tensor_scalar(a_nmax, a_max, -1.0, None, ALU.mult).then_inc(sg("a_max"), 1)
                for n in range(3):
                    gconv_dve(dve, 4 + 3 * t + n, step)
                dve.wait_ge(sg("a_exp"), AH * (t + 1))
                dve.wait_ge(sg("a_sinkexp"), t + 1)
                step.then(dve.tensor_tensor(a_rec, a_sum, a_sink, ALU.add))
                step.then(dve.reciprocal(a_rec, a_rec))
                dve.wait_ge(sg("a_pv"), t + 1)
                dve.tensor_tensor(XN[:, t, 0:512].rearrange("p (h d) -> p h d", h=AH), PB[6][:, :].rearrange("p (h d) -> p h d", h=AH),
                                  a_rec[:, :, None].to_broadcast([P, AH, ADH]), ALU.mult).then_inc(sg("a_y"), 1)

        t4 = lambda a: a.rearrange("p (t n) -> p t n", t=NT)
        r_ = Carve(ring[:, 0:2, :].rearrange("p a n -> p (a n)"), 2 * SLOT)
        CV = [r_(3 * 512).rearrange("p (s n) -> p s n", s=3) for _ in range(GH)]
        xc = r_(3 * 515).rearrange("p (s n) -> p s n", s=3)
        zs_at = lambda h: XN[:, :, 512 + h * GD:512 + (h + 1) * GD]

        def g_bank(n):
            return PB[(7, 5, 4, 7, 5)[n] if n < 5 else (7, 5, 7)[(n - 5) % 3]]

        def g_left_bank(eng, n):
            eng.wait_ge(*((sg("d_zs"), n // 4 + 1) if n % 4 == 3 else (sg("d_x"), 3 * (n // 4) + n % 4 + 1)))

        def gproj_pe(pe, n):
            if n >= 4 * GH:
                return
            h, s = n // 4, n % 4
            w = [a.rearrange("p (k s n) -> p k s n", k=KT, s=4)[:, :, s, :] for a in (WU0, ring_r[:, gdn_at[h] % RING, :])]
            pe.wait_ge(sg("e_lower"), E_GDN + n + 1)
            if n >= 3:
                g_left_bank(pe, max(m for m in range(n) if g_bank(m) is g_bank(n)))
            for k in range(KT):
                mm = split_mm(pe, g_bank(n)[:, :], [a[:, k, :] for a in w], (HTU0[:, k, :], HT_r[:, k, :]), k == 0, k == KT - 1)
            mm.then_inc(sg("d_z" if s == 3 else "d_proj"), 1)

        def gproj_act(act, n):
            if n >= 4 * GH:
                return
            h, s = n // 4, n % 4
            if s < 3:
                act.wait_ge(sg("d_proj"), 3 * h + s + 1)
                if n == 0:
                    act.wait_ge(sg("d_conv_ready"), 2)
                if h:
                    act.wait_ge(sg("d_conv"), 3 * (h - 1) + s + 1)
                act.copy(xc[:, s, 3:515], g_bank(n)[:, :]).then_inc(sg("d_x"), 1)
            else:
                act.wait_ge(sg("d_z"), h + 1)
                act.activation(zs_at(h), t4(g_bank(n)[:, :]), ACT.Silu).then_inc(sg("d_zs"), 1)
            if n != 4:
                split_gdn_act(act, n + 4)

        def gsilu_act(act, n):
            if n >= 4 * GH:
                return
            h, s = n // 4, n % 4
            if s < 3:
                act.wait_ge(sg("d_conv"), 3 * h + s + 1)
                act.activation(CV[h][:, s, :], CV[h][:, s, :], ACT.Silu).then_inc(sg("d_silu"), 1)

        def gconv_dve(dve, n, step):
            h, s = n // 4, n % 4
            if s == 3 or n >= 4 * GH:
                return
            o = CV[h][:, s, :]
            dve.wait_ge(sg("d_x"), 3 * h + s + 1)
            tap = lambda i: cw[:, i * 12 + 4 * s + h:i * 12 + 4 * s + h + 1]
            step.then(dve.tensor_scalar(o, xc[:, s, 0:512], tap(0), None, ALU.mult))
            for i in (1, 2):
                step.then(dve.scalar_tensor_tensor(o, xc[:, s, i:i + 512], tap(i), o, ALU.mult, ALU.add))
            dve.scalar_tensor_tensor(o, xc[:, s, 3:515], tap(3), o, ALU.mult, ALU.add).then_inc(sg("d_conv"), 1)

        s_.n = mixed
        hb_ = Carve(HT[:, :, :].rearrange("p k n -> p (k n)"), KT * SEQ)
        heads = []
        for u in range(2):
            def b512(u=u):
                return t4((hb_ if u and hb_.n + 512 <= hb_.size else s_)(512))
            w = dict(N1=b512(), nwT=b512(), e_dec=b512(), e_decT=b512(), eGB=b512(), Tm=b512(), TTm=b512(), Cm=b512(),
                     qd=b512(), kbg=b512(), kd=b512(), vb=b512(), og=b512(), VN=s_(128), St=s_(128),
                     n_ss=small(16), n_rs=small(16), o_ss=small(4), o_rs=small(4), bank=[PB[4 * u + i] for i in range(4)])
            heads.append(type("Head", (), w))
        pairs = [(2 * g, 2 * g + 1) for g in range(GH // 2)]

        def gb_bank(h):
            return heads[h % 2].bank[h // 2]

        def nth(h, n=0, of=1):
            return 2 * of * (h // 2) + 2 * n + h % 2 + 1

        def set_free(eng, h):
            if h < 2:
                eng.wait_ge(sg("a_y"), NT)
                eng.wait_ge(sg("d_z"), GH)
            else:
                eng.wait_ge(sg("d_v"), nth(h - 2, 2 * NT - 1, 2 * NT))
                eng.wait_ge(sg("d_o"), nth(h - 2, 2 * NT - 1, 2 * NT))
                eng.wait_ge(sg("d_oss"), nth(h - 2))

        def squares_at(h):
            H = heads[h % 2]
            return (H.N1, H.nwT) if h < 2 else (H.og, H.kd)

        def norm_col(h, s, t):
            return 8 * (h // 2) + 4 * s + t

        def gdn_norms_pe(pe):
            for h in range(GH):
                pe.wait_ge(sg("d_sq"), h + 1)
                for s in range(2):
                    for t in range(NT):
                        c = norm_col(h, s, t)
                        mm = pe.matmul(heads[h % 2].bank[1][:, c:c + 1], squares_at(h)[s][:, t, :], ones[:, 0:1], start=True, stop=True)
                mm.then_inc(sg("d_ss"), 1)

        def gdn_pe(pe):
            def pair_steps(pair):
                for n in range(2 * NT):
                    t, half = n // 2, (n % 2) * CH
                    r, m = slice(half, half + CH), n % 2
                    for h in pair:
                        H = heads[h % 2]
                        pe.matmul(H.bank[3 * m][r, 0:GD], H.TTm[:, t, r], H.vb[:, t, :], start=True, stop=False)
                        pe.wait_ge(sg("d_S"), nth(h, n, 2 * NT + 1))
                        pe.matmul(H.bank[3 * m][r, 0:GD], H.nwT[:, t, r], H.St, start=False, stop=True).then_inc(sg("d_v"), 1)
                        if n >= 2:
                            pe.wait_ge(sg("d_o_out"), nth(h, n - 2, 2 * NT))
                        pe.matmul(H.bank[1][r, m * GD:(m + 1) * GD], H.qd[:, t, r], H.St, start=True, stop=False)
                    for h in pair:
                        H = heads[h % 2]
                        pe.wait_ge(sg("d_v_out"), nth(h, n, 2 * NT))
                        pe.matmul(H.bank[2][:, 0:GD], H.kd[r, t, :], H.VN[r, :], start=True, stop=True).then_inc(sg("d_kv_new"), 1)
                        pe.matmul(H.bank[1][r, m * GD:(m + 1) * GD], H.e_decT[r, t, r], H.VN[r, :], start=False, stop=True).then_inc(sg("d_o"), 1)

            for pair in pairs:
                for h in pair:
                    if h == 0:
                        pe.wait_ge(sg("a_masked"), 4 * NT)
                    elif h == 1:
                        pe.wait_ge(sg("a_pt_out"), 4 * NT)
                        pe.wait_ge(sg("a_y"), NT)
                        g_left_bank(pe, 4 * GH - 1)
                    else:
                        pe.wait_ge(sg("d_v_out"), nth(h - 2, 2 * NT - 1, 2 * NT))
                        pe.wait_ge(sg("d_o_out"), nth(h - 2, 2 * NT - 1, 2 * NT))
                        pe.wait_ge(sg("d_S"), nth(h - 2, 2 * NT, 2 * NT + 1))
                    for t in range(NT):
                        mm = pe.matmul(gb_bank(h)[:, t * P:(t + 1) * P], g_val[:, 4 * t + h:4 * t + h + 1].to_broadcast([P, P]), const("cum"), start=True, stop=True)
                    mm.then_inc(sg("d_gb"), 1)
                if pair[0] == 0:
                    gdn_norms_pe(pe)
                for h in pair:
                    H = heads[h % 2]
                    pe.wait_ge(sg("d_rs"), h % 2 + 1)
                    for s in range(2):
                        for t in range(NT):
                            mm = pe.matmul(H.bank[2 + s][:, t * P:(t + 1) * P], H.n_rs[:, norm_col(h, s, t):norm_col(h, s, t) + 1].to_broadcast([P, P]), ident, start=True, stop=True)
                    mm.then_inc(sg("d_rb"), 1)
                for h in pair:
                    H, cv = heads[h % 2], CV[h]
                    pe.wait_ge(sg("d_qk"), nth(h))
                    pe.wait_ge(sg("d_egb"), nth(h))
                    if h >= 2:
                        pe.wait_ge(sg("d_y"), h - 1)
                    pe.wait_ge(sg("d_ss_out"), h % 2 + 1)
                    for t in range(NT):
                        mm = pe.matmul(H.bank[t // 2][:, (t % 2) * 256:(t % 2) * 256 + 256], cv[:, 1, t * P:(t + 1) * P], cv[:, 0:2, t * P:(t + 1) * P],
                                       start=True, stop=True)
                    mm.then_inc(sg("d_kk"), 1)
                    for s in range(2):
                        for t in range(NT):
                            mm = pe.transpose(H.bank[2 + s][:, t * P:(t + 1) * P], cv[:, 1 + s, t * P:(t + 1) * P], ident)
                    mm.then_inc(sg("d_kv"), 1)
                for lv in range(LEVELS):
                    for h in pair:
                        H = heads[h % 2]
                        pe.wait_ge(sg("d_T"), nth(h, lv, LEVELS))
                        for t in range(NT):
                            mm = pe.matmul(H.bank[0][:, t * P:(t + 1) * P], H.Cm[:, t, :], H.TTm[:, t, :] if lv else ident, start=True, stop=True)
                        mm.then_inc(sg("d_n1"), 1)
                    for h in pair if lv else ():
                        H = heads[h % 2]
                        pe.wait_ge(sg("d_n1_out"), nth(h, lv - 1, LEVELS - 1))
                        pe.wait_ge(sg("d_Tm"), nth(h, lv - 1, LEVELS - 1))
                        for t in range(NT):
                            mm = pe.matmul(H.bank[1][:, t * P:(t + 1) * P], H.Tm[:, t, :], H.N1[:, t, :], start=True, stop=True)
                        mm.then_inc(sg("d_tt"), 1)
                        if lv < LEVELS - 1:
                            if lv == 1:
                                pe.wait_ge(sg("d_scaled"), nth(h))
                            for t in range(NT):
                                mm = pe.matmul(H.bank[2][:, t * P:(t + 1) * P], H.N1[:, t, :], H.Tm[:, t, :], start=True, stop=True)
                            mm.then_inc(sg("d_t"), 1)
                for h in pair:
                    H = heads[h % 2]
                    pe.wait_ge(sg("d_inv"), nth(h))
                    for t in range(NT):
                        mm = pe.matmul(H.bank[3][:, t * P:(t + 1) * P], H.kbg[:, t, :], H.TTm[:, t, :], start=True, stop=True)
                    mm.then_inc(sg("d_w"), 1)
                for h in pair:
                    pe.wait_ge(sg("d_w_out"), nth(h))
                    pe.wait_ge(sg("d_qd"), nth(h))
                pair_steps(pair)
                for h in pair:
                    pe.wait_ge(sg("d_v_out"), nth(h, 2 * NT - 1, 2 * NT))
                    pe.wait_ge(sg("d_zs"), h + 1)
                    for t in range(NT):
                        mm = pe.transpose(heads[h % 2].bank[0][:, t * P:(t + 1) * P], zs_at(h)[:, t, :], ident)
                    mm.then_inc(sg("d_zt"), 1)

        def gdn_act(act, step):
            act.wait_ge(*g_stage("g_left"))
            act.activation(kd_scale, GL_col, ACT.Exp).then_inc(sg("d_eg"), 1)
            act.activation(eG, G_col, ACT.Exp).then_inc(sg("d_eg"), 1)
            act.wait_ge(sg("d_eg"), 2)
            for h in range(GH):
                act.wait_ge(sg("d_silu"), 3 * h + 3)
                set_free(act, h % 2)
                for s in range(2):
                    ins = act.activation(squares_at(h)[s], t4(CV[h][:, s, :]), ACT.Square)
                    if s == 0:
                        step.then(ins)
                ins.then_inc(sg("d_sq"), 1)
            for pair in pairs:
                for h in pair:
                    H = heads[h % 2]
                    act.wait_ge(sg("d_diff"), nth(h))
                    act.activation(H.eGB, t4(gb_bank(h)[:, :]), ACT.Exp).then_inc(sg("d_egb"), 1)
                    step(act.activation(H.e_dec, H.e_dec, ACT.Exp))
                    step.wait()
                    act.activation(H.e_decT, H.e_decT, ACT.Exp, scale=-1.0).then_inc(sg("d_dec"), 1)
                for h in pair:
                    H = heads[h % 2]
                    act.wait_ge(sg("d_kv"), nth(h))
                    act.wait_ge(sg("d_kbs"), 1)
                    for t in range(NT):
                        c = slice(4 * t + h, 4 * t + h + 1)
                        step(act.activation(H.kbg[:, t, :], H.bank[2][:, t * P:(t + 1) * P], ACT.Copy, scale=kb_scale[:, c]))
                        step(act.activation(H.kd[:, t, :], H.bank[2][:, t * P:(t + 1) * P], ACT.Copy, scale=kd_scale[:, c]))
                        if t == NT - 1:
                            step.wait()
                        last = act.activation(H.vb[:, t, :], H.bank[3][:, t * P:(t + 1) * P], ACT.Copy, scale=beta[:, c])
                        if t < NT - 1:
                            step(last)
                    last.then_inc(sg("d_scaled"), 1)
                for lv in range(1, LEVELS):
                    for h in pair:
                        H = heads[h % 2]
                        act.wait_ge(sg("d_n1"), nth(h, lv, LEVELS))
                        act.copy(H.N1, t4(H.bank[0][:, :])).then_inc(sg("d_n1_out"), 1)
                        if pair[0] and lv > 1:
                            split_oute_act(act, 2 * (lv - 2) + h % 2)
                for h in pair:
                    H = heads[h % 2]
                    act.wait_ge(sg("d_w"), nth(h))
                    act.activation(H.nwT, t4(H.bank[3][:, :]), ACT.Copy, scale=-1.0).then_inc(sg("d_w_out"), 1)
                for n in range(2 * NT):
                    t, half = n // 2, (n % 2) * CH
                    r, m = slice(half, half + CH), n % 2
                    for h in pair:
                        H = heads[h % 2]
                        act.wait_ge(sg("d_v"), nth(h, n, 2 * NT))
                        act.copy(H.VN[r, :], H.bank[3 * m][r, 0:GD]).then_inc(sg("d_v_out"), 1)
                    for h in pair:
                        H = heads[h % 2]
                        act.wait_ge(sg("d_o"), nth(h, n, 2 * NT))
                        act.copy(H.og[r, t, :], H.bank[1][r, m * GD:(m + 1) * GD]).then_inc(sg("d_o_out"), 1)
                for h in pair:
                    H = heads[h % 2]
                    act.wait_ge(sg("d_o_out"), nth(h, 2 * NT - 1, 2 * NT))
                    for t in range(NT):
                        last = act.activation(H.N1[:, t, :], H.og[:, t, :], ACT.Square, accum_out=H.o_ss[:, t:t + 1])
                        if t < NT - 1:
                            step(last)
                            step.wait()
                    last.then_inc(sg("d_oss"), 1)

        def gdn_pool(pool, step):
            for u, H in enumerate(heads):
                pool.wait_ge(sg("d_ss_out"), u + 1)
                step.then(pool.tensor_scalar(H.n_rs, H.n_ss, 1.0, EPS, ALU.mult, ALU.add))
                step.then(pool.tensor_tensor(H.n_rs, H.n_rs, mhalf[:, 0:16], ALU.pow))
                q = H.n_rs.rearrange("p (g s) -> p g s", g=2)[:, :, 0:4]
                pool.tensor_scalar(q, q, GD ** -0.5, None, ALU.mult).then_inc(sg("d_rs"), 1)
            for pair in pairs:
                if pair[0]:
                    split_oute_pool(pool)
                for h in pair:
                    H = heads[h % 2]
                    pool.wait_ge(sg("d_oss"), nth(h))
                    step.then(pool.tensor_scalar(H.o_rs, H.o_ss, 1.0 / GD, EPS, ALU.mult, ALU.add))
                    pool.tensor_tensor(H.o_rs, H.o_rs, mhalf[:, 0:4], ALU.pow).then_inc(sg("d_ors"), 1)

        def gdn_dve(dve, step):
            bc = lambda name: const(name)[:, None, :].to_broadcast([P, NT, P])

            def unit(pair):
                for h in pair:
                    H, cv = heads[h % 2], CV[h]
                    dve.wait_ge(sg("d_rb"), nth(h))
                    step.then(dve.tensor_tensor(cv[:, 0, :], cv[:, 0, :], H.bank[2][:, :], ALU.mult))
                    dve.tensor_tensor(cv[:, 1, :], cv[:, 1, :], H.bank[3][:, :], ALU.mult).then_inc(sg("d_qk"), 1)

            for pair in pairs:
                if pair[0]:
                    unit(pair)
                for h in pair:
                    H = heads[h % 2]
                    set_free(dve, h)
                    dve.wait_ge(sg("d_gb"), nth(h))
                    Gi = G_col.rearrange("p (t h) -> p t h", h=4)[:, :, h:h + 1].to_broadcast([P, NT, P])
                    step.then(dve.tensor_tensor(H.e_dec, Gi, t4(gb_bank(h)[:, :]), ALU.subtract))
                    step.then(dve.tensor_scalar(H.e_decT, H.e_dec, 0.0, None, ALU.max))
                    dve.tensor_scalar(H.e_dec, H.e_dec, 0.0, None, ALU.min).then_inc(sg("d_diff"), 1)
                if pair[0] == 0:
                    for u, H in enumerate(heads):
                        dve.wait_ge(sg("d_ss"), 3 + u)
                        dve.tensor_copy(H.n_ss, H.bank[1][:, 0:16]).then_inc(sg("d_ss_out"), 1)
                    dve.wait_ge(sg("d_eg"), 2)
                    dve.tensor_tensor(kb_scale, beta, eG, ALU.mult).then_inc(sg("d_kbs"), 1)
                    unit(pair)
                for h in pair:
                    H = heads[h % 2]
                    dve.wait_ge(sg("d_dec"), nth(h))
                    for t in range(NT):
                        step(dve.scalar_tensor_tensor(H.e_dec[:, t, :], H.e_dec[:, t, :], beta[:, 4 * t + h:4 * t + h + 1], const("strict"), ALU.mult, ALU.mult))
                    step(dve.tensor_tensor(H.e_decT, H.e_decT, bc("inclT"), ALU.mult))
                for h in pair:
                    H = heads[h % 2]
                    step.wait()
                    dve.wait_ge(sg("d_kk"), nth(h))
                    for b in range(2):
                        kk = H.bank[b][:, :].rearrange("p (t s n) -> p t s n", t=2, s=2)
                        step(dve.tensor_tensor(H.e_dec[:, 2 * b:2 * b + 2, :], kk[:, :, 1, :], H.e_dec[:, 2 * b:2 * b + 2, :], ALU.mult))
                        step(dve.tensor_tensor(H.e_decT[:, 2 * b:2 * b + 2, :], kk[:, :, 0, :], H.e_decT[:, 2 * b:2 * b + 2, :], ALU.mult))
                    step.wait()
                    dve.tensor_tensor(H.Cm, H.e_dec, bc("level0"), ALU.mult).then_inc(sg("d_T"), 1)
                for h in pair:
                    H = heads[h % 2]
                    dve.wait_ge(sg("d_T"), nth(h, 0, LEVELS))
                    dve.tensor_tensor(H.Tm, bc("ident"), H.Cm, ALU.subtract).then_inc(sg("d_Tm"), 1)
                for h in pair:
                    H = heads[h % 2]
                    dve.wait_ge(sg("d_egb"), nth(h))
                    dve.tensor_tensor(H.qd, t4(CV[h][:, 0, :]), H.eGB, ALU.mult).then_inc(sg("d_qd"), 1)
                for lv in range(LEVELS):
                    for h in pair:
                        H = heads[h % 2]
                        dve.wait_ge(sg("d_n1"), nth(h, lv, LEVELS))
                        if lv == 0:
                            dve.wait_ge(sg("d_Tm"), nth(h, 0, LEVELS - 1))
                        if lv < LEVELS - 1:
                            step(dve.tensor_tensor(H.Cm, H.e_dec, bc(f"level{lv + 1}"), ALU.mult))
                    for h in pair:
                        H = heads[h % 2]
                        if lv:
                            dve.wait_ge(sg("d_tt"), nth(h, lv - 1, LEVELS - 1))
                            dve.wait_ge(sg("d_T"), nth(h, lv, LEVELS))
                        step.wait()
                        dve.tensor_tensor(H.TTm, H.TTm if lv else bc("ident"), t4(H.bank[1 if lv else 0][:, :]), ALU.subtract)\
                            .then_inc(sg("d_T" if lv < LEVELS - 1 else "d_inv"), 1)
                    for h in pair if 0 < lv < LEVELS - 1 else ():
                        H = heads[h % 2]
                        dve.wait_ge(sg("d_t"), nth(h, lv - 1, LEVELS - 2))
                        dve.wait_ge(sg("d_Tm"), nth(h, lv - 1, LEVELS - 1))
                        dve.tensor_tensor(H.Tm, H.Tm, t4(H.bank[2][:, :]), ALU.subtract).then_inc(sg("d_Tm"), 1)
                for h in pair:
                    dve.memset(heads[h % 2].St, 0.0).then_inc(sg("d_S"), 1)
                for n in range(2 * NT):
                    t, half = n // 2, (n % 2) * CH
                    for h in pair:
                        H = heads[h % 2]
                        dve.wait_ge(sg("d_S"), nth(h, n, 2 * NT + 1))
                        dve.wait_ge(sg("d_kv_new"), nth(h, n, 2 * NT))
                        dve.scalar_tensor_tensor(H.St, H.St, H.eGB[:, t, half + CH - 1:half + CH], H.bank[2][:, 0:GD], ALU.mult, ALU.add).then_inc(sg("d_S"), 1)
                for h in pair:
                    H = heads[h % 2]
                    dve.wait_ge(sg("d_ors"), nth(h))
                    for t in range(NT):
                        step(dve.scalar_tensor_tensor(H.og[:, t, :], H.og[:, t, :], H.o_rs[:, t:t + 1], gdn_gain, ALU.mult, ALU.mult))
                    step.wait()
                    dve.wait_ge(sg("d_zt"), h + 1)
                    dve.tensor_tensor(zs_at(h), H.og, t4(H.bank[0][:, :]), ALU.mult).then_inc(sg("d_y"), 1)


        YTU = SCR_r[:, mixed:mixed + 2 * 2048].rearrange("p (k n) -> p k n", k=KT)

        def oute_pe(pe):
            pe.wait_ge(sg("d_y"), GH)
            for n in range(8):
                t, g = n // 2, n % 2
                if n >= 4:
                    pe.wait_ge(sg("m_tr_d"), n - 3)
                for j in range(4):
                    mm = pe.transpose(PB[n % 4][:, j * P:(j + 1) * P], XN[:, t, g * 512 + j:(g + 1) * 512:4], ident)
                mm.then_inc(sg("m_tr"), 1)
            for n in range(8):
                t, half = n // 2, n % 2
                pe.wait_ge(sg("m_tr_d"), 2 * t + 2)
                if n >= 2:
                    pe.wait_ge(resid, n - 1)
                for g in range(2):
                    w = [ring_r[:, i, :].rearrange("p (k n) -> p k n", k=4) for i in (4 + g, (c_oute + g) % RING)]
                    for j in range(4):
                        if n == 0:
                            pe.wait_ge(sg("e_lower"), E_OUT + 4 * g + j + 1)
                        mm = split_mm(pe, PB[4 + n % 2][:, :], [a[:, 4 * g + j, t * P:(t + 1) * P] for a in (YTU, HT_r)],
                                      [a[:, j, half * 512:(half + 1) * 512] for a in w], g + j == 0, g == 1 and j == 3)
                mm.then_inc(sg("m_out"), 1)

        def oute_act(act):
            for n in range(8):
                t, g = n // 2, n % 2
                act.wait_ge(sg("m_tr"), n + 1)
                act.copy(YTU[:, 4 * g:4 * g + 4, t * P:(t + 1) * P], PB[n % 4][:, :].rearrange("p (k q) -> p k q", k=4)).then_inc(sg("m_tr_a"), 1)

        def oute_dve(dve):
            for n in range(8):
                t, g = n // 2, n % 2
                at = (slice(None), slice(4 * g, 4 * g + 4), slice(t * P, (t + 1) * P))
                dve.wait_ge(sg("m_tr_a"), n + 1)
                dve.tensor_tensor(HT_r[at], PB[n % 4][:, :].rearrange("p (k q) -> p k q", k=4), YTU[at].bitcast(F32), ALU.subtract).then_inc(sg("m_tr_d"), 1)
            for n in range(8):
                t, half = n // 2, n % 2
                dve.wait_ge(sg("m_out"), n + 1)
                xs = X[:, t, half * 512:(half + 1) * 512]
                dve.tensor_tensor(xs, xs, PB[4 + n % 2][:, :], ALU.add).then_inc(resid, 1)
                if half:
                    norm_dve(dve, 1, t - 1)
            norm_dve(dve, 1, NT - 1)

        def r32(a):
            return SCR_r[:, s_.n - a.shape[1]:s_.n]

        PAIRS = NE // 2
        s_.n, s_.size = 0, CO_AT
        tg = lambda a: a.rearrange("p (t n) -> p t n", t=NT)
        OH = [tg(r32(s_(NT * P))) for _ in range(2)]
        XG, XTt = s_(D), s_(D).rearrange("p (k n) -> p k n", k=KT)
        SIL, HHT = s_(512), s_(4 * SLOTS)
        YU, YL = r32(s_(D)), r32(s_(D))
        OT = r32(s_(512))
        GSL = s_(2)
        XNU = HT_r[:, :, :].rearrange("p k n -> p (k n)").rearrange("p (t n) -> p t n", t=NT)
        LT = XG[:, 0:512]
        LG = tg(s_(NT * NR))
        dg, eg, selg, ohg = (tg(s_(16)) for _ in range(4))
        EL4 = s_(NT * 32).rearrange("p (t e g) -> p t e g", t=NT, g=NG)
        EL, EL2, dd, oh1, oh2 = (tg(s_(NT * EPG)) for _ in range(5))
        gmax, vmax, m1, m2, e2, gate1, gate2, rsg = (s_(NT) for _ in range(8))
        M1, M2, POSM, GG = (tg(s_(NT * NE)) for _ in range(4))
        MMz = s_((NT + 1) * NE)
        MM = tg(MMz[:, 0:NT * NE])
        cnt_f = s_(1)
        cnt = sb("cnt", [P, 1], I32)

        PER_LAYER = dict(logits=1, logitsT=1, logitsT_out=1, masks=1, counts=1, gdiff=1, ediff=1, rexp=2, routed=1, xn_upper=NT, xn_lower=NT,
                         **dict.fromkeys(("oh", "ot", "ot_out", "gs", "gs_out"), PAIRS),
                         **dict.fromkeys(("gat", "xg", "xt", "xt_out", "gu", "sil", "hh", "ht", "ht_out", "y"), NE),
                         **dict.fromkeys(("y_upper", "y_lower"), 2 * NE), **dict.fromkeys(("comb", "added"), 8 * PAIRS))

        def moe_sem(l, name):
            return sg(f"m_{name}" if name in PER_LAYER else f"m{l}_{name}")

        OVER = dict(pe=("v_gat", "v_xt", "v_g0", "v_u0", "v_ht0", "v_y0", "v_g1", "v_u1", "v_ht1", "v_y1", "v_comb"),
                    act=("v_xg", "v_sil0", "v_ht_out0", "v_y_upper0", "v_sil1", "v_ht_out1", "v_y_upper1"),
                    dve=("v_oh", "v_xt_out", "v_hh0", "v_y_lower0", "v_hh1", "v_y_lower1", "v_added"))

        def over_done(l, name):
            return next(sg(f"m{l}_over_{eng}") for eng, stages in OVER.items() if name in stages)

        def over_wait(l, name, n):
            stages = next(x for x in OVER.values() if name in x)
            return over_done(l, name), n * len(stages) + stages.index(name) + 1

        def moe_wait(l, name, value):
            return moe_sem(l, name), value + l * PER_LAYER.get(name, 0)

        def one_hot(dve, step, out_oh, diff):
            n = out_oh.shape[2]
            step.then(dve.tensor_scalar(out_oh, diff, 0.0, None, ALU.is_equal))
            step.then(dve.tensor_tensor(out_oh, out_oh, const("first")[:, None, 0:n].to_broadcast([P, NT, n]), ALU.mult))
            step.then(dve.tensor_reduce(vmax, out_oh, AX, ALU.max))
            step.then(dve.tensor_tensor(out_oh, out_oh, vmax[:, :, None].to_broadcast([P, NT, n]), ALU.is_equal))

        def route_pool(pool, l):
            if l:
                pool.wait_ge(*moe_wait(0, "logits", 1))
                pool.wait_ge(*moe_wait(0, "routed", 1))
            pool.dma_start(WR[:, :, 0:NG], k_rows(w_router_group[l], 0, NG)).then_inc(router_in, 16)
            pool.dma_start(WR[:, :, NG:NR], k_rows(w_router_expert[l], 0, NE)).then_inc(router_in, 16)
            pool.dma_start(br[:, 0:NG], b_router_group[l:l + 1, :].to_broadcast([P, NG])).then_inc(router_in, 16)
            pool.dma_start(br[:, NG:NR], b_router_expert[l:l + 1, :].to_broadcast([P, NE])).then_inc(router_in, 16)

        def logits_pe(pe, l, t):
            if t == 0:
                pe.wait_ge(router_in, 64 * (l + 1))
            pe.wait_ge(tr_out_a, TR_OUT[2 * l + 1] + t + 1)
            pe.wait_ge(tr_out_d, TR_OUT[2 * l + 1] + t + 1)
            for k in range(KT):
                mm = pe.matmul(PB[6][0:NR, t * P:(t + 1) * P], WR[:, k, :], HT[:, k, t * P:(t + 1) * P], start=(k == 0), stop=(k == KT - 1))
            if t == NT - 1:
                mm.then_inc(moe_sem(l, "logitsT"), 1)
            for u in range(NT) if t == NT - 1 else ():
                pe.wait_ge(*moe_wait(l, "logitsT_out", 1))
                mm = pe.transpose(PB[7][:, u * NR:(u + 1) * NR], LT[0:NR, u * P:(u + 1) * P], ident[0:NR, 0:NR])
            if t == NT - 1:
                mm.then_inc(moe_sem(l, "logits"), 1)

        def route_pe(pe, l):
            ms = lambda n: moe_sem(l, n)
            mw = lambda n, v: moe_wait(l, n, v)
            pe.wait_ge(*mw("masks", 1))
            pe.matmul(PB[5][:, 0:(NT + 1) * NE], const("before"), MMz, start=True, stop=False)
            for u in range(NT):
                mm = pe.matmul(PB[5][:, (u + 1) * NE:(NT + 1) * NE], ones, MM[:, u:u + 1, :].to_broadcast([P, NT - u, NE]), start=False, stop=(u == NT - 1))
            mm.then_inc(ms("counts"), 1)

        def route_act(act, l):
            ms = lambda n: moe_sem(l, n)
            mw = lambda n, v: moe_wait(l, n, v)
            split_tokens_act(act, l)
            act.wait_ge(*mw("gdiff", 1))
            act.activation(eg, dg, ACT.Exp).then_inc(ms("rexp"), 1)
            act.wait_ge(*mw("ediff", 1))
            act.activation(e2, m2, ACT.Exp).then_inc(ms("rexp"), 1)

        def route_dve(dve, l, step):
            ms = lambda n: moe_sem(l, n)
            mw = lambda n, v: moe_wait(l, n, v)
            bt = lambda a, n: a[:, :, None].to_broadcast([P, NT, n])
            dve.wait_ge(*mw("logitsT", 1))
            dve.tensor_copy(LT[0:NR, :], PB[6][0:NR, :]).then_inc(ms("logitsT_out"), 1)
            dve.wait_ge(*mw("logits", 1))
            dve.wait_ge(router_in, 64 * (l + 1))
            step.then(dve.tensor_tensor(LG, tg(PB[7][:, 0:NT * NR]), br[:, None, :].to_broadcast([P, NT, NR]), ALU.add))
            step.then(dve.tensor_reduce(gmax, LG[:, :, 0:NG], AX, ALU.max))
            dve.tensor_tensor(dg, LG[:, :, 0:NG], bt(gmax, NG), ALU.subtract).then_inc(ms("gdiff"), 1)
            dve.wait_ge(*mw("gdiff", 1))
            one_hot(dve, step, ohg, dg)
            step.then(dve.tensor_tensor(EL4, LG[:, :, NG:NR].rearrange("p t (g e) -> p t e g", g=NG),
                                        ohg[:, :, None, :].to_broadcast([P, NT, EPG, NG]), ALU.mult))
            step.then(dve.tensor_reduce(EL, EL4, AX, ALU.add))
            step.then(dve.tensor_reduce(m1, EL, AX, ALU.max))
            step.then(dve.tensor_tensor(dd, EL, bt(m1, EPG), ALU.subtract))
            one_hot(dve, step, oh1, dd)
            step.then(dve.scalar_tensor_tensor(EL2, oh1, -BIG, EL, ALU.mult, ALU.add))
            step.then(dve.tensor_reduce(m2, EL2, AX, ALU.max))
            step.then(dve.tensor_tensor(dd, EL2, bt(m2, EPG), ALU.subtract))
            one_hot(dve, step, oh2, dd)
            dve.tensor_tensor(m2, m2, m1, ALU.subtract).then_inc(ms("ediff"), 1)
            for M, oh in ((M1, oh1), (M2, oh2)):
                step(dve.tensor_tensor(M.rearrange("p t (g e) -> p t g e", g=NG), ohg[:, :, :, None].to_broadcast([P, NT, NG, EPG]),
                                       oh[:, :, None, :].to_broadcast([P, NT, NG, EPG]), ALU.mult))
            step(dve.memset(MMz[:, NT * NE:(NT + 1) * NE], 0.0))
            step.wait()
            dve.tensor_tensor(MM, M1, M2, ALU.add).then_inc(ms("masks"), 1)
            dve.wait_ge(*mw("counts", 1))
            dve.wait_ge(*mw("masks", 1))
            step.then(dve.scalar_tensor_tensor(POSM, tg(PB[5][:, 0:NT * NE]), 1.0, MM, ALU.add, ALU.mult))
            step.then(dve.tensor_scalar(POSM, POSM, -1.0, None, ALU.add))

        def gates_dve(dve, l, step):
            ms = lambda n: moe_sem(l, n)
            mw = lambda n, v: moe_wait(l, n, v)
            bt = lambda a: a[:, :, None].to_broadcast([P, NT, NE])
            dve.wait_ge(*mw("rexp", 2))
            step.then(dve.tensor_reduce(rsg, eg, AX, ALU.add))
            step.then(dve.scalar_tensor_tensor(gate1, e2, 1.0, rsg, ALU.add, ALU.mult))
            step.then(dve.reciprocal(gate1, gate1))
            step.then(dve.tensor_tensor(gate2, gate1, e2, ALU.mult))
            step(dve.tensor_tensor(M1, M1, bt(gate1), ALU.mult))
            step.then(dve.tensor_tensor(M2, M2, bt(gate2), ALU.mult))
            step(dve.tensor_tensor(GG, M1, M2, ALU.add))
            step.then(dve.tensor_reduce(cnt_f, PB[5][:, NT * NE:(NT + 1) * NE], AX, ALU.max))
            dve.tensor_copy(cnt[:, :], cnt_f).then_inc(ms("routed"), 1)
            dve.wait_ge(*mw("routed", 1))

        BX, BXT, BGU, BH, BY, BC = PB[0:2], (PB[2], PB[0]), PB[3], PB[4], PB[5], PB[6:8]

        def one(e):
            return slice(e, e + 1) if isinstance(e, int) else bass.ds(e, 1)

        def split_tokens_act(act, l):
            act.wait_ge(*moe_wait(l, "logitsT", 1))
            for t in range(NT):
                act.copy(XNU[:, t, :], XN[:, t, :]).then_inc(moe_sem(l, "xn_upper"), 1)

        def split_tokens_pool(pool, l):
            for t in range(NT):
                pool.wait_ge(*moe_wait(l, "xn_upper", t + 1))
                pool.tensor_tensor(XN_r[:, t, :], XN[:, t, :], XNU[:, t, :].bitcast(F32), ALU.subtract).then_inc(moe_sem(l, "xn_lower"), 1)

        def gather_mm(pe, oh, half):
            for t in range(NT):
                for i, part in enumerate((XNU, XN_r)):
                    mm = pe.matmul(BX[half][:, :], oh[:, t, :], part[:, t, half * 512:(half + 1) * 512], start=(t + i == 0), stop=(t == NT - 1 and i == 1))
            return mm

        def xt_mm(pe, g):
            for k in range(4 * g, 4 * g + 4):
                mm = pe.transpose(BXT[g][:, (k % 4) * P:(k % 4 + 1) * P], XG[:, (k % 2) * 512 + k // 2:(k % 2 + 1) * 512:4], ident)
            return mm

        def ot_mm(pe, oh):
            for t in range(NT):
                mm = pe.transpose(BXT[0][:, t * P:(t + 1) * P], oh[:, t, :].bitcast(F32), ident)
            return mm

        def gs_mm(pe, oh, e0):
            for u in range(2):
                for t in range(NT):
                    mm = pe.matmul(BH[0:SLOTS, 4 * SLOTS + u:4 * SLOTS + u + 1], oh[:, t, u * SLOTS:(u + 1) * SLOTS].bitcast(F32), GG[:, t, one(e0 + u)],
                                   start=(t == 0), stop=(t == NT - 1))
            return mm

        def x_tile(k, u):
            return XTt[:, k, u * SLOTS:(u + 1) * SLOTS]

        def ht_mm(pe):
            for j in range(4):
                mm = pe.transpose(BH[:, j * SLOTS:(j + 1) * SLOTS], SIL[0:SLOTS, j:512:4], ident[0:SLOTS, 0:SLOTS])
            return mm

        def down_mm(pe, w):
            for j in range(4):
                for half in range(2):
                    mm = pe.matmul(BY[64 * half:64 * half + 64, :], HHT[:, j * SLOTS:(j + 1) * SLOTS], w[:, j, half * 512:(half + 1) * 512],
                                   start=(j == 0), stop=(j == 3))
            return mm

        def comb_mm(pe, bank, m):
            t, half = m // 2, m % 2
            for i, part in enumerate((YU, YL)):
                mm = pe.matmul(bank[:, :], OT[:, t * P:(t + 1) * P], part[:, half * 512:(half + 1) * 512], start=(i == 0), stop=(i == 1))
            return mm

        def y_upper(act, u, half):
            return act.copy(YU[64 * u:64 * u + 64, half * 512:(half + 1) * 512], BY[64 * half:64 * half + 64, :])

        def y_lower(dve, u, half):
            o = (slice(64 * u, 64 * u + 64), slice(half * 512, (half + 1) * 512))
            return dve.tensor_tensor(YL[o], BY[64 * half:64 * half + 64, :], YU[o].bitcast(F32), ALU.subtract)

        def hidden_mul(dve, u):
            return dve.scalar_tensor_tensor(SIL[0:SLOTS, :], SIL[0:SLOTS, :], GSL[0:SLOTS, u:u + 1], BGU[SLOTS:2 * SLOTS, :], ALU.mult, ALU.mult)

        def x_part(m):
            return X[:, m // 2, (m % 2) * 512:(m % 2) * 512 + 512]

        w_over = lambda l: slot_of(c_moe[l])

        def w_need(l, u, j, i):
            c = c_moe[l] + 3 * u + j
            return w_landed[c % RING], landed(c) + 16 * i

        def pairs_loop(eng, pair):
            pair(0, 0)
            pair(1, 1)
            with eng.Fori(1, PAIRS // 2 - 1) as q:
                pair(2 * q, 0)
                pair(2 * q + 1, 1)
            pair(PAIRS - 2, 0)
            pair(PAIRS - 1, 1)

        def is_at(i, n):
            return isinstance(i, int) and i == n

        def experts_pe(pe, l):
            ms = lambda n: moe_sem(l, n)
            mw = lambda n, v: moe_wait(l, n, v)
            last = PAIRS - 1

            def gate_up(i, u):
                for j in range(2):
                    pe.wait_ge(*w_need(l, u, j, i))
                if u == 0:
                    pe.wait_ge(*mw("xt_out", 2 * i + 2))
                    if not is_at(i, 0):
                        pe.wait_ge(*mw("hh", 2 * i))
                wg, wu = (slot_of(c_moe[l] + 3 * u + j).rearrange("p (k n) -> p k n", k=KT) for j in range(2))
                for k in range(KT):
                    pe.matmul(BGU[0:SLOTS, :], x_tile(k, u), wg[:, k, :], start=(k == 0), stop=(k == KT - 1))
                    mm = pe.matmul(BGU[SLOTS:2 * SLOTS, :], x_tile(k, u), wu[:, k, :], start=(k == 0), stop=(k == KT - 1))
                mm.then_inc(ms("gu"), 1)

            def down(i, b, u):
                pe.wait_ge(*mw("hh", 2 * i + u + 1))
                alone(pe)
                ht_mm(pe).then_inc(ms("ht"), 1)
                pe.wait_ge(*mw("ht_out", 2 * i + u + 1))
                if u and not is_at(i, last):
                    gs_mm(pe, OH[1 - b], 2 * (i + 1)).then_inc(ms("gs"), 1)
                pe.wait_ge(*w_need(l, u, 2, i))
                if not (is_at(i, 0) and u == 0):
                    pe.wait_ge(*mw("y_lower", 4 * i + 2 * u))
                down_mm(pe, slot_of(c_moe[l] + 3 * u + 2).rearrange("p (k n) -> p k n", k=4)).then_inc(ms("y"), 1)

            def combine(i, ms_):
                for m in ms_:
                    if m == 0:
                        pe.wait_ge(*mw("y_lower", 4 * i + 4))
                        pe.wait_ge(*mw("ot_out", i + 1))
                    if not (is_at(i, 0) and m < 2):
                        pe.wait_ge(*mw("added", 8 * i + m - 1))
                    comb_mm(pe, BC[m % 2], m).then_inc(ms("comb"), 1)

            def gather(i, b, half):
                if half == 0:
                    pe.wait_ge(*mw("oh", i + 1))
                    if is_at(i, 0):
                        pe.wait_ge(*mw("xn_lower", NT))
                gather_mm(pe, OH[b], half).then_inc(ms("gat"), 1)

            def x_transposed(i):
                pe.wait_ge(*mw("xg", 2 * i + 2))
                if not is_at(i, 0):
                    pe.wait_ge(*mw("ot_out", i))
                for g in range(2):
                    xt_mm(pe, g).then_inc(ms("xt"), 1)

            def pair(i, b):
                gate_up(i, 0)
                more = not is_at(i, last)
                before = not is_at(i, 0)
                if before:
                    combine(i - 1, (0, 1))
                if more:
                    gather(i + 1, 1 - b, 0)
                if before:
                    combine(i - 1, (2, 3))
                if more:
                    gather(i + 1, 1 - b, 1)
                if before:
                    combine(i - 1, (4, 5))
                ot_mm(pe, OH[b]).then_inc(ms("ot"), 1)
                if before:
                    combine(i - 1, (6, 7))
                pe.wait_ge(*mw("gs_out", i + 1))
                down(i, b, 0)
                gate_up(i, 1)
                if more:
                    x_transposed(i + 1)
                down(i, b, 1)

            gather(0, 0, 0)
            gather(0, 0, 1)
            pe.wait_ge(*mw("routed", 1))
            gs_mm(pe, OH[0], 0).then_inc(ms("gs"), 1)
            x_transposed(0)
            pairs_loop(pe, pair)
            combine(last, range(8))
            n_most = pe.value_load(cnt[0:1, 0:1], min_val=0, max_val=SEQ)
            with pe.If(n_most > SLOTS):
                with pe.Fori(1, SEQ // SLOTS) as b:
                    with pe.Fori(0, PAIRS) as i:
                        n = (b - 1) * PAIRS + i

                        def wait(name):
                            pe.wait_ge(*over_wait(l, name, n))
                            alone(pe)

                        wait("v_oh")
                        for half in range(2):
                            gather_mm(pe, OH[0], half)
                        ot_mm(pe, OH[0])
                        gs_mm(pe, OH[0], 2 * i).then_inc(over_done(l, "v_gat"), 1)
                        wait("v_xg")
                        for g in range(2):
                            mm = xt_mm(pe, g)
                        mm.then_inc(over_done(l, "v_xt"), 1)
                        wait("v_xt_out")
                        for u in range(2):
                            for half, name in enumerate((f"v_g{u}", f"v_u{u}")):
                                pe.wait_ge(ms("v_w"), 16 * (6 * n + 3 * u + half + 1))
                                alone(pe)
                                w = w_over(l).rearrange("p (k n) -> p k n", k=KT)
                                for k in range(KT):
                                    mm = pe.matmul(BGU[SLOTS * half:SLOTS * half + SLOTS, :], x_tile(k, u), w[:, k, :], start=(k == 0), stop=(k == KT - 1))
                                mm.then_inc(over_done(l, name), 1)
                            wait(f"v_hh{u}")
                            ht_mm(pe).then_inc(over_done(l, f"v_ht{u}"), 1)
                            wait(f"v_ht_out{u}")
                            pe.wait_ge(ms("v_w"), 16 * (6 * n + 3 * u + 3))
                            alone(pe)
                            down_mm(pe, w_over(l).rearrange("p (k n) -> p k n", k=4)).then_inc(over_done(l, f"v_y{u}"), 1)
                        wait("v_y_lower1")
                        for m in range(8):
                            mm = comb_mm(pe, PB[m], m)
                        mm.then_inc(over_done(l, "v_comb"), 1)
                        wait("v_added")

        def experts_act(act, l, step):
            ms = lambda n: moe_sem(l, n)
            mw = lambda n, v: moe_wait(l, n, v)
            last = PAIRS - 1

            def x_gathered(i):
                for half in range(2):
                    act.wait_ge(*mw("gat", 2 * i + half + 1))
                    act.copy(XG[:, half * 512:(half + 1) * 512], BX[half][:, :]).then_inc(ms("xg"), 1)

            def y_out(i, u):
                act.wait_ge(*mw("ht", 2 * i + u + 1))
                act.copy(HHT, BH[:, 0:4 * SLOTS]).then_inc(ms("ht_out"), 1)
                if u and not is_at(i, last):
                    slot_gates(i + 1)
                for half in range(2):
                    act.wait_ge(*mw("y", 2 * i + u + 1))
                    y_upper(act, u, half).then_inc(ms("y_upper"), 1)

            def slot_gates(i):
                act.wait_ge(*mw("gs", i + 1))
                act.copy(GSL[0:SLOTS, :], BH[0:SLOTS, 4 * SLOTS:4 * SLOTS + 2]).then_inc(ms("gs_out"), 1)

            def silu(i, u):
                act.wait_ge(*mw("gu", 2 * i + u + 1))
                act.activation(SIL[0:SLOTS, :], BGU[0:SLOTS, :], ACT.Silu).then_inc(ms("sil"), 1)

            def pair(i, b):
                silu(i, 0)
                if not is_at(i, last):
                    x_gathered(i + 1)
                act.wait_ge(*mw("ot", i + 1))
                if not is_at(i, 0):
                    act.wait_ge(*mw("comb", 8 * i))
                act.copy(OT, BXT[0][:, :]).then_inc(ms("ot_out"), 1)
                y_out(i, 0)
                silu(i, 1)
                y_out(i, 1)

            x_gathered(0)
            slot_gates(0)
            pairs_loop(act, pair)
            n_most = act.value_load(cnt[0:1, 0:1], min_val=0, max_val=SEQ)
            with act.If(n_most > SLOTS):
                with act.Fori(1, SEQ // SLOTS) as b:
                    with act.Fori(0, PAIRS) as i:
                        n = (b - 1) * PAIRS + i
                        act.wait_ge(*over_wait(l, "v_gat", n))
                        for half in range(2):
                            act.copy(XG[:, half * 512:(half + 1) * 512], BX[half][:, :])
                        act.copy(OT, BXT[0][:, :])
                        act.copy(GSL[0:SLOTS, :], BH[0:SLOTS, 4 * SLOTS:4 * SLOTS + 2]).then_inc(over_done(l, "v_xg"), 1)
                        for u in range(2):
                            act.wait_ge(*over_wait(l, f"v_u{u}", n))
                            act.activation(SIL[0:SLOTS, :], BGU[0:SLOTS, :], ACT.Silu).then_inc(over_done(l, f"v_sil{u}"), 1)
                            act.wait_ge(*over_wait(l, f"v_ht{u}", n))
                            act.copy(HHT, BH[:, 0:4 * SLOTS]).then_inc(over_done(l, f"v_ht_out{u}"), 1)
                            act.wait_ge(*over_wait(l, f"v_y{u}", n))
                            y_upper(act, u, 0)
                            y_upper(act, u, 1).then_inc(over_done(l, f"v_y_upper{u}"), 1)

        def experts_dve(dve, l, step):
            ms = lambda n: moe_sem(l, n)
            mw = lambda n, v: moe_wait(l, n, v)
            last = PAIRS - 1
            pair_slots = const("slot")[:, None, None, :].to_broadcast([P, NT, 2, SLOTS])

            def one_hots(i, buf):
                col = POSM[:, :, slice(2 * i, 2 * i + 2) if isinstance(i, int) else bass.ds(2 * i, 2)]
                return dve.tensor_tensor(OH[buf].rearrange("p t (u s) -> p t u s", u=2), pair_slots,
                                         col[:, :, :, None].to_broadcast([P, NT, 2, SLOTS]), ALU.is_equal)

            def x_out(i):
                for g in range(2):
                    dve.wait_ge(*mw("xt", 2 * i + g + 1))
                    dve.tensor_copy(XTt[:, 4 * g:4 * g + 4, :], BXT[g][:, :].rearrange("p (k n) -> p k n", k=4)).then_inc(ms("xt_out"), 1)

            def hidden(i, u):
                dve.wait_ge(*mw("sil", 2 * i + u + 1))
                if u == 0:
                    dve.wait_ge(*mw("gs_out", i + 1))
                hidden_mul(dve, u).then_inc(ms("hh"), 1)

            def y_out(i, u):
                for half in range(2):
                    dve.wait_ge(*mw("y_upper", 4 * i + 2 * u + 2))
                    y_lower(dve, u, half).then_inc(ms("y_lower"), 1)

            def add(i, m):
                dve.wait_ge(*mw("comb", 8 * i + m + 1))
                if not is_at(i, 0):
                    dve.wait_ge(*mw("added", 8 * i + m - 7))
                dve.tensor_tensor(x_part(m), x_part(m), BC[m % 2][:, :], ALU.add).then_inc(ms("added"), 1)

            def pair(i, b):
                if not is_at(i, 0):
                    add(i - 1, 0)
                hidden(i, 0)
                if not is_at(i, 0):
                    for m in range(1, 8):
                        add(i - 1, m)
                if not (is_at(i, last) or is_at(i, last - 1)):
                    dve.wait_ge(*mw("ot", i + 1))
                    one_hots(i + 2, b).then_inc(ms("oh"), 1)
                y_out(i, 0)
                hidden(i, 1)
                if not is_at(i, last):
                    x_out(i + 1)
                y_out(i, 1)

            one_hots(0, 0).then_inc(ms("oh"), 1)
            one_hots(1, 1).then_inc(ms("oh"), 1)
            gates_dve(dve, l, step)
            x_out(0)
            pairs_loop(dve, pair)
            base = (R_EVEN, R_ODD)[l]
            n_most = dve.value_load(cnt[0:1, 0:1], min_val=0, max_val=SEQ)
            with dve.If(n_most < SLOTS + 1):
                for m in range(8):
                    add(last, m)
                    if m % 2:
                        dve.wait_ge(*mw("added", 8 * last + m + 1))
                        dve.sem_inc(resid, 1)
                    if m % 2 and l == 0:
                        norm_dve(dve, 2, m // 2 - 1)
            with dve.If(n_most > SLOTS):
                for m in range(8):
                    add(last, m)
                dve.wait_ge(*mw("added", 8 * PAIRS))
                with dve.Fori(1, SEQ // SLOTS) as b:
                    dve.tensor_scalar(POSM, POSM, -float(SLOTS), None, ALU.add).then_inc(ms("v_pos"), 1)
                    dve.wait_ge(ms("v_pos"), b)
                    alone(dve)
                    with dve.Fori(0, PAIRS) as i:
                        n = (b - 1) * PAIRS + i
                        one_hots(i, 0).then_inc(over_done(l, "v_oh"), 1)
                        dve.wait_ge(*over_wait(l, "v_xt", n))
                        dve.tensor_copy(XTt[:, 0:4, :], BXT[0][:, :].rearrange("p (k n) -> p k n", k=4))
                        dve.tensor_copy(XTt[:, 4:8, :], BXT[1][:, :].rearrange("p (k n) -> p k n", k=4)).then_inc(over_done(l, "v_xt_out"), 1)
                        for u in range(2):
                            dve.wait_ge(*over_wait(l, f"v_sil{u}", n))
                            hidden_mul(dve, u).then_inc(over_done(l, f"v_hh{u}"), 1)
                            dve.wait_ge(*over_wait(l, f"v_y_upper{u}", n))
                            y_lower(dve, u, 0)
                            y_lower(dve, u, 1).then_inc(over_done(l, f"v_y_lower{u}"), 1)
                        dve.wait_ge(*over_wait(l, "v_comb", n))
                        for m in range(8):
                            ins = dve.tensor_tensor(x_part(m), x_part(m), PB[m][:, :], ALU.add)
                        ins.then_inc(over_done(l, "v_added"), 1)
                        dve.wait_ge(*over_wait(l, "v_added", n))
                        alone(dve)
                dve.sem_inc(resid, NT)
                if l == 0:
                    for t in range(NT - 1):
                        norm_dve(dve, 2, t)
            if l == 0:
                norm_dve(dve, 2, NT - 1)

        def experts_sp(sp, l):
            mw = lambda n, v: moe_wait(l, n, v)
            mats = (w_gate[l], w_up[l], w_down[l])

            def load(i, u, j):
                e = 2 * i + u
                c = c_moe[l] + 3 * u + j
                if isinstance(i, int) and i == 0:
                    sp.wait_ge(*released[c - RING])
                else:
                    sp.wait_ge(*mw("gu" if j < 2 else "y", e - 1))
                src = mats[j].rearrange("e (p k) n -> p e (k n)", p=P)[:, one(e), :]
                sp.dma_start(slot_of(c), src.rearrange("p e n -> p (e n)"), max_dma_last_dim=4096).then_inc(w_landed[c % RING], 16)

            for u in range(2):
                for j in range(3):
                    load(0, u, j)
            with sp.Fori(1, PAIRS) as i:
                for u in range(2):
                    for j in range(3):
                        load(i, u, j)

        def overflow_sp(sp, l):
            ms = lambda n: moe_sem(l, n)
            mw = lambda n, v: moe_wait(l, n, v)
            sp.wait_ge(*mw("routed", 1))
            n_most = sp.value_load(cnt[0:1, 0:1], min_val=0, max_val=SEQ)
            with sp.If(n_most > SLOTS):
                sp.wait_ge(*mw("y", NE))
                with sp.Fori(1, SEQ // SLOTS) as b:
                    with sp.Fori(0, PAIRS) as i:
                        n = (b - 1) * PAIRS + i
                        for u in range(2):
                            for j, name in enumerate(("v_g", "v_u", "v_y")):
                                src = (w_gate[l], w_up[l], w_down[l])[j].rearrange("e (p k) n -> p e (k n)", p=P)[:, bass.ds(2 * i + u, 1), :]
                                sp.dma_start(w_over(l), src.rearrange("p e n -> p (e n)"), max_dma_last_dim=4096).then_inc(ms("v_w"), 16)
                                sp.wait_ge(*over_wait(l, name + str(u), n))
                        alone(sp)

        def const_odd_(name):
            a, b = co[name]
            return SCR[:, CO_AT + a:CO_AT + b]

        s_.n = 0
        two = lambda a: a.rearrange("p (m n) -> p m n", m=2)
        QR, KR, QX, Sr = (two(s_(1024)) for _ in range(4))
        YTl = SCR_r[:, s_.n - 2048:s_.n].rearrange("p (j n) -> p j n", j=4)
        ATr = t4(s_(512))
        KZ = s_(3 * 256).rearrange("p (t m n) -> p t m n", t=3, m=2)
        rtmp = [s_(512) for _ in range(4)]
        YTr = r32(s_(2048)).rearrange("p (j n) -> p j n", j=4)
        r_ss, r_rs = s_(NT), s_(NT)
        rjunk = s_(512)
        VO = XN[:, 0:2, :].rearrange("p a (b n) -> p (a b) n", b=2)
        ZS = XN[:, 2:4, :].rearrange("p a (b n) -> p (a b) n", b=2)

        def odd_chunk(name, h):
            j, c = odd_at[name, h]
            return j, c, (WU[j % 2], ring_r[:, c % RING, :])

        def split_act(act, j):
            c = odd_at[odd_order[j]][1]
            act.wait_ge(w_landed[c % RING], landed(c))
            if j < 2:
                act.wait_ge(*moe_wait(0, "gu", NE))
            else:
                act.wait_ge(*left[j - 2])
            for q in range(4):
                at = slice(q * SLOT // 4, (q + 1) * SLOT // 4)
                act.copy(WU[j % 2][:, at], slot_of(c)[:, at]).then_inc(sg("r_upper"), 1)

        def split_pool(pool, j):
            c = odd_at[odd_order[j]][1]
            for q in range(4):
                at = slice(q * SLOT // 4, (q + 1) * SLOT // 4)
                pool.wait_ge(sg("r_upper"), 4 * j + q + 1)
                pool.tensor_tensor(ring_r[:, c % RING, at], slot_of(c)[:, at], WU[j % 2][:, at].bitcast(F32), ALU.subtract).then_inc(sg("r_lower"), 1)

        left = []
        for name, h in odd_order:
            left.append({"qk": ("r_qk", 2 * h + 2), "v": ("r_v", NT * (h + 1)), "z": ("r_z", NT * (h + 1)), "out": ("r_out", 8 * (h + 1))}[name])
        left = [(sg(a), b) for a, b in left]

        def ret_qk_pe(pe, h):
            j, c, w = odd_chunk("qk", h)
            w = [a.rearrange("p (k s n) -> p k s n", k=KT, s=2) for a in w]
            if h:
                pe.wait_ge(sg("r_o_out"), NT * h)
                pe.wait_ge(sg("r_S"), 6 * h)
            for s in range(2):
                for par in range(2):
                    for k in range(KT):
                        if s + par == 0:
                            pe.wait_ge(sg("r_lower"), 4 * j + k // 2 + 1)
                        mm = split_mm(pe, PB[2 * s + par][:, :], [a[:, k, s, par:RQ:2] for a in w], (HTU[:, k, :], HT_r[:, k, :]), k == 0, k == KT - 1)
                mm.then_inc(sg("r_qk"), 1)

        def ret_pe(pe):
            ret_qk_pe(pe, 0)
            for h in range(RH):
                j, c, w = odd_chunk("v", h)
                w = [a.rearrange("p (k n) -> p k n", k=KT) for a in w]
                for t in range(NT):
                    if t >= 2:
                        pe.wait_ge(sg("r_v_out"), NT * h + t - 1)
                    elif h:
                        pe.wait_ge(resid, R_MOE0 + 8 * h - 1 + t)
                    for k in range(KT):
                        if t == 0:
                            pe.wait_ge(sg("r_lower"), 4 * j + k // 2 + 1)
                        mm = split_mm(pe, PB[4 + t % 2][:, :], [a[:, k, t * P:(t + 1) * P] for a in (HTU, HT_r)], [a[:, k, :] for a in w], k == 0, k == KT - 1)
                    mm.then_inc(sg("r_v"), 1)
                pe.wait_ge(sg("r_rot"), 2 * h + 2)
                for t in range(NT):
                    for m in range(2):
                        mm = pe.matmul(PB[0][:, t * P:(t + 1) * P], KR[:, m, t * P:(t + 1) * P], QR[:, m, t * P:(t + 1) * P], start=(m == 0), stop=(m == 1))
                mm.then_inc(sg("r_in"), 1)
                for t in range(NT - 1):
                    for m in range(2):
                        mm = pe.transpose(PB[6 + t // 2][:, (2 * (t % 2) + m) * P:(2 * (t % 2) + m + 1) * P], KR[:, m, t * P:(t + 1) * P], ident)
                mm.then_inc(sg("r_kt"), 1)
                j, c, w = odd_chunk("z", h)
                w = [a.rearrange("p (k n) -> p k n", k=KT) for a in w]
                for t in range(NT):
                    if t < 2:
                        pe.wait_ge(sg("r_v_out"), NT * h + t + 3)
                    else:
                        pe.wait_ge(sg("r_zs"), NT * h + t - 1)
                    for k in range(KT):
                        if t == 0:
                            pe.wait_ge(sg("r_lower"), 4 * j + k // 2 + 1)
                        mm = split_mm(pe, PB[4 + t % 2][:, :], [a[:, k, t * P:(t + 1) * P] for a in (HTU, HT_r)], [a[:, k, :] for a in w], k == 0, k == KT - 1)
                    mm.then_inc(sg("r_z"), 1)
                pe.wait_ge(sg("r_at"), h + 1)
                pe.wait_ge(sg("r_kz"), h + 1)
                for t in range(NT):
                    b = PB[1 + t % 2]
                    if t >= 2:
                        pe.wait_ge(sg("r_o_out"), NT * h + t - 1)
                    mm = pe.matmul(b[:, :], ATr[:, t, :], VO[:, t, :], start=True, stop=(t == 0))
                    if t:
                        pe.wait_ge(sg("r_S"), 6 * h + 2 * t)
                        for m in range(2):
                            mm = pe.matmul(b[:, :], QX[:, m, t * P:(t + 1) * P], Sr[:, m, :], start=False, stop=(m == 1))
                    mm.then_inc(sg("r_o"), 1)
                    if t < NT - 1:
                        for m in range(2):
                            pe.matmul(PB[(3, 7)[m]][:, :], KZ[:, t, m, :], VO[:, t, :], start=True, stop=True).then_inc(sg("r_su"), 1)
                if h < RH - 1:
                    ret_qk_pe(pe, h + 1)
                pe.wait_ge(sg("r_y"), NT * (h + 1))
                pe.wait_ge(sg("r_S"), 6 * (h + 1))
                for t in range(NT):
                    if t >= 2:
                        pe.wait_ge(sg("r_ytl"), NT * h + t - 1)
                    for j in range(4):
                        mm = pe.transpose(PB[6 + t % 2][:, j * P:(j + 1) * P], VO[:, t, j:512:4], ident)
                    mm.then_inc(sg("r_tr"), 1)
                i, c, w = odd_chunk("out", h)
                w = [a.rearrange("p (k n) -> p k n", k=4) for a in w]
                pe.wait_ge(sg("r_zs"), NT * (h + 1))
                for n in range(8):
                    t, half = n // 2, n % 2
                    pe.wait_ge(sg("r_ytl"), NT * h + t + 1)
                    if n >= 2:
                        pe.wait_ge(resid, R_MOE0 + 8 * h + n - 1)
                    for j in range(4):
                        if n == 0:
                            pe.wait_ge(sg("r_lower"), 4 * i + j + 1)
                        mm = split_mm(pe, PB[4 + n % 2][:, :], [a[:, j, t * P:(t + 1) * P] for a in (YTr, YTl)],
                                      [a[:, j, half * 512:(half + 1) * 512] for a in w], j == 0, j == 3)
                    mm.then_inc(sg("r_out"), 1)

        def ret_act(act, step):
            act.wait_ge(odd_in, 16)
            at = lambda name, h: odd_at[name, h][0]
            for h in range(RH):
                split_act(act, at("z", h))
                for t in range(NT):
                    act.wait_ge(sg("r_v"), NT * h + t + 1)
                    act.copy(VO[:, t, :], PB[4 + t % 2][:, :]).then_inc(sg("r_v_out"), 1)
                act.wait_ge(sg("r_kt"), h + 1)
                for t in range(NT - 1):
                    ins = act.activation(KZ[:, t, :, :], PB[6 + t // 2][:, (t % 2) * 256:(t % 2) * 256 + 256].rearrange("p (m n) -> p m n", m=2), ACT.Copy,
                                         scale=const_odd_("zeta")[:, h:h + 1])
                    if t == NT - 2:
                        ins.then_inc(sg("r_kz"), 1)
                split_act(act, at("qk", h + 1) if h < RH - 1 else at("out", h))
                for t in range(NT):
                    act.wait_ge(sg("r_z"), NT * h + t + 1)
                    act.activation(ZS[:, t, :], PB[4 + t % 2][:, :], ACT.Silu).then_inc(sg("r_zs"), 1)
                for t in range(NT):
                    act.wait_ge(sg("r_o"), NT * h + t + 1)
                    step.then(act.activation(rjunk, PB[1 + t % 2][:, :], ACT.Square, accum_out=r_ss[:, t:t + 1]))
                    if t < NT - 1:
                        act.wait_ge(sg("r_su"), 6 * h + 2 * t + 2)
                    act.copy(VO[:, t, :], PB[1 + t % 2][:, :]).then_inc(sg("r_o_out"), 1)
                if h < RH - 1:
                    split_act(act, at("out", h))
                for t in range(NT):
                    act.wait_ge(sg("r_tr"), NT * h + t + 1)
                    act.copy(YTr[:, :, t * P:(t + 1) * P], PB[6 + t % 2][:, :].rearrange("p (j q) -> p j q", j=4)).then_inc(sg("r_yt"), 1)
                if h < RH - 1:
                    split_act(act, at("v", h + 1))

        def ret_pool(pool, step):
            at = lambda name, h: odd_at[name, h][0]
            for h in range(RH):
                split_pool(pool, at("z", h))
                split_pool(pool, at("qk", h + 1) if h < RH - 1 else at("out", h))
                pool.wait_ge(sg("r_o_out"), NT * (h + 1))
                step.then(pool.tensor_scalar(r_rs, r_ss, 1.0 / RV, EPS, ALU.mult, ALU.add))
                pool.tensor_tensor(r_rs, r_rs, mhalf[:, 0:NT], ALU.pow).then_inc(sg("r_rstd"), 1)
                if h < RH - 1:
                    split_pool(pool, at("out", h))
                    split_pool(pool, at("v", h + 1))

        def ret_dve(dve, step):
            dve.wait_ge(odd_in, 16)
            cs, sn = const_odd_("xcos"), const_odd_("xsin")

            def rotate(h, which):
                for s, R in which:
                    dve.wait_ge(sg("r_qk"), 2 * h + s + 1)
                    e_, o_ = PB[2 * s][:, :], PB[2 * s + 1][:, :]
                    step(dve.tensor_tensor(rtmp[0], e_, cs, ALU.mult))
                    step(dve.tensor_tensor(rtmp[1], o_, sn, ALU.mult))
                    step(dve.tensor_tensor(rtmp[2], o_, cs, ALU.mult))
                    step(dve.tensor_tensor(rtmp[3], e_, sn, ALU.mult))
                    step.wait()
                    step(dve.tensor_tensor(R[:, 0, :], rtmp[0], rtmp[1], ALU.subtract))
                    dve.tensor_tensor(R[:, 1, :], rtmp[2], rtmp[3], ALU.add).then_inc(sg("r_rot"), 1)
                    step.wait()
                    dve.wait_ge(sg("r_rot"), 2 * h + s + 1)

            both = ((0, QR), (1, KR))
            rotate(0, both)
            for h in range(RH):
                for m in range(2):
                    step(dve.tensor_tensor(t4(QX[:, m, :]), t4(QR[:, m, :]), const_odd_(f"xi{h}")[:, None, :].to_broadcast([P, NT, P]), ALU.mult))
                dve.wait_ge(sg("r_in"), h + 1)
                step.wait()
                dve.tensor_tensor(ATr, t4(PB[0][:, :]), const_odd_(f"decay{h}")[:, None, :].to_broadcast([P, NT, P]), ALU.mult).then_inc(sg("r_at"), 1)
                for t in range(NT - 1):
                    for m in range(2):
                        dve.wait_ge(sg("r_su"), 6 * h + 2 * t + m + 1)
                        b = PB[(3, 7)[m]][:, :]
                        if t:
                            dve.wait_ge(sg("r_S"), 6 * h + 2 * (t - 1) + m + 1)
                            dve.wait_ge(sg("r_o"), NT * h + t + 1)
                            ins = dve.scalar_tensor_tensor(Sr[:, m, :], Sr[:, m, :], gamma[h], b, ALU.mult, ALU.add)
                        else:
                            ins = dve.tensor_copy(Sr[:, m, :], b)
                        ins.then_inc(sg("r_S"), 1)
                dve.wait_ge(sg("r_rstd"), h + 1)
                dve.wait_ge(sg("r_zs"), NT * (h + 1))
                for t in range(NT):
                    dve.scalar_tensor_tensor(VO[:, t, :], VO[:, t, :], r_rs[:, t:t + 1], ZS[:, t, :], ALU.mult, ALU.mult).then_inc(sg("r_y"), 1)
                if h < RH - 1:
                    dve.wait_ge(sg("r_o"), NT * (h + 1))
                    rotate(h + 1, both[0:1])
                for t in range(NT):
                    dve.wait_ge(sg("r_yt"), NT * h + t + 1)
                    b = (slice(None), slice(None), slice(t * P, (t + 1) * P))
                    dve.tensor_tensor(YTl[b], PB[6 + t % 2][:, :].rearrange("p (j q) -> p j q", j=4), YTr[b].bitcast(F32), ALU.subtract).then_inc(sg("r_ytl"), 1)
                if h < RH - 1:
                    rotate(h + 1, both[1:2])
                for n in range(8):
                    t, half = n // 2, n % 2
                    dve.wait_ge(sg("r_out"), 8 * h + n + 1)
                    xs = X[:, t, half * 512:(half + 1) * 512]
                    dve.wait_ge(resid, R_MOE0 + 8 * h)
                    dve.tensor_tensor(xs, xs, PB[4 + n % 2][:, :], ALU.add).then_inc(resid, 1)
                    if half and h == RH - 1:
                        norm_dve(dve, 3, t - 1)
            norm_dve(dve, 3, NT - 1)

        released = {c_kv: (sg("a_proj"), 4), c_q: (sg("a_proj"), 8)}
        for h in range(GH):
            released[gdn_at[h]] = (sg("d_z"), h + 1)
        for c in range(c_oute - 2, c_oute):
            released[c] = (sg("m_out"), 8)
        for g in range(2):
            released[c_oute + g] = (sg("m_out"), 8)
        for l in range(2):
            for e in range(NE):
                released[c_moe[l] + 3 * e] = released[c_moe[l] + 3 * e + 1] = moe_wait(l, "gu", e + 1)
                released[c_moe[l] + 3 * e + 2] = moe_wait(l, "y", e + 1)
        for j, name in enumerate(odd_order):
            released[odd_at[name][1]] = left[j]
        for c in range(c_moe[0] + 3 * NE, c_moe[1]):
            if c not in released:
                released[c] = left[-1] if c % RING != 1 else left[odd_at["z", RH - 1][0]]

        stored = sem("stored")
        R_END = (0, R_EVEN, R_MOE0, R_ODD, R_MOE1)[upto]
        block = ctx.enter_context(nc.Block())

        @block.sync
        def _(sp):
            tokens = x[0].rearrange("(t p) d -> p t d", p=P)
            sp.dma_start(X[:, 0:2, :], tokens[:, 0:2, :]).then_inc(x_in, 16)
            sp.dma_start(X[:, 2:4, :], tokens[:, 2:4, :]).then_inc(sg("x_in_late"), 16)
            sp.dma_start(CE[:, :], const_even).then_inc(consts_in, 16)

            def load(c):
                if c in (c_oute, c_oute + 1):
                    sp.wait_ge(sg("d_kv"), GH)
                    sp.wait_ge(sg("d_qd"), GH)
                elif c == gdn_at[1]:
                    sp.wait_ge(sg("a_proj"), 8)
                elif c >= RING:
                    sp.wait_ge(*released[c - RING])
                for dst, src in chunks[c]:
                    sp.dma_start(dst(slot_of(c)), src).then_inc(w_landed[c % RING], 16)

            for c in range(c_moe[0]):
                if chunks[c]:
                    load(c)
            if upto > 1:
                experts_sp(sp, 0)
                overflow_sp(sp, 0)
            if upto > 2:
                for c in (odd_at[name][1] for name in odd_order):
                    load(c)
            if upto > 3:
                experts_sp(sp, 1)
                overflow_sp(sp, 1)
            for t in range(NT):
                sp.wait_ge(resid, R_END - NT + t + 1 if upto == 4 else R_END)
                sp.dma_start(out[0].rearrange("(t p) d -> p t d", p=P)[:, t, :], X[:, t, :]).then_inc(stored, 16)
            sp.wait_ge(stored, 16 * NT)

        @block.gpsimd
        def _(pool):
            step = Steps(pool, pool_step)
            pool.memset(mhalf[:, :], -0.5).then_inc(mhalf_set, 1)
            gain_pool(pool, 0)
            pool.wait_ge(mhalf_set, 1)
            norm_pool(pool, 0, step)
            split_kvq_pool(pool)
            for dst, src in ((qk_gain[:, 0:512].rearrange("p (h d) -> p h d", h=AH), q_gain_even[0:1, None, :].to_broadcast([P, AH, ADH])),
                             (qk_gain[:, 512:640].rearrange("p (h d) -> p h d", h=AKV), k_gain_even[0:1, None, :].to_broadcast([P, AKV, ADH])),
                             (sink_b, sinks_even[0:1, :].to_broadcast([P, AH])),
                             (alog_b, a_log_even[0:1, :].to_broadcast([P, GH])),
                             (dtb_b, dt_bias_even[0:1, :].to_broadcast([P, GH])),
                             (gdn_gain, gdn_gain_even[0:1, :].to_broadcast([P, GD]))):
                pool.dma_start(dst, src).then_inc(params_in, 16)
            pool.dma_start(cwr[0:48, :], conv_w_even[0].rearrange("i (c n) -> (i c) n", n=P)).then_inc(params_in, 16)
            if upto > 1:
                route_pool(pool, 0)
            if upto > 1:
                gain_pool(pool, 1)
            for n in range(4):
                split_gdn_pool(pool, n)
            attn_pool(pool, step)
            for n in range(4, 4 * GH):
                split_gdn_pool(pool, n)
            gdn_pool(pool, step)
            if upto > 1:
                norm_pool(pool, 1, step)
                pool.wait_ge(resid, R_EVEN)
                pool.dma_start(SCR[:, CO_AT:SCR_N], const_odd).then_inc(odd_in, 16)
                if upto > 2:
                    gain_pool(pool, 2)
                split_tokens_pool(pool, 0)
            if upto > 2:
                if upto > 3:
                    route_pool(pool, 1)
                norm_pool(pool, 2, step)
                split_pool(pool, 0)
                split_pool(pool, 1)
                if upto > 3:
                    gain_pool(pool, 3)
                ret_pool(pool, step)
            if upto > 3:
                norm_pool(pool, 3, step)
                split_tokens_pool(pool, 1)

        @block.scalar
        def _(act):
            step = Steps(act, act_step)
            norm_act(act, 0)
            norm_act_out(act, 0, lambda n: split_kvq_act(act, (n - 3) // 2) if n in (3, 5) else None)
            for i in range(2, 6):
                split_kvq_act(act, i)
            attn_act(act, step)
            gdn_act(act, step)
            oute_act(act)
            for l in range(2):
                if upto > 2 * l + 1:
                    norm_act(act, 2 * l + 1)
                    norm_act_out(act, 2 * l + 1)
                    route_act(act, l)
                    experts_act(act, l, step)
                if l == 0 and upto > 2:
                    split_act(act, 0)
                    norm_act(act, 2)
                    norm_act_out(act, 2)
                    split_act(act, 1)
                    ret_act(act, step)

        @block.vector
        def _(dve):
            step = Steps(dve, dve_step)
            for t in range(NT):
                norm_dve(dve, 0, t)
            norm_dve_out(dve, 0)
            attn_dve(dve, step)
            gdn_dve(dve, step)
            oute_dve(dve)
            for l in range(2):
                if upto > 2 * l + 1:
                    norm_dve_out(dve, 2 * l + 1)
                    route_dve(dve, l, step)
                    experts_dve(dve, l, step)
                if l == 0 and upto > 2:
                    norm_dve_out(dve, 2)
                    ret_dve(dve, step)

        @block.tensor
        def _(pe):
            norm_pe(pe, 0)
            attn_pe(pe)
            gdn_pe(pe)
            oute_pe(pe)
            for l in range(2):
                if upto > 2 * l + 1:
                    norm_pe(pe, 2 * l + 1, lambda t, l=l: logits_pe(pe, l, t))
                    route_pe(pe, l)
                    experts_pe(pe, l)
                if l == 0 and upto > 2:
                    norm_pe(pe, 2)
                    ret_pe(pe)


_INS = ['x', 'ln_mix_even', 'w_in_even', 'conv_w_even', 'a_log_even', 'dt_bias_even', 'q_gain_even', 'k_gain_even',
        'sinks_even', 'gdn_gain_even', 'w_out_even', 'ln_mix_odd', 'w_in_odd', 'w_out_odd', 'ln_ffn',
        'w_router_group', 'b_router_group', 'w_router_expert', 'b_router_expert', 'w_gate', 'w_up', 'w_down']


def packed(tables):
    return np.ascontiguousarray(np.concatenate([np.asarray(a, np.float32) for a in tables.values()], axis=1))


def kernel(**inputs):
    import concourse.bacc as bacc
    from concourse.bass_utils import run_bass_kernel_spmd

    nc = bacc.Bacc("TRN2", target_bir_lowering=False, num_devices=1)
    arrays, args = {}, []
    tab_even, tab_odd, _ = constants()
    for name, a in [(n, inputs[n]) for n in _INS] + [("const_even", packed(tab_even)), ("const_odd", packed(tab_odd))]:
        a = np.ascontiguousarray(a)
        arrays[f"in_{name}_dram"] = a
        args.append(nc.dram_tensor(f"in_{name}_dram", a.shape, mybir.dt.from_np(a.dtype), kind="ExternalInput").ap())
    args.append(nc.dram_tensor("out_0_dram", (1, SEQ, D), F32, kind="ExternalOutput").ap())
    program(nc, *args)
    r = run_bass_kernel_spmd(nc, [arrays], core_ids=[0])
    return r.results[0]["out_0_dram"]
```
